# Optimizing a Trainium2 kernel written in Bass

```python
import jax, jax.numpy as jnp
from jax import lax
import numpy as np
import jax
import jax.numpy as jnp

D_MODEL = 1024
BATCH = 1
SEQ = 256
DEPTH = 1

D_MIX = D_MODEL
ATT_HEADS = 8
ATT_HEAD_DIM = 64
ATT_WIDTH = ATT_HEADS * ATT_HEAD_DIM
DILATED_PATTERNS = ((128, 1), (512, 4), (2048, 16))
Q_BLOCK = 128
ROPE_THETA = 10000.0
GLA_HEADS = 4
GLA_KEY_DIM = 64
GLA_VAL_DIM = 128
GLA_KEY_WIDTH = GLA_HEADS * GLA_KEY_DIM
GLA_VAL_WIDTH = GLA_HEADS * GLA_VAL_DIM
GLA_GATE_RANK = 16
GLA_GATE_NORMALIZER = 16.0
GLA_CHUNK = 64
IN_SPLITS = (ATT_WIDTH, ATT_WIDTH, ATT_WIDTH, GLA_KEY_WIDTH, GLA_KEY_WIDTH,
             GLA_VAL_WIDTH, GLA_VAL_WIDTH, GLA_GATE_RANK)
D_IN = sum(IN_SPLITS)
N_EXPERTS = 32
TOP_K = 4
D_FF = D_MODEL
SWIGLU_LIMIT = 7.0
SWIGLU_ALPHA = 1.702
MOE_BLOCK = 128
NORM_EPS = 1e-6
N_MOD = 6


def rms_norm(x, g):
    xf = x.astype(jnp.float32)
    y = xf * lax.rsqrt(jnp.mean(xf * xf, axis=-1, keepdims=True) + NORM_EPS)
    return (y * g.astype(jnp.float32)).astype(x.dtype)

def rope(x, positions):
    half = x.shape[-1] // 2
    inv_freq = ROPE_THETA ** (-jnp.arange(half, dtype=jnp.float32) / half)
    ang = positions.astype(jnp.float32)[:, None] * inv_freq[None, :]
    cos, sin = jnp.cos(ang), jnp.sin(ang)
    xf = x.astype(jnp.float32)
    x1, x2 = xf[..., :half], xf[..., half:]
    return jnp.concatenate([x1 * cos - x2 * sin, x2 * cos + x1 * sin], axis=-1).astype(x.dtype)

def dilated_attention(q, k, v):
    B, H, S, hd = q.shape
    n_blk = S // Q_BLOCK

    def block(i):
        q0 = i * Q_BLOCK
        qb = lax.dynamic_slice_in_dim(q, q0, Q_BLOCK, axis=2).astype(jnp.float32)
        t = q0 + jnp.arange(Q_BLOCK)
        outs, lses = [], []
        for window, dil in DILATED_PATTERNS:
            offs = jnp.arange(window // dil + 1) * dil
            idx = t[:, None] - offs[None, :]
            valid = idx >= 0
            idx = jnp.maximum(idx, 0)
            kg = jnp.take(k, idx, axis=2).astype(jnp.float32)
            vg = jnp.take(v, idx, axis=2).astype(jnp.float32)
            s = jnp.einsum('bhqd,bhqjd->bhqj', qb, kg)
            s = jnp.where(valid, s, -jnp.inf)
            m = jnp.max(s, axis=-1, keepdims=True)
            p = jnp.exp(s - m)
            l = jnp.sum(p, axis=-1, keepdims=True)
            outs.append(jnp.einsum('bhqj,bhqjd->bhqd', p, vg) / l)
            lses.append(m + jnp.log(l))
        w = jax.nn.softmax(jnp.stack(lses, axis=0), axis=0)
        return jnp.sum(w * jnp.stack(outs, axis=0), axis=0)

    o = lax.map(block, jnp.arange(n_blk))
    o = o.transpose(1, 0, 3, 2, 4).reshape(B, S, H * hd)
    return o.astype(q.dtype)

def gated_linear_attention(q, k, v, log_a):
    B, H, S, dk = q.shape
    dv = v.shape[-1]
    C = GLA_CHUNK
    N = S // C
    qf = q.astype(jnp.float32).reshape(B, H, N, C, dk) * (dk ** -0.5)
    kf = k.astype(jnp.float32).reshape(B, H, N, C, dk)
    vf = v.astype(jnp.float32).reshape(B, H, N, C, dv)
    b = jnp.cumsum(log_a.reshape(B, H, N, C, dk), axis=3)
    b_last = b[:, :, :, -1:, :]
    q_dec = qf * jnp.exp(b)
    att = jnp.einsum('bhncd,bhnjd->bhncj', q_dec, kf * jnp.exp(-b))
    causal = jnp.tril(jnp.ones((C, C), dtype=bool))
    att = jnp.where(causal, att, 0.0)
    o_intra = jnp.einsum('bhncj,bhnje->bhnce', att, vf)
    u = jnp.einsum('bhncd,bhnce->nbhde', kf * jnp.exp(b_last - b), vf)
    a = jnp.exp(b_last[:, :, :, 0, :]).transpose(2, 0, 1, 3)

    def step(state, inp):
        a_n, u_n = inp
        return a_n[..., None] * state + u_n, state

    _, s_prev = lax.scan(step, jnp.zeros((B, H, dk, dv), jnp.float32), (a, u))
    o_inter = jnp.einsum('bhncd,nbhde->bhnce', q_dec, s_prev)
    return (o_intra + o_inter).reshape(B, H, S, dv)

def hybrid_mixer(h, w_in, w_gate_lr, b_gate, g_gla, w_out):
    B, S, _ = h.shape
    proj = h @ w_in
    split_points = [int(s) for s in np.cumsum(IN_SPLITS)[:-1]]
    q_a, k_a, v_a, q_g, k_g, v_g, r_g, g_lr = jnp.split(proj, split_points, axis=-1)

    def heads(t, n):
        return t.reshape(B, S, n, -1).transpose(0, 2, 1, 3)

    pos = jnp.arange(S)
    qa = rope(heads(q_a, ATT_HEADS), pos) * (ATT_HEAD_DIM ** -0.5)
    ka = rope(heads(k_a, ATT_HEADS), pos)
    o_att = dilated_attention(qa, ka, heads(v_a, ATT_HEADS))
    gate_logit = (g_lr @ w_gate_lr + b_gate).astype(jnp.float32)
    log_a = jax.nn.log_sigmoid(gate_logit) / GLA_GATE_NORMALIZER
    o_g = gated_linear_attention(heads(q_g, GLA_HEADS), heads(k_g, GLA_HEADS),
                                 heads(v_g, GLA_HEADS), heads(log_a, GLA_HEADS))
    o_g = rms_norm(o_g, g_gla)
    o_g = o_g.transpose(0, 2, 1, 3).reshape(B, S, GLA_VAL_WIDTH).astype(h.dtype) * jax.nn.silu(r_g)
    return jnp.concatenate([o_att, o_g], axis=-1) @ w_out

def moe_ffn(h, router_w, router_b, w_gate_up, b_gate_up, w_down, b_down):
    B, S, D = h.shape
    T = B * S
    xt = h.reshape(T, D)
    logits = (xt @ router_w + router_b).astype(jnp.float32)
    top_v, top_i = lax.top_k(logits, TOP_K)
    gates = jax.nn.softmax(top_v, axis=-1)
    A = T * TOP_K
    e_flat = top_i.reshape(A)
    tok_flat = jnp.arange(A, dtype=jnp.int32) // TOP_K
    g_flat = gates.reshape(A)
    order = jnp.argsort(e_flat)
    e_sorted = e_flat[order]
    counts = jnp.bincount(e_flat, length=N_EXPERTS)
    start = jnp.cumsum(counts) - counts
    padded = (counts + MOE_BLOCK - 1) // MOE_BLOCK * MOE_BLOCK
    pend = jnp.cumsum(padded)
    pstart = pend - padded
    dest = pstart[e_sorted] + jnp.arange(A, dtype=jnp.int32) - start[e_sorted]
    n_blocks = -(-(A + N_EXPERTS * (MOE_BLOCK - 1)) // MOE_BLOCK)
    P = n_blocks * MOE_BLOCK
    tok_buf = jnp.full((P,), T, dtype=jnp.int32).at[dest].set(tok_flat[order])
    gate_buf = jnp.zeros((P,), jnp.float32).at[dest].set(g_flat[order])
    blk_e = jnp.minimum(jnp.searchsorted(pend, jnp.arange(n_blocks) * MOE_BLOCK, side='right'),
                        N_EXPERTS - 1)
    xpad = jnp.concatenate([xt, jnp.zeros((1, D), xt.dtype)], axis=0)

    def expert_block(args):
        idx, e = args
        xb = xpad[idx]
        gu = xb @ w_gate_up[e] + b_gate_up[e]
        x_glu = jnp.minimum(gu[:, ::2], SWIGLU_LIMIT)
        x_lin = jnp.clip(gu[:, 1::2], -SWIGLU_LIMIT, SWIGLU_LIMIT)
        act = x_glu * jax.nn.sigmoid(SWIGLU_ALPHA * x_glu) * (x_lin + 1.0)
        return act @ w_down[e] + b_down[e]

    out_buf = lax.map(expert_block, (tok_buf.reshape(n_blocks, MOE_BLOCK), blk_e))
    out_buf = out_buf.reshape(P, D) * gate_buf[:, None].astype(out_buf.dtype)
    out = jnp.zeros((T + 1, D), out_buf.dtype).at[tok_buf].add(out_buf)
    return out[:T].reshape(B, S, D)

def first_inputs(seed: int = 0) -> dict:
    key = jax.random.key(seed)
    ks = jax.random.split(key, 20)
    L = DEPTH

    def nrm(k, shape, scale):
        return jax.random.normal(k, shape, jnp.float32) * scale

    return {
        "x": nrm(ks[0], (BATCH, SEQ, D_MODEL), 1.0),
        "c": nrm(ks[1], (BATCH, D_MODEL), 1.0),
        "w_mod": nrm(ks[2], (L, D_MODEL, N_MOD * D_MODEL), 0.5 * D_MODEL ** -0.5),
        "b_mod": nrm(ks[3], (L, N_MOD * D_MODEL), 0.02),
        "g_pre_mix": 1.0 + nrm(ks[4], (L, D_MODEL), 0.05),
        "w_in": nrm(ks[5], (L, D_MODEL, D_IN), D_MODEL ** -0.5),
        "w_gate_lr": nrm(ks[6], (L, GLA_GATE_RANK, GLA_KEY_WIDTH), GLA_GATE_RANK ** -0.5),
        "b_gate": nrm(ks[7], (L, GLA_KEY_WIDTH), 0.1),
        "g_gla": 1.0 + nrm(ks[8], (L, GLA_VAL_DIM), 0.05),
        "w_out": nrm(ks[9], (L, D_MIX, D_MODEL), D_MIX ** -0.5),
        "g_post_mix": 1.0 + nrm(ks[10], (L, D_MODEL), 0.05),
        "g_pre_ffn": 1.0 + nrm(ks[11], (L, D_MODEL), 0.05),
        "router_w": nrm(ks[12], (L, D_MODEL, N_EXPERTS), D_MODEL ** -0.5),
        "router_b": nrm(ks[13], (L, N_EXPERTS), 0.01),
        "w_gate_up": nrm(ks[14], (L, N_EXPERTS, D_MODEL, 2 * D_FF), D_MODEL ** -0.5),
        "b_gate_up": nrm(ks[15], (L, N_EXPERTS, 2 * D_FF), 0.02),
        "w_down": nrm(ks[16], (L, N_EXPERTS, D_FF, D_MODEL), D_FF ** -0.5),
        "b_down": nrm(ks[17], (L, N_EXPERTS, D_MODEL), 0.02),
        "g_post_ffn": 1.0 + nrm(ks[18], (L, D_MODEL), 0.05),
    }

def first_block(x, c, w_mod, b_mod, g_pre_mix, w_in, w_gate_lr, b_gate, g_gla, w_out,
              g_post_mix, g_pre_ffn, router_w, router_b, w_gate_up, b_gate_up,
              w_down, b_down, g_post_ffn):
    for l in range(DEPTH):
        mod = jax.nn.silu(c) @ w_mod[l] + b_mod[l]
        shift1, scale1, gate1, shift2, scale2, gate2 = jnp.split(mod[:, None, :], N_MOD, axis=-1)
        h = rms_norm(x, g_pre_mix[l]) * (1.0 + scale1) + shift1
        y = hybrid_mixer(h, w_in[l], w_gate_lr[l], b_gate[l], g_gla[l], w_out[l])
        x = x + gate1 * rms_norm(y, g_post_mix[l])
        h = rms_norm(x, g_pre_ffn[l]) * (1.0 + scale2) + shift2
        y = moe_ffn(h, router_w[l], router_b[l], w_gate_up[l], b_gate_up[l], w_down[l], b_down[l])
        x = x + gate2 * rms_norm(y, g_post_ffn[l])
    return x


DN_HEADS = 4
DN_HEAD_DIM = 128
DN_WIDTH = DN_HEADS * DN_HEAD_DIM
DN_CONV = 4
DN_CHUNK = 64
MB_HEADS = 8
MB_HEAD_DIM = 64
MB_WIDTH = MB_HEADS * MB_HEAD_DIM
MB_BLOCK = 256
MB_TOPK = 3
MB_QCHUNK = 32
N_BRANCH = 2
IN_COLS = 4 * DN_WIDTH + 2 * DN_HEADS + 4 * MB_WIDTH + N_BRANCH * D_MODEL


def rms_norm_2(x, gain):
    xf = x.astype(jnp.float32)
    y = xf * lax.rsqrt(jnp.mean(xf * xf, axis=-1, keepdims=True) + NORM_EPS)
    return (y * gain.astype(jnp.float32)).astype(x.dtype)

def l2_normalize(x):
    xf = x.astype(jnp.float32)
    return (xf * lax.rsqrt(jnp.sum(xf * xf, axis=-1, keepdims=True) + NORM_EPS)).astype(x.dtype)

def causal_depthwise_conv(x, w):
    k_width, channels = w.shape
    return lax.conv_general_dilated(
        x, w[:, None, :].astype(x.dtype), window_strides=(1,),
        padding=((k_width - 1, 0),), dimension_numbers=('NWC', 'WIO', 'NWC'),
        feature_group_count=channels)

def to_heads(t, n_heads):
    b, s, _ = t.shape
    return t.reshape(b, s, n_heads, -1).transpose(0, 2, 1, 3)

def gated_delta_rule_chunked(q, k, v, g, beta):
    out_dtype = v.dtype
    f32 = jnp.float32
    b, h, s, dk = k.shape
    dv = v.shape[-1]
    c = DN_CHUNK
    n = s // c
    beta = beta.astype(f32)[..., None]
    qf = (q.astype(f32) * (dk ** -0.5)).reshape(b, h, n, c, dk)
    kf = k.astype(f32)
    vf = v.astype(f32)
    k_beta = (kf * beta).reshape(b, h, n, c, dk)
    v_beta = (vf * beta).reshape(b, h, n, c, dv)
    kf = kf.reshape(b, h, n, c, dk)
    g = jnp.cumsum(g.astype(f32).reshape(b, h, n, c), axis=-1)
    causal = jnp.tril(jnp.ones((c, c), dtype=bool))
    strict = jnp.tril(jnp.ones((c, c), dtype=bool), k=-1)
    decay = jnp.exp(jnp.where(causal, g[..., :, None] - g[..., None, :], -jnp.inf))
    a = jnp.where(strict, jnp.einsum('bhnid,bhnjd->bhnij', k_beta, kf) * decay, 0.0)
    eye = jnp.eye(c, dtype=f32)
    t_inv = lax.linalg.triangular_solve(eye + a, jnp.broadcast_to(eye, a.shape),
                                        left_side=True, lower=True)
    u = t_inv @ v_beta
    w = t_inv @ (k_beta * jnp.exp(g)[..., None])
    qk = jnp.einsum('bhnid,bhnjd->bhnij', qf, kf) * decay

    def chunk_step(state, xs):
        q_i, k_i, u_i, w_i, qk_i, g_i = xs
        v_new = u_i - w_i @ state
        o_i = (q_i * jnp.exp(g_i)[..., None]) @ state + qk_i @ v_new
        g_last = g_i[..., -1:]
        state = state * jnp.exp(g_last)[..., None] + jnp.einsum(
            'bhcd,bhce->bhde', k_i * jnp.exp(g_last - g_i)[..., None], v_new)
        return state, o_i

    xs = tuple(jnp.moveaxis(t_, 2, 0) for t_ in (qf, kf, u, w, qk, g))
    state0 = jnp.zeros((b, h, dk, dv), f32)
    _, o = lax.scan(chunk_step, state0, xs)
    return jnp.moveaxis(o, 0, 2).reshape(b, h, s, dv).astype(out_dtype)

def moba_attention(q, k, v):
    b, h, s, dh = q.shape
    nb = s // MB_BLOCK
    n_sel = min(MB_TOPK, nb)
    scale = dh ** -0.5
    kb = k.reshape(b, h, nb, MB_BLOCK, dh)
    vb = v.reshape(b, h, nb, MB_BLOCK, dh)
    k_mean = jnp.mean(kb.astype(jnp.float32), axis=3).astype(k.dtype)
    bi = jnp.arange(b)[:, None, None, None]
    hi = jnp.arange(h)[None, :, None, None]
    blk_ids = jnp.arange(nb)

    def attend_chunk(ci):
        start = ci * MB_QCHUNK
        own = start // MB_BLOCK
        q_c = lax.dynamic_slice_in_dim(q, start, MB_QCHUNK, axis=2)
        q_pos = start + jnp.arange(MB_QCHUNK)
        gate = jnp.einsum('bhqd,bhnd->bhqn', q_c, k_mean).astype(jnp.float32)
        gate = jnp.where(blk_ids < own, gate, -jnp.inf)
        _, sel = lax.top_k(gate, n_sel)
        sel_ok = sel < own
        k_sel = kb[bi, hi, sel]
        v_sel = vb[bi, hi, sel]
        s_sel = jnp.einsum('bhqd,bhqjtd->bhqjt', q_c, k_sel).astype(jnp.float32) * scale
        s_sel = jnp.where(sel_ok[..., None], s_sel, -jnp.inf).reshape(b, h, MB_QCHUNK, n_sel * MB_BLOCK)
        k_own = lax.dynamic_slice_in_dim(k, own * MB_BLOCK, MB_BLOCK, axis=2)
        v_own = lax.dynamic_slice_in_dim(v, own * MB_BLOCK, MB_BLOCK, axis=2)
        k_pos = own * MB_BLOCK + jnp.arange(MB_BLOCK)
        s_own = jnp.einsum('bhqd,bhtd->bhqt', q_c, k_own).astype(jnp.float32) * scale
        s_own = jnp.where(k_pos[None, :] <= q_pos[:, None], s_own, -jnp.inf)
        p = jax.nn.softmax(jnp.concatenate([s_own, s_sel], axis=-1), axis=-1).astype(v.dtype)
        p_own = p[..., :MB_BLOCK]
        p_sel = p[..., MB_BLOCK:].reshape(b, h, MB_QCHUNK, n_sel, MB_BLOCK)
        return (jnp.einsum('bhqt,bhtd->bhqd', p_own, v_own)
                + jnp.einsum('bhqjt,bhqjtd->bhqd', p_sel, v_sel))

    out = lax.map(attend_chunk, jnp.arange(s // MB_QCHUNK))
    return jnp.moveaxis(out, 0, 2).reshape(b, h, s, dh)

def hybrid_layer(x, c, w_ada, b_ada, g_pre, g_post, w_in, conv_w, a_log, dt_bias,
                 dn_norm_g, w_proj_dn, w_proj_mb, w_out):
    b, s, _ = x.shape
    f32 = jnp.float32
    shift, scale, gate = jnp.split(jax.nn.silu(c) @ w_ada + b_ada, 3, axis=-1)
    h = rms_norm_2(x, g_pre) * (1 + scale[:, None, :]) + shift[:, None, :]
    sizes = (3 * DN_WIDTH, DN_WIDTH, DN_HEADS, DN_HEADS, 3 * MB_WIDTH, MB_WIDTH, N_BRANCH * D_MODEL)
    cuts = np.cumsum(sizes)[:-1].tolist()
    qkv_dn, z_dn, beta_logit, a_logit, qkv_mb, z_mb, merge_logit = jnp.split(h @ w_in, cuts, axis=-1)

    qkv_dn = jax.nn.silu(causal_depthwise_conv(qkv_dn, conv_w))
    q_dn, k_dn, v_dn = (to_heads(t_, DN_HEADS) for t_ in jnp.split(qkv_dn, 3, axis=-1))
    beta = jax.nn.sigmoid(beta_logit).transpose(0, 2, 1)
    g = (-jnp.exp(a_log.astype(f32))
         * jax.nn.softplus(a_logit.astype(f32) + dt_bias.astype(f32))).transpose(0, 2, 1)
    o_dn = gated_delta_rule_chunked(l2_normalize(q_dn), l2_normalize(k_dn), v_dn, g, beta)
    o_dn = rms_norm_2(o_dn.transpose(0, 2, 1, 3), dn_norm_g) * jax.nn.silu(
        z_dn.reshape(b, s, DN_HEADS, DN_HEAD_DIM))
    y_dn = o_dn.reshape(b, s, DN_WIDTH) @ w_proj_dn

    pad = (-s) % MB_BLOCK
    q_mb, k_mb, v_mb = (jnp.pad(to_heads(t_, MB_HEADS), ((0, 0), (0, 0), (0, pad), (0, 0)))
                        for t_ in jnp.split(qkv_mb, 3, axis=-1))
    o_mb = moba_attention(q_mb, k_mb, v_mb)[:, :, :s]
    o_mb = o_mb.transpose(0, 2, 1, 3).reshape(b, s, MB_WIDTH) * jax.nn.silu(z_mb)
    y_mb = o_mb @ w_proj_mb

    gate_dn, gate_mb = jnp.split(jax.nn.sigmoid(merge_logit), N_BRANCH, axis=-1)
    mixed = (gate_dn * y_dn + gate_mb * y_mb) @ w_out
    return x + gate[:, None, :] * rms_norm_2(mixed, g_post)

def second_inputs(seed: int = 0) -> dict:
    key = jax.random.key(seed)
    ks = jax.random.split(key, 16)
    nrm = jax.random.normal
    d = D_MODEL
    dt = jnp.exp(jax.random.uniform(ks[9], (DEPTH, DN_HEADS), minval=np.log(1e-3), maxval=np.log(1e-1)))
    return {
        'x': nrm(ks[0], (BATCH, SEQ, d), jnp.float32),
        'c': nrm(ks[1], (BATCH, d), jnp.float32),
        'w_ada': nrm(ks[2], (DEPTH, d, 3 * d), jnp.float32) * (0.5 * d ** -0.5),
        'b_ada': nrm(ks[3], (DEPTH, 3 * d), jnp.float32) * 0.1,
        'g_pre': 1.0 + 0.02 * nrm(ks[4], (DEPTH, d), jnp.float32),
        'g_post': 1.0 + 0.02 * nrm(ks[5], (DEPTH, d), jnp.float32),
        'w_in': nrm(ks[6], (DEPTH, d, IN_COLS), jnp.float32) * d ** -0.5,
        'conv_w': nrm(ks[7], (DEPTH, DN_CONV, 3 * DN_WIDTH), jnp.float32) * DN_CONV ** -0.5,
        'a_log': jnp.log(jax.random.uniform(ks[8], (DEPTH, DN_HEADS), minval=1.0, maxval=16.0)),
        'dt_bias': dt + jnp.log(-jnp.expm1(-dt)),
        'dn_norm_g': 1.0 + 0.02 * nrm(ks[10], (DEPTH, DN_HEAD_DIM), jnp.float32),
        'w_proj_dn': nrm(ks[11], (DEPTH, DN_WIDTH, d), jnp.float32) * DN_WIDTH ** -0.5,
        'w_proj_mb': nrm(ks[12], (DEPTH, MB_WIDTH, d), jnp.float32) * MB_WIDTH ** -0.5,
        'w_out': nrm(ks[13], (DEPTH, d, d), jnp.float32) * d ** -0.5,
    }

def second_block(x, c, w_ada, b_ada, g_pre, g_post, w_in, conv_w, a_log, dt_bias,
              dn_norm_g, w_proj_dn, w_proj_mb, w_out):
    for l in range(DEPTH):
        x = hybrid_layer(x, c, w_ada[l], b_ada[l], g_pre[l], g_post[l], w_in[l], conv_w[l],
                         a_log[l], dt_bias[l], dn_norm_g[l], w_proj_dn[l], w_proj_mb[l], w_out[l])
    return x


DEPTH_3 = 2

CHUNK = 64
HGRN_BLOCK = 16
SB_BLOCK = 128
N_EVEN = (DEPTH_3 + 1) // 2
N_ODD = DEPTH_3 // 2
A_HEADS = 4
A_DK = 128
A_DV = 128
A_QK = A_HEADS * A_DK
A_V = A_HEADS * A_DV
B_HEADS = 4
B_HD = 128
B_WIDTH = B_HEADS * B_HD
P_EVEN = 2 * A_QK + 2 * A_V + 3 * B_WIDTH
MIX_EVEN = A_V + B_WIDTH
C_HEADS = 8
C_DQK = 64
C_DV = 128
C_QK = C_HEADS * C_DQK
C_V = C_HEADS * C_DV
C_CONV = 4
P_ODD = 2 * C_QK + 2 * C_V + 2 * C_HEADS
FFN_DIM = 2816
FFN_CONV = 3
EPS = 1e-6


def rmsnorm(x, g):
    xf = x.astype(jnp.float32)
    y = xf * lax.rsqrt(jnp.mean(xf * xf, axis=-1, keepdims=True) + EPS)
    return y * g.astype(jnp.float32)

def modulate(x, g, shift, scale):
    return (rmsnorm(x, g) * (1.0 + scale) + shift).astype(x.dtype)

def head_rmsnorm(o, g):
    b, t, h, d = o.shape
    y = o * lax.rsqrt(jnp.mean(o * o, axis=-1, keepdims=True) + EPS)
    return y.reshape(b, t, h * d) * g.astype(jnp.float32)

def causal_dwconv(x, w, b):
    k = w.shape[0]
    y = lax.conv_general_dilated(x, w[:, None, :].astype(x.dtype), window_strides=(1,),
                                 padding=[(k - 1, 0)], dimension_numbers=('NWC', 'WIO', 'NWC'),
                                 feature_group_count=x.shape[-1])
    return y + b.astype(x.dtype)

def to_chunks(a, size):
    bsz, t = a.shape[0], a.shape[1]
    a = a.reshape((bsz, t // size, size) + a.shape[2:])
    return jnp.swapaxes(jnp.moveaxis(a, 1, 0), 2, 3)

def from_chunks(o):
    n, bsz, h, l, d = o.shape
    return jnp.moveaxis(jnp.swapaxes(o, 2, 3), 0, 1).reshape(bsz, n * l, h, d)

def hgrn2_scan(q, log_f, k, v):
    bsz = q.shape[0]
    mask = jnp.tril(jnp.ones((HGRN_BLOCK, HGRN_BLOCK), dtype=bool))

    def step(state, inp):
        qc, lf, kc, vc = inp
        b = jnp.cumsum(lf, axis=2)
        rel = jnp.where(mask[:, :, None], b[:, :, :, None, :] - b[:, :, None, :, :], -jnp.inf)
        scores = jnp.einsum('bhtd,bhsd,bhtsd->bhts', qc, kc, jnp.exp(rel))
        o = (jnp.einsum('bhts,bhse->bhte', scores, vc)
             + jnp.einsum('bhtd,bhde->bhte', qc * jnp.exp(b), state))
        b_end = b[:, :, -1:, :]
        state = (jnp.exp(b_end[:, :, 0, :])[..., None] * state
                 + jnp.einsum('bhsd,bhse->bhde', kc * jnp.exp(b_end - b), vc))
        return state, o

    s0 = jnp.zeros((bsz, A_HEADS, A_DK, A_DV), jnp.float32)
    xs = (to_chunks(q, HGRN_BLOCK), to_chunks(log_f, HGRN_BLOCK),
          to_chunks(k, HGRN_BLOCK), to_chunks(v, HGRN_BLOCK))
    _, o = lax.scan(step, s0, xs)
    return from_chunks(o)

def stick_breaking(q, k, v):
    bsz, t, h, hd = q.shape
    nb = t // SB_BLOCK

    def blocks(a):
        return a.reshape(bsz, nb, SB_BLOCK, h, hd).transpose(0, 3, 1, 2, 4)

    qb = blocks(q * (hd ** -0.5))
    kb = blocks(k)
    vb = blocks(v)
    incl = jnp.tril(jnp.ones((SB_BLOCK, SB_BLOCK), jnp.float32))
    strict = jnp.tril(jnp.ones((SB_BLOCK, SB_BLOCK), dtype=bool), k=-1)
    out = jnp.zeros((bsz, h, nb, SB_BLOCK, hd), jnp.float32)
    acc = jnp.zeros((bsz, h, nb, SB_BLOCK), jnp.float32)
    for d in range(nb):
        z = jnp.einsum('bhnqd,bhnkd->bhnqk', qb[:, :, d:], kb[:, :, :nb - d]).astype(jnp.float32)
        lk = jax.nn.log_sigmoid(-z)
        if d == 0:
            lk = jnp.where(strict, lk, 0.0)
        r = jnp.einsum('bhnqj,js->bhnqs', lk, incl) + acc[:, :, d:, :, None]
        a = jnp.exp(z + r)
        if d == 0:
            a = jnp.where(strict, a, 0.0)
        out = out.at[:, :, d:].add(
            jnp.einsum('bhnqk,bhnkd->bhnqd', a, vb[:, :, :nb - d].astype(jnp.float32)))
        acc = acc.at[:, :, d:].set(r[..., 0])
    return out.transpose(0, 2, 3, 1, 4).reshape(bsz, t, h, hd)

def mlstm_scan(q, k, v, ig, lf):
    bsz = q.shape[0]
    mask = jnp.tril(jnp.ones((CHUNK, CHUNK), dtype=bool))

    def step(carry, inp):
        cmem, nvec, m = carry
        qc, kc, vc, igc, lfc = inp
        b = jnp.cumsum(lfc, axis=-1)
        log_d = jnp.where(mask, b[..., :, None] - b[..., None, :] + igc[..., None, :], -jnp.inf)
        log_inter = b + m[..., None]
        m_t = jnp.maximum(log_inter, jnp.max(log_d, axis=-1))
        w = jnp.einsum('bhtd,bhsd->bhts', qc, kc) * jnp.exp(log_d - m_t[..., None])
        w_inter = jnp.exp(log_inter - m_t)
        num = (jnp.einsum('bhts,bhse->bhte', w, vc)
               + w_inter[..., None] * jnp.einsum('bhtd,bhde->bhte', qc, cmem))
        den = jnp.sum(w, axis=-1) + w_inter * jnp.einsum('bhtd,bhd->bht', qc, nvec)
        hc = num / jnp.maximum(jnp.abs(den), jnp.exp(-m_t))[..., None]
        m_new = m_t[..., -1]
        w_end = jnp.exp(b[..., -1:] - b + igc - m_new[..., None])
        decay = jnp.exp(b[..., -1] + m - m_new)
        cmem = decay[..., None, None] * cmem + jnp.einsum('bhs,bhsd,bhse->bhde', w_end, kc, vc)
        nvec = decay[..., None] * nvec + jnp.einsum('bhs,bhsd->bhd', w_end, kc)
        return (cmem, nvec, m_new), hc

    init = (jnp.zeros((bsz, C_HEADS, C_DQK, C_DV), jnp.float32),
            jnp.zeros((bsz, C_HEADS, C_DQK), jnp.float32),
            jnp.zeros((bsz, C_HEADS), jnp.float32))
    xs = (to_chunks(q, CHUNK), to_chunks(k, CHUNK), to_chunks(v, CHUNK),
          to_chunks(ig, CHUNK), to_chunks(lf, CHUNK))
    _, hc = lax.scan(step, init, xs)
    return from_chunks(hc)

def even_mixer(h, w_in, lb, norm_g, w_out):
    bsz, t, _ = h.shape
    p = jnp.matmul(h, w_in).astype(jnp.float32)
    splits = [A_QK, 2 * A_QK, 2 * A_QK + A_V, 2 * A_QK + 2 * A_V,
              2 * A_QK + 2 * A_V + B_WIDTH, 2 * A_QK + 2 * A_V + 2 * B_WIDTH]
    qa, fa, ia, ga, qb, kb, vb = jnp.split(p, splits, axis=-1)
    lb_h = lb.astype(jnp.float32).reshape(A_HEADS, A_DK)
    zf = fa.reshape(bsz, t, A_HEADS, A_DK)
    log_f = jnp.logaddexp(jnp.log(lb_h), jnp.log1p(-lb_h) + jax.nn.log_sigmoid(zf))
    k_a = (1.0 - lb_h) * jax.nn.sigmoid(-zf)
    o_a = hgrn2_scan(qa.reshape(bsz, t, A_HEADS, A_DK), log_f, k_a, ia.reshape(bsz, t, A_HEADS, A_DV))
    o_a = head_rmsnorm(o_a, norm_g) * jax.nn.silu(ga)
    o_b = stick_breaking(qb.reshape(bsz, t, B_HEADS, B_HD), kb.reshape(bsz, t, B_HEADS, B_HD),
                         vb.reshape(bsz, t, B_HEADS, B_HD)).reshape(bsz, t, B_WIDTH)
    o = jnp.concatenate([o_a, o_b], axis=-1).astype(h.dtype)
    return jnp.matmul(o, w_out)

def odd_mixer(h, w_in, conv_w, conv_b, gate_b, norm_g, w_out):
    bsz, t, _ = h.shape
    p = jnp.matmul(h, w_in).astype(jnp.float32)
    qk, v, og, gates = jnp.split(p, [2 * C_QK, 2 * C_QK + C_V, 2 * C_QK + 2 * C_V], axis=-1)
    qk = jax.nn.silu(causal_dwconv(qk, conv_w.astype(jnp.float32), conv_b.astype(jnp.float32)))
    q, k = jnp.split(qk, 2, axis=-1)
    q = q.reshape(bsz, t, C_HEADS, C_DQK)
    k = k.reshape(bsz, t, C_HEADS, C_DQK) * (C_DQK ** -0.5)
    gates = gates + gate_b.astype(jnp.float32)
    ig = gates[..., :C_HEADS]
    lf = jax.nn.log_sigmoid(gates[..., C_HEADS:])
    hc = mlstm_scan(q, k, v.reshape(bsz, t, C_HEADS, C_DV), ig, lf)
    o = head_rmsnorm(hc, norm_g) * jax.nn.sigmoid(og)
    return jnp.matmul(o.astype(h.dtype), w_out)

def conv_glu_ffn(h, w_in, conv_w, conv_b, w_out):
    u = jnp.matmul(h, w_in)
    a, g = jnp.split(u, 2, axis=-1)
    a = causal_dwconv(a, conv_w, conv_b)
    return jnp.matmul(jax.nn.gelu(a) * g, w_out)

def third_inputs(seed: int = 0) -> dict:
    key = jax.random.key(seed)
    ks = jax.random.split(key, 24)

    def nrm(k, shape, scale):
        return jax.random.normal(k, shape, jnp.float32) * scale

    d = D_MODEL
    gate_b = jnp.concatenate([
        nrm(ks[13], (N_ODD, C_HEADS), 0.1),
        jnp.linspace(3.0, 6.0, C_HEADS, dtype=jnp.float32)[None, :] + nrm(ks[14], (N_ODD, C_HEADS), 0.1)], axis=-1)
    return {
        'x': nrm(ks[0], (BATCH, SEQ, d), 1.0),
        'c': nrm(ks[1], (BATCH, d), 1.0),
        'ada_w': nrm(ks[2], (DEPTH_3, d, 6 * d), 0.5 * d ** -0.5),
        'ada_b': nrm(ks[3], (DEPTH_3, 6 * d), 0.02),
        'norm_mix_g': 1.0 + nrm(ks[4], (DEPTH_3, d), 0.02),
        'norm_ffn_g': 1.0 + nrm(ks[5], (DEPTH_3, d), 0.02),
        'even_w_in': nrm(ks[6], (N_EVEN, d, P_EVEN), d ** -0.5),
        'even_w_out': nrm(ks[7], (N_EVEN, MIX_EVEN, d), MIX_EVEN ** -0.5),
        'hgrn_lb': nrm(ks[8], (N_EVEN, A_QK), 0.5),
        'hgrn_norm_g': 1.0 + nrm(ks[9], (N_EVEN, A_V), 0.02),
        'odd_w_in': nrm(ks[10], (N_ODD, d, P_ODD), d ** -0.5),
        'odd_conv_w': nrm(ks[11], (N_ODD, C_CONV, 2 * C_QK), C_CONV ** -0.5),
        'odd_conv_b': nrm(ks[12], (N_ODD, 2 * C_QK), 0.02),
        'odd_gate_b': gate_b,
        'odd_norm_g': 1.0 + nrm(ks[15], (N_ODD, C_V), 0.02),
        'odd_w_out': nrm(ks[16], (N_ODD, C_V, d), C_V ** -0.5),
        'ffn_w_in': nrm(ks[17], (DEPTH_3, d, 2 * FFN_DIM), d ** -0.5),
        'ffn_conv_w': nrm(ks[18], (DEPTH_3, FFN_CONV, FFN_DIM), FFN_CONV ** -0.5),
        'ffn_conv_b': nrm(ks[19], (DEPTH_3, FFN_DIM), 0.02),
        'ffn_w_out': nrm(ks[20], (DEPTH_3, FFN_DIM, d), FFN_DIM ** -0.5),
        'final_g': 1.0 + nrm(ks[21], (d,), 0.02),
    }

def third_block(x, c, ada_w, ada_b, norm_mix_g, norm_ffn_g, even_w_in, even_w_out, hgrn_lb,
              hgrn_norm_g, odd_w_in, odd_conv_w, odd_conv_b, odd_gate_b, odd_norm_g, odd_w_out,
              ffn_w_in, ffn_conv_w, ffn_conv_b, ffn_w_out, final_g):
    lb_all = jnp.cumsum(jax.nn.softmax(hgrn_lb.astype(jnp.float32), axis=0), axis=0)
    lb_all = lb_all - lb_all[:1]
    cs = jax.nn.silu(c)
    for layer in range(DEPTH_3):
        j = layer // 2
        mod = jnp.matmul(cs, ada_w[layer]) + ada_b[layer]
        sh_m, sc_m, g_m, sh_f, sc_f, g_f = [m[:, None, :] for m in jnp.split(mod, 6, axis=-1)]
        h = modulate(x, norm_mix_g[layer], sh_m, sc_m)
        if layer % 2 == 0:
            y = even_mixer(h, even_w_in[j], lb_all[j], hgrn_norm_g[j], even_w_out[j])
        else:
            y = odd_mixer(h, odd_w_in[j], odd_conv_w[j], odd_conv_b[j], odd_gate_b[j],
                          odd_norm_g[j], odd_w_out[j])
        x = x + (g_m * y).astype(x.dtype)
        h = modulate(x, norm_ffn_g[layer], sh_f, sc_f)
        x = x + (g_f * conv_glu_ffn(h, ffn_w_in[layer], ffn_conv_w[layer], ffn_conv_b[layer],
                                    ffn_w_out[layer])).astype(x.dtype)
    return rmsnorm(x, final_g).astype(x.dtype)


def setup_inputs(seed=0):
    out = dict(first_inputs(seed))
    for name, value in second_inputs(seed + 1).items():
        if name != "x":
            out[name + "_2"] = value
    for name, value in third_inputs(seed + 2).items():
        if name != "x":
            out[name + "_3"] = value
    return out


def reference(
    x, c, w_mod, b_mod, g_pre_mix, w_in, w_gate_lr, b_gate, g_gla, w_out, g_post_mix, g_pre_ffn,
    router_w, router_b, w_gate_up, b_gate_up, w_down, b_down, g_post_ffn, c_2, w_ada_2, b_ada_2,
    g_pre_2, g_post_2, w_in_2, conv_w_2, a_log_2, dt_bias_2, dn_norm_g_2, w_proj_dn_2,
    w_proj_mb_2, w_out_2, c_3, ada_w_3, ada_b_3, norm_mix_g_3, norm_ffn_g_3, even_w_in_3,
    even_w_out_3, hgrn_lb_3, hgrn_norm_g_3, odd_w_in_3, odd_conv_w_3, odd_conv_b_3,
    odd_gate_b_3, odd_norm_g_3, odd_w_out_3, ffn_w_in_3, ffn_conv_w_3, ffn_conv_b_3,
    ffn_w_out_3, final_g_3,
):
    x = first_block(
        x, c, w_mod, b_mod, g_pre_mix, w_in, w_gate_lr, b_gate, g_gla, w_out, g_post_mix,
        g_pre_ffn, router_w, router_b, w_gate_up, b_gate_up, w_down, b_down, g_post_ffn,
    )
    x = second_block(
        x, c_2, w_ada_2, b_ada_2, g_pre_2, g_post_2, w_in_2, conv_w_2, a_log_2, dt_bias_2,
        dn_norm_g_2, w_proj_dn_2, w_proj_mb_2, w_out_2,
    )
    return third_block(
        x, c_3, ada_w_3, ada_b_3, norm_mix_g_3, norm_ffn_g_3, even_w_in_3, even_w_out_3,
        hgrn_lb_3, hgrn_norm_g_3, odd_w_in_3, odd_conv_w_3, odd_conv_b_3, odd_gate_b_3,
        odd_norm_g_3, odd_w_out_3, ffn_w_in_3, ffn_conv_w_3, ffn_conv_b_3, ffn_w_out_3,
        final_g_3,
    )


_drawn_inputs = setup_inputs


def setup_inputs(seed=0):
    import zlib

    import numpy as np

    out = dict(_drawn_inputs(seed))
    spreads = {}
    factors = {'b_gate': 2.745,
     'router_b': 2.98,
     'b_gate_up': 7.382,
     'b_down': 8.0,
     'g_post_ffn': 3.481,
     'g_pre_2': 5.869,
     'g_post_2': 8.0,
     'dn_norm_g_2': 8.0,
     'norm_mix_g_3': 6.987,
     'norm_ffn_g_3': 7.462,
     'hgrn_norm_g_3': 8.0,
     'odd_conv_b_3': 200.0,
     'odd_norm_g_3': 200.0,
     'ffn_conv_b_3': 8.0,
     'final_g_3': 21.263,
     'odd_conv_w_3': 3.844}
    for name, (base, spread) in spreads.items():
        noise = np.random.default_rng([zlib.crc32(name.encode()), seed]).standard_normal(out[name].shape)
        drawn = base * np.exp(spread * noise) if base else spread * noise
        out[name] = jnp.asarray(drawn.astype(out[name].dtype))
    for name, factor in factors.items():
        out[name] = (out[name] * factor).astype(out[name].dtype)
    return out
```

```python
from contextlib import ExitStack

import numpy as np

import concourse.bass as bass
from concourse import mybir

ALU = mybir.AluOpType
ACT = mybir.ActivationFunctionType
F32 = mybir.dt.float32
U32 = mybir.dt.uint32
I32 = mybir.dt.int32
AX = mybir.AxisListType
ADD, SUB, MUL, MAX, MIN = ALU.add, ALU.subtract, ALU.mult, ALU.max, ALU.min

D = 1024
EPS = 1e-6
NEG = -1e30
E_N = 32
FFN = 2816
FT = FFN // 128
CAP = 128



def const_table():
    p = np.arange(128)[:, None]
    f = np.arange(128)[None, :]
    same = (p // 64) == (f // 64)
    c = {}
    c["ident"] = p == f
    c["ones"] = np.ones((128, 128))
    c["U64"] = (p <= f) & same
    c["SU64"] = (p < f) & same
    c["UF"] = p <= f
    c["LF"] = p >= f
    c["SU"] = p < f
    c["B64"] = same
    c["NM"] = np.where(p < f, 0.0, NEG)
    for L in (1, 2, 4, 8, 16, 32, 64):
        c[f"H{L}"] = (p // (2 * L) == f // (2 * L)) & (p % (2 * L) < L) & (f % (2 * L) >= L)
    k = np.arange(256)[None, :]
    for t in (0, 1):
        d = (t * 128 + p) - k
        n = (d <= 128) * 1 + (d % 4 == 0) * 1 + (d % 16 == 0) * 1
        dil = np.where((d >= 0) & (n > 0), np.log(np.maximum(n, 1)), NEG)
        cau = np.where(d >= 0, 0.0, NEG)
        c[f"AB{t}"] = dil[:, :128 * (t + 1)]
        c[f"CB{t}"] = cau[:, :128 * (t + 1)]
    half = 32
    inv = (np.float32(10000.0) ** (-np.arange(half, dtype=np.float32) / np.float32(half))).astype(np.float32)
    ang = (np.arange(256, dtype=np.float32)[:, None] * inv[None, :]).astype(np.float32)
    for n, v in (("cos", np.cos(ang)), ("sin", np.sin(ang))):
        v = v.reshape(2, 128, half).transpose(1, 0, 2).reshape(128, 64)
        c[n] = v
        c[n + "q"] = v * 0.125
    c["iota"] = np.broadcast_to(np.arange(128)[None, :], (128, 128))
    t = np.arange(256)[None, :]
    c["R64"] = np.broadcast_to((t % 64 != 0), (128, 256))
    c["R128"] = np.broadcast_to((t % 128 != 0), (128, 256))
    at, cols, n = {}, [], 0
    for name, v in c.items():
        v = np.ascontiguousarray(v, dtype=np.float32)
        at[name] = (n, n + v.shape[1])
        n += v.shape[1]
        cols.append(v)
    return at, np.concatenate(cols, axis=1)


def sel_table():
    s = np.zeros((8, 8, 128), np.float32)
    for h in range(8):
        s[h, h, :] = 1.0
    return s.reshape(8, 1024)


VECS = [("c", 8), ("c_2", 8), ("c_3", 8), ("g_pre_mix", 8), ("g_pre_ffn", 8), ("g_pre_2", 8),
        ("norm_mix_g_3", 16), ("norm_ffn_g_3", 16), ("b_mod", 48), ("b_ada_2", 24), ("ada_b_3", 96),
        ("b_gate", 2), ("g_gla", 1), ("dn_norm_g_2", 1), ("hgrn_norm_g_3", 4), ("odd_norm_g_3", 8),
        ("conv_w_2", 48), ("odd_conv_w_3", 32), ("odd_conv_b_3", 8), ("ffn_conv_w_3", 132), ("ffn_conv_b_3", 44)]




def flat(x, out):
    if x is None:
        return out
    if isinstance(x, tuple):
        out.append(x)
    else:
        for y in x:
            flat(y, out)
    return out


class Queue:

    def __init__(self, sem, chain):
        self.sem, self.n, self.ops, self.pend, self.chain = sem, 0, [], [], chain

    @property
    def last(self):
        return (self.sem, self.n)

    def do(self, fn, after=None, sig=True):
        waits = flat(after, list(self.pend))
        if self.chain and self.n:
            waits.append(self.last)
        self.pend = []
        if sig:
            self.n += 1
        self.ops.append((waits, fn, (self.sem, 1) if sig else None))
        return self.last if sig else None

    def dma(self, out, in_, sem, after=None):
        waits = flat(after, list(self.pend))
        self.pend = []
        self.ops.append((waits, lambda e: e.dma_start(out, in_), (sem, 16)))

    def raw(self, fn):
        self.ops.append((None, fn, None))

    def emit(self, eng):
        seen = {}
        outer = None
        for waits, fn, inc in self.ops:
            if waits is None:
                outer = fn(eng, seen, outer)
                continue
            for sem, val in waits:
                if seen.get(sem.name, 0) < val:
                    eng.wait_ge(sem, val)
                    seen[sem.name] = val
            ins = fn(eng)
            if inc:
                ins.then_inc(inc[0], inc[1])

    def tt(self, out, a, b, op, after=None):
        return self.do(lambda e: e.tensor_tensor(out, a, b, op), after)

    def ts(self, out, a, s1, op0, s2=None, op1=None, after=None):
        if op1 is None:
            return self.do(lambda e: e.tensor_scalar(out, a, s1, None, op0), after)
        return self.do(lambda e: e.tensor_scalar(out, a, s1, s2, op0, op1), after)

    def stt(self, out, a, s, b, op0, op1, after=None):
        return self.do(lambda e: e.scalar_tensor_tensor(out=out, in0=a, scalar=s, in1=b, op0=op0, op1=op1), after)

    def ttr(self, out, a, b, op0, op1, init, acc, after=None):
        return self.do(lambda e: e.tensor_tensor_reduce(out, a, b, 1.0, init, op0, op1, acc), after)

    def cp(self, out, a, after=None):
        return self.do(lambda e: e.tensor_copy(out, a), after)

    def red(self, out, a, op, after=None):
        return self.do(lambda e: e.tensor_reduce(out, a, AX.X, op), after)

    def rec(self, out, a, after=None):
        return self.do(lambda e: e.reciprocal(out, a), after)

    def scan(self, out, a, b, init, op0, op1, after=None):
        return self.do(lambda e: e.tensor_tensor_scan(out, a, b, init, op0, op1), after)

    def cpred(self, out, mask, data, after=None):
        return self.do(lambda e: e.copy_predicated(out, mask, data), after)

    def mset(self, out, v, after=None):
        return self.do(lambda e: e.memset(out, v), after)

    def act(self, out, a, func, bias=None, scale=None, acc=None, after=None):
        kw = {}
        if bias is not None:
            kw["bias"] = bias
        if scale is not None:
            kw["scale"] = scale
        if acc is not None:
            kw["accum_out"] = acc
        return self.do(lambda e: e.activation(out, a, func, **kw), after)

    def mm(self, out, lhsT, rhs, start, stop, after=None, sig=False):
        return self.do(lambda e: e.matmul(out, lhsT, rhs, start=start, stop=stop, skip_group_check=True), after, sig)

    def mms(self, out, pairs, after=None, sig=True, start=True, stop=True):
        n = len(pairs)
        tok = None
        for i, (a, b) in enumerate(pairs):
            tok = self.mm(out, a, b, start and i == 0, stop and i == n - 1, after if i == 0 else None,
                          sig and i == n - 1)
        return tok

    def tr(self, out, in_, ident, after=None, sig=False):
        return self.do(lambda e: e.transpose(out, in_, ident), after, sig)


class Banks:

    def __init__(self, ps):
        self.ps, self.k, self.free = ps, 0, [None] * 8

    def take(self):
        i = self.k % 8
        self.k += 1
        return Bank(self, i, self.ps[:, i, :], self.free[i])


class Bank:
    def __init__(self, banks, i, ap, free):
        self.banks, self.i, self.ap, self.free = banks, i, ap, free

    def done(self, *toks):
        self.banks.free[self.i] = list(toks)


class Loads:

    def __init__(self, sem):
        self.sem, self.n = sem, 0

    def go(self, q, out, in_, after=None):
        q.dma(out, in_, self.sem, after)
        self.n += 16

    @property
    def tok(self):
        return (self.sem, self.n)


class Weights:

    def __init__(self, q, tiles, sems):
        self.q, self.tiles, self.sems = q, tiles, sems
        self.k, self.uses = 0, [0] * len(tiles)
        self.free = [None] * len(tiles)

    def load(self, src, kc, n):
        i = self.k % len(self.tiles)
        self.k += 1
        assert self.uses[i] == 0 or self.free[i] is not None
        ap = self.tiles[i][:, 0:kc * n].rearrange("p (k n) -> p k n", k=kc)
        self.q.dma(ap, src, self.sems[i], self.free[i])
        self.uses[i] += 1
        self.free[i] = None
        return Tile(self, i, ap, (self.sems[i], 16 * self.uses[i]))


class Tile:
    def __init__(self, ring, i, ap, tok):
        self.ring, self.i, self.ap, self.tok = ring, i, ap, tok

    def done(self, *toks):
        self.ring.free[self.i] = list(toks)


def build(nc, T, out, parts="123", flip=False):
    at, _ = const_table()
    vat, n = {}, 0
    for name, r in VECS:
        vat[name] = n
        n += r
    NV = -(-n // 128)
    ctx = ExitStack()
    with ctx:
        def sem(name):
            return ctx.enter_context(nc.semaphore(name))

        nsb = [0]

        def sb(name, shape, dt=F32, c=None):
            nsb[0] += 1
            return (c or ctx).enter_context(nc.sbuf_tensor(f"{name}_{nsb[0]}", shape, dt))

        PE, AC, VE, PO, SP = (
            Queue(sem(f"s_{x}"), x in ("act", "dve", "pool")) for x in ("pe", "act", "dve", "pool", "sp"))
        ps = ctx.enter_context(nc.psum_tensor("ps", [128, 8, 512], F32))
        B = Banks(ps)
        NS = 4
        SLOT = 8 * 520
        ring = Weights(SP, [sb(f"w{i}", [128, SLOT]) for i in range(NS)], [sem(f"s_w{i}") for i in range(NS)])

        CT = sb("CT", [128, max(b for _, b in at.values())])
        SEL = sb("SEL", [8, 1024])
        VT = sb("VT", [128, NV * 128])
        CS = sb("CS", [128, 24])
        EPSC = sb("EPSC", [128, 1])
        X = sb("X", [128, 2, D])
        MOD = sb("MOD", [128, 14, 8])
        GR = sb("GR", [128, 5, D])
        AC2 = sb("AC2", [128, 4, 512])
        ROW = sb("ROW", [1, D])
        GB = sb("GB", [128, D])
        st = sb("st", [128, 64])

        def C(name, a=0, b=None):
            lo, hi = at[name]
            return CT[:, lo + a:(hi if b is None else lo + b)]

        def V(name, j=0, k=1):
            return VT[:, vat[name] + j:vat[name] + j + k]

        ident = C("ident")
        ones = C("ones")

        def barrier():
            toks = [q.last for q in (PE, AC, VE, PO) if q.n]
            for q in (PE, AC, VE, PO):
                q.pend = q.pend + toks

        nsem = [0]

        def loads(name):
            nsem[0] += 1
            return Loads(sem(f"s_l{nsem[0]}_{name}"))

        with ExitStack() as ph:
            VR = sb("VR", [128, NV, 128], c=ph)
            lc = loads("const")
            lc.go(AC, CT[:, :], T["consts"])
            lc.go(AC, SEL[:, :], T["sel"])
            lx = loads("x")
            lx.go(AC, X[:, :, :], T["x"].rearrange("a (t p) d -> p (a t) d", p=128))
            lv = loads("vecs")
            VR0 = VE.mset(VR[:, NV - 1, :], 0.0)
            for name, r in VECS:
                a = T[name]
                names = " ".join(f"a{i}" for i in range(len(a.shape)))
                src = a.rearrange(f"{names} -> ({names})").rearrange("(r q) -> r q", q=128)
                done = 0
                while done < r:
                    g = vat[name] + done
                    k = min(r - done, 128 - g % 128)
                    lv.go(AC, VR[g % 128:g % 128 + k, g // 128, :], src[done:done + k, :],
                          VR0 if g // 128 == NV - 1 else None)
                    done += k
            VE.mset(EPSC[:, :], EPS)
            b0, b1 = B.take(), B.take()
            for i in range(NV):
                b = b0 if i < 4 else b1
                PE.tr(b.ap[:, (i % 4) * 128:(i % 4) * 128 + 128], VR[:, i, :], ident,
                      [lc.tok, lv.tok, VR0], sig=True)
            t0 = VE.cp(VT[:, 0:512], b0.ap, PE.last)
            t1 = VE.cp(VT[:, 512:NV * 128], b1.ap[:, 0:NV * 128 - 512], PE.last)
            b0.done(t0)
            b1.done(t1)
            AC.act(CS[:, :], VT[:, 0:24], ACT.Silu, after=[t0, lx.tok])
        barrier()

        accfree = [None, None]
        nacc = [0]

        def ada_acc(src, c0, ccol):
            i = nacc[0] % 2
            nacc[0] += 1
            w = ring.load(src[:, c0:c0 + 512].rearrange("(k p) n -> p k n", p=128), 8, 512)
            toks = [None, None]
            for k in range(8):
                acc = AC2[:, 2 * i + k % 2, :]
                if k < 2:
                    toks[k] = VE.ts(acc, w.ap[:, k, :], CS[:, ccol + k:ccol + k + 1], MUL,
                                    after=[w.tok, accfree[i]])
                else:
                    toks[k % 2] = VE.stt(acc, w.ap[:, k, :], CS[:, ccol + k:ccol + k + 1], acc, MUL, ADD,
                                         after=[toks[k % 2]])
            w.done(toks[1])
            return i, toks

        class AdaCols:

            def __init__(self, src, c0, ccol, bias, g, slot):
                self.a = (src, c0, ccol, bias, g, slot)
                self.j = 0
                self.tok = None

            def step(self):
                src, c0, ccol, bias, g, slot = self.a
                j = self.j
                if j == 0:
                    self.toks = []
                i, toks = ada_acc(src, c0 + 512 * j, ccol)
                b = B.take()
                for f in range(4):
                    for h in range(2):
                        PE.mm(b.ap[:, f:f + 1], AC2[:, 2 * i + h, f * 128:(f + 1) * 128], ones[:, 0:1],
                              h == 0, h == 1, [toks, b.free], sig=True)
                accfree[i] = PE.last
                o = MOD[:, 2 * slot + j // 2, 4 * (j % 2):4 * (j % 2) + 4]
                bv = VT[:, bias + 4 * j:bias + 4 * j + 4]
                if j < 2:
                    t = VE.tt(o, b.ap[:, 0:4], bv, ADD, PE.last)
                    b.done(t)
                else:
                    t = VE.stt(o, b.ap[:, 0:4], 1.0, bv, ADD, ADD, PE.last)
                    b.done(t)
                    t = VE.tt(o, o, VT[:, g + 4 * (j - 2):g + 4 * (j - 2) + 4], MUL, t)
                self.toks.append(t)
                self.j += 1
                if self.j == 4:
                    self.tok = self.toks
                    return True
                return False

        rowfree = [None]
        gbfree = [None]

        class AdaRow:

            def __init__(self, src, c0, ccol, bias, gpost, slot, after=None):
                self.a = (src, c0, ccol, bias, gpost, slot)
                self.j = 0
                self.after = after

            def step(self):
                src, c0, ccol, bias, gpost, slot = self.a
                if self.j == 0:
                    self.l = loads("row")
                    self.l.go(PO, ROW[0:1, :], bias, rowfree[0])
                    if gpost is not None:
                        self.l.go(PO, GB[:, :], gpost.broadcast_to([128, D]), gbfree[0])
                    self.toks = []
                j = self.j
                i, toks = ada_acc(src, c0 + 512 * j, ccol)
                b = B.take()
                PE.mm(b.ap, ones, AC2[:, 2 * i, :], True, False, [toks, b.free])
                PE.mm(b.ap, ones, AC2[:, 2 * i + 1, :], False, False)
                t = PE.mm(b.ap, ones[0:1, :], ROW[0:1, 512 * j:512 * j + 512], False, True, self.l.tok, sig=True)
                accfree[i] = t
                rowfree[0] = t
                o = GR[:, slot, 512 * j:512 * j + 512]
                if gpost is not None:
                    t = VE.tt(o, b.ap, GB[:, 512 * j:512 * j + 512], MUL, [t, self.l.tok, self.after])
                    gbfree[0] = t
                else:
                    t = VE.cp(o, b.ap, [t, self.after])
                b.done(t)
                self.toks.append(t)
                self.j += 1
                if self.j == 2:
                    self.tok = self.toks
                    return True
                return False

        def rstd(ins, n, width, scratch, dst, after):
            for i in range(n):
                t = AC.act(scratch, ins(i), ACT.Square, acc=st[:, 32 + i:33 + i], after=[after])
            t = AC.act(st[:, 40:40 + n], st[:, 32:32 + n], ACT.Sqrt, bias=EPSC[:, :], scale=1.0 / width, after=t)
            return VE.rec(dst, st[:, 40:40 + n], t)

        def to_features(src, dst, scale, shift, after, ncols=8):
            toks = []
            for k in range(0, ncols, 2):
                b = B.take()
                m = min(2, ncols - k)
                for j in range(m):
                    for t in range(2):
                        tp = PE.tr(b.ap[:, j * 256 + t * 128:j * 256 + t * 128 + 128], src(t, k + j), ident,
                                   [after, b.free], sig=(j == m - 1 and t == 1))
                fr = []
                for j in range(m):
                    o, i_ = dst[:, k + j, :], b.ap[:, j * 256:j * 256 + 256]
                    s_, b_ = scale(k + j), shift(k + j)
                    dve = (k // 2) % 2
                    if s_ is None:
                        fr.append(VE.cp(o, i_, tp) if dve else AC.act(o, i_, ACT.Copy, after=tp))
                    elif b_ is None:
                        fr.append(VE.ts(o, i_, s_, MUL, after=tp) if dve else
                                  AC.act(o, i_, ACT.Copy, scale=s_, after=tp))
                    elif dve:
                        fr.append(VE.ts(o, i_, s_, MUL, b_, ADD, tp))
                    else:
                        fr.append(AC.act(o, i_, ACT.Identity, bias=b_, scale=s_, after=tp))
                b.done(*fr)
                toks += fr
            return toks

        def norm_mod(XN, HT, slot, modtok, after):
            t = rstd(lambda i: X[:, i, :], 2, D, XN[:, 0, :], st[:, 0:2], after)
            a = VE.ts(XN[:, 0, :], X[:, 0, :], st[:, 0:1], MUL, after=t)
            b = VE.ts(XN[:, 1, :], X[:, 1, :], st[:, 1:2], MUL)
            return to_features(lambda t_, k: XN[:, t_, k * 128:(k + 1) * 128], HT,
                               lambda k: MOD[:, 2 * slot + 1, k:k + 1], lambda k: MOD[:, 2 * slot, k:k + 1],
                               [a, b, modtok])

        def wtile(src, c0, n, r0=0, rows=1024):
            return ring.load(src[r0:r0 + rows, c0:c0 + n].rearrange("(k p) n -> p k n", p=128), rows // 128, n)

        def feat(w, c, m, HT, b, col, after):
            kc = w.ap.shape[1]
            return PE.mms(b.ap[0:m, col:col + 256], [(w.ap[:, k, c:c + m], HT[:, k, :]) for k in range(kc)],
                          [w.tok, b.free, after])

        def toks_(w, c, n, HT, t, b, col, after, start=True, stop=True, k0=0):
            kc = w.ap.shape[1]
            return PE.mms(b.ap[:, col:col + n],
                          [(HT[:, k0 + k, t * 128:(t + 1) * 128], w.ap[:, k, c:c + n]) for k in range(kc)],
                          [w.tok, b.free, after], start=start, stop=stop)

        def feats(w, ntile, HT, after, put):
            for j in range(0, ntile, 2):
                b = B.take()
                fr = []
                for i in range(min(2, ntile - j)):
                    tp = feat(w, (j + i) * 128, 128, HT, b, i * 256, after)
                for i in range(min(2, ntile - j)):
                    fr.append(put(j + i, b.ap[:, i * 256:i * 256 + 256], tp))
                b.done(*fr)
            w.done(tp)

        def bytoks(w, c, n, HT, after, put, done=True):
            for t in range(2):
                b = B.take()
                tp = toks_(w, c, n, HT, t, b, 0, after)
                b.done(put(t, b.ap[:, 0:n], tp))
            if done:
                w.done(tp)

        def out_proj(srcs, OT, after, put):
            for half in range(2):
                bs = [B.take(), B.take()]
                n = len(srcs)
                for s, (src, r0, kc) in enumerate(srcs):
                    w = wtile(src, half * 512, 512, r0, kc * 128)
                    for t in range(2):
                        tp = toks_(w, 0, 512, OT, t, bs[t], 0, after, start=s == 0, stop=s == n - 1, k0=r0 // 128)
                        if s == n - 1:
                            bs[t].tok = tp
                    w.done(tp)
                for t in range(2):
                    bs[t].done(put(t, half, bs[t].ap, bs[t].tok))

        def post_norm(Y, slot, after, scratch, modtok):
            t = rstd(lambda i: Y[:, i, :], 2, D, scratch, st[:, 2:4], after)
            for i in range(2):
                a = VE.stt(Y[:, i, :], Y[:, i, :], st[:, 2 + i:3 + i], GR[:, slot, :], MUL, MUL, [t, modtok])
                a = VE.tt(X[:, i, :], X[:, i, :], Y[:, i, :], ADD, a)
            return a

        def softmax_attn(ph, qT, kT, v, mask, O, after):
            SB = sb("att_s", [128, 8, 384], c=ph)
            PT = sb("att_p", [128, 4, 256], c=ph)
            pv = [None] * 4
            mx = sb("att_m", [128, 4, 8], c=ph)
            for t in range(2):
                nk = 128 * (t + 1)
                c0 = 0 if t == 0 else 128
                stok = {}
                for g in range(2):
                    bs = [B.take(), B.take()]
                    for par in range(2):
                        for i in range(2):
                            h = 4 * g + 2 * i + par
                            hp = 64 * par
                            stok[h] = PE.mm(bs[par].ap[:, i * 256:i * 256 + nk],
                                            qT[hp:hp + 64, h // 2, t * 128:t * 128 + 128],
                                            kT[hp:hp + 64, h // 2, 0:nk], True, True, [bs[par].free, after], sig=True)
                    mt = {}
                    sall = PE.last
                    for par in range(2):
                        for i in range(2):
                            h = 4 * g + 2 * i + par
                            mt[h] = VE.ttr(SB[:, h, c0:c0 + nk], bs[par].ap[:, i * 256:i * 256 + nk], mask(t), ADD, MAX,
                                           -3e38, mx[:, 0 + t, h:h + 1], sall)
                        bs[par].done(mt[4 * g + 2 + par])
                nt = VE.ts(mx[:, t, :], mx[:, t, :], -1.0, MUL, after=VE.last)
                bo = B.take()
                for h in range(0, 8, 2):
                    b = B.take()
                    for i in range(2):
                        et = AC.act(SB[:, h + i, c0:c0 + nk], SB[:, h + i, c0:c0 + nk], ACT.Exp,
                                    bias=mx[:, t, h + i:h + i + 1], acc=mx[:, 2 + t, h + i:h + i + 1], after=nt)
                        for k in range(t + 1):
                            tp = PE.tr(b.ap[:, i * 256 + k * 128:i * 256 + k * 128 + 128],
                                       SB[:, h + i, c0 + k * 128:c0 + k * 128 + 128], ident, [et, b.free],
                                       sig=(i == 1 and k == t))
                    ct = VE.cp(PT[:, h % 4:h % 4 + 2, 0:nk],
                               b.ap.rearrange("p (i n) -> p i n", i=2)[:, :, 0:nk], [tp, pv[h % 4]])
                    b.done(ct)
                    for i in range(2):
                        tp = PE.mms(bo.ap[:, (h + i) * 64:(h + i) * 64 + 64],
                                    [(PT[:, (h + i) % 4, k * 128:k * 128 + 128], v[:, k, (h + i) * 64:(h + i) * 64 + 64])
                                     for k in range(t + 1)], [ct, bo.free])
                    pv[h % 4] = tp
                rt = VE.rec(mx[:, 2 + t, :], mx[:, 2 + t, :], et)
                ot = VE.tt(O(t).rearrange("p (h d) -> p h d", h=8), bo.ap.rearrange("p (h d) -> p h d", h=8),
                           mx[:, 2 + t, :].unsqueeze(2).broadcast_to([128, 8, 64]), MUL, [rt, tp])
                bo.done(ot)
            return ot

        def head_norm(b, tp, gate, O, nh, SQ, col):
            r = st[:, col:col + nh]
            a = AC.act(SQ, b.ap, ACT.Square, after=tp)
            a = VE.red(r, SQ.rearrange("p (h d) -> p h d", h=nh), ADD, a)
            a = AC.act(r, r, ACT.Sqrt, bias=EPSC[:, :], scale=1.0 / 128, after=a)
            a = VE.rec(r, r, a)
            a = VE.tt(O.rearrange("p (h d) -> p h d", h=nh), b.ap.rearrange("p (h d) -> p h d", h=nh),
                      r.unsqueeze(2).broadcast_to([128, nh, 128]), MUL, a)
            b.done(a)
            return VE.tt(O, O, gate, MUL, [a])

        pending = []

        def background(n=1):
            for _ in range(n):
                if pending and pending[0].step():
                    pending.pop(0)

        def first():
            wm, wi = T["w_mod"][0], T["w_in"][0]
            bm = vat["b_mod"]
            m1 = AdaCols(wm, 0, 0, bm, vat["g_pre_mix"], 0)
            while not m1.step():
                pass
            with ExitStack() as ph:
                XN = sb("XN", [128, 2, D], c=ph)
                HT = sb("HT", [128, 8, 256], c=ph)
                h = norm_mod(XN, HT, 0, m1.tok, None)
                qT = sb("qT", [128, 4, 256], c=ph)
                kT = sb("kT", [128, 4, 256], c=ph)
                va = sb("va", [128, 2, 512], c=ph)
                R, tm = XN[:, :, 0:512], XN[:, :, 512:768]

                def rope(w, dst, cn, sn):
                    toks = []

                    def put(t, p, tp):
                        x = p.rearrange("p (h a d) -> p h a d", h=8, a=2)
                        o = R[:, t, :].rearrange("p (h a d) -> p h a d", h=8, a=2)
                        cs = C(cn, 32 * t, 32 * t + 32).unsqueeze(1).broadcast_to([128, 8, 32])
                        sn_ = C(sn, 32 * t, 32 * t + 32).unsqueeze(1).broadcast_to([128, 8, 32])
                        u = tm[:, t, :].rearrange("p (h d) -> p h d", h=8)
                        VE.tt(o[:, :, 0, :], x[:, :, 0, :], cs, MUL, tp)
                        a = VE.tt(u, x[:, :, 1, :], sn_, MUL)
                        a = VE.tt(o[:, :, 0, :], o[:, :, 0, :], u, SUB, a)
                        VE.tt(o[:, :, 1, :], x[:, :, 1, :], cs, MUL)
                        a = VE.tt(u, x[:, :, 0, :], sn_, MUL, a)
                        toks.append(VE.tt(o[:, :, 1, :], o[:, :, 1, :], u, ADD, a))
                        return a
                    bytoks(w, 0, 512, HT, h, put)
                    r = to_features(lambda t, k: R[:, t, k * 128:(k + 1) * 128], dst, lambda k: None, lambda k: None,
                                    toks, 4)
                    VE.pend = VE.pend + [PE.last]
                    return r

                tq = rope(wtile(wi, 0, 512), qT, "cosq", "sinq")
                tk = rope(wtile(wi, 512, 512), kT, "cos", "sin")
                bytoks(wtile(wi, 1024, 512), 0, 512, HT, h, lambda t, p, tp: AC.act(va[:, t, :], p, ACT.Copy, after=tp))
                tv = AC.last
                qg = sb("qg", [128, 2, 256], c=ph)
                kg = sb("kg", [128, 2, 256], c=ph)
                vg = sb("vg", [128, 2, 512], c=ph)
                rg = sb("rg", [128, 2, 512], c=ph)
                la = sb("la", [128, 2, 256], c=ph)
                bb = sb("bb", [128, 2, 256], c=ph)
                glr = sb("glr", [16, 256], c=ph)
                wlr = sb("wlr", [16, 256], c=ph)
                lw = loads("wlr")
                lw.go(PO, wlr[:, :], T["w_gate_lr"][0])

                def put_qk(j, p, tp):
                    if j < 2:
                        return AC.act(qg[:, j, :], p, ACT.Copy, scale=0.125, after=tp)
                    return AC.act(kg[:, j - 2, :], p, ACT.Copy, after=tp)
                feats(wtile(wi, 1536, 512), 4, HT, h, put_qk)
                bytoks(wtile(wi, 2048, 512), 0, 512, HT, h, lambda t, p, tp: AC.act(vg[:, t, :], p, ACT.Copy, after=tp))
                bytoks(wtile(wi, 2560, 512), 0, 512, HT, h, lambda t, p, tp: AC.act(rg[:, t, :], p, ACT.Silu, after=tp))
                w = wtile(wi, 3072, 16)
                b = B.take()
                tp = feat(w, 0, 16, HT, b, 0, h)
                w.done(tp)
                a = VE.cp(glr[:, :], b.ap[0:16, 0:256], tp)
                b.done(a)
                b = B.take()
                for j in range(2):
                    tp = PE.mm(b.ap[:, j * 256:j * 256 + 256], wlr[:, j * 128:j * 128 + 128], glr[:, :], True, True,
                               [a, lw.tok, b.free], sig=True)
                fr = [VE.ts(la[:, j, :], b.ap[:, j * 256:j * 256 + 256], V("b_gate", j), ADD, after=tp) for j in range(2)]
                b.done(*fr)
                laf, bbf = la[:, :, :].rearrange("p a t -> p (a t)"), bb[:, :, :].rearrange("p a t -> p (a t)")
                a = AC.act(bbf, laf, ACT.Abs, after=fr)
                a = AC.act(bbf, bbf, ACT.Exp, scale=-1.0, after=a)
                a = AC.act(bbf, bbf, ACT.Ln, bias=1.0, after=a)
                a = VE.stt(laf, laf, 0.0, bbf, MIN, SUB, a)
                for j in range(2):
                    a2 = VE.scan(bb[:, j, :], C("R64"), la[:, j, :], 0.0, MUL, ADD, a)
                qd = sb("qd", [128, 2, 256], c=ph)
                ki = sb("ki", [128, 2, 256], c=ph)
                ke = sb("ke", [128, 2, 256], c=ph)
                al = sb("al", [128, 2, 4], c=ph)
                qdf, kif, kef = (x[:, :, :].rearrange("p a t -> p (a t)") for x in (qd, ki, ke))
                qgf, kgf = (x[:, :, :].rearrange("p a t -> p (a t)") for x in (qg, kg))
                bl = bb[:, :, :].rearrange("p a (n c) -> p (a n) c", c=64)
                x1 = AC.act(qdf, bbf, ACT.Exp, scale=1.0 / 16, after=a2)
                x2 = AC.act(kif, bbf, ACT.Exp, scale=-1.0 / 16, after=a2)
                x3 = VE.tt(ke[:, :, :].rearrange("p a (n c) -> p (a n) c", c=64),
                           bl[:, :, 63:64].broadcast_to([128, 8, 64]), bl, SUB, a2)
                x4 = AC.act(kef, kef, ACT.Exp, scale=1.0 / 16, after=x3)
                x5 = AC.act(al[:, :, :].rearrange("p a n -> p (a n)"), bl[:, :, 63], ACT.Exp, scale=1.0 / 16, after=a2)
                x1 = VE.tt(qdf, qdf, qgf, MUL, [x1, AC.last])
                x2 = VE.tt(kif, kif, kgf, MUL, x2)
                x4 = VE.tt(kef, kef, kgf, MUL, x4)
                O = sb("O", [128, 2, D], c=ph)
                with ExitStack() as pa:
                    to = softmax_attn(pa, qT, kT, va, lambda t: C(f"AB{t}"), lambda t: O[:, t, 0:512], [tq, tk, tv])
                barrier()
                keT = sb("keT", [128, 2, 256], c=ph)
                b = B.take()
                for j in range(2):
                    for t in range(2):
                        tp = PE.tr(b.ap[:, t * 256 + j * 128:t * 256 + j * 128 + 128], ke[:, j, t * 128:t * 128 + 128],
                                   ident, [x4, b.free], sig=True)
                a = AC.act(keT[:, :, :].rearrange("p a t -> p (a t)"), b.ap, ACT.Copy, after=tp)
                b.done(a)
                tke = a
                AT = sb("AT", [128, 8, 128], c=ph)
                z = VE.mset(AT[:, :, :], 0.0)
                att = []
                for t in range(2):
                    bs = [B.take(), B.take()]
                    for par in range(2):
                        for j in range(2):
                            hp = 64 * par
                            tp = PE.mm(bs[par].ap[:, j * 128:j * 128 + 128], ki[hp:hp + 64, j, t * 128:t * 128 + 128],
                                       qd[hp:hp + 64, j, t * 128:t * 128 + 128], True, True, [x1, x2, bs[par].free], sig=True)
                    for par in range(2):
                        for j in range(2):
                            a = VE.cpred(AT[:, t * 4 + 2 * j + par, :], C("U64").bitcast(U32),
                                         bs[par].ap[:, j * 128:j * 128 + 128], [z, tp])
                        bs[par].done(a)
                    att.append(a)
                S = sb("S", [128, 4, 2, 128], c=ph)
                sz = VE.mset(S[:, 0, :, :], 0.0)
                stk = [sz]
                for n in range(3):
                    t, c0 = n // 2, 64 * (n % 2)
                    bs = [B.take(), B.take()]
                    for j in range(2):
                        for par in range(2):
                            tp = PE.mm(bs[par].ap[64 * par:64 * par + 64, j * 128:j * 128 + 128],
                                       keT[c0:c0 + 64, t, j * 128 + 64 * par:j * 128 + 64 * par + 64],
                                       vg[c0:c0 + 64, t, (2 * j + par) * 128:(2 * j + par) * 128 + 128], True, True,
                                       [tke, bs[par].free], sig=True)
                    nw = []
                    for par in range(2):
                        for j in range(2):
                            hs = slice(64 * par, 64 * par + 64)
                            nw.append(VE.stt(S[hs, n + 1, j, :], S[hs, n, j, :], al[hs, j, n:n + 1],
                                             bs[par].ap[hs, j * 128:j * 128 + 128], MUL, ADD, [tp, x5, stk[-1]]))
                        bs[par].done(nw[-1])
                    stk.append(nw)
                SQ = XN[:, 0, 512:1024]
                for t in range(2):
                    bs = [B.take(), B.take()]
                    for par in range(2):
                        for j in range(2):
                            hd = 2 * j + par
                            o = bs[par].ap[:, j * 128:j * 128 + 128]
                            PE.mm(o, AT[:, t * 4 + hd, :], vg[:, t, hd * 128:hd * 128 + 128], True, False,
                                  [att[t], stk, bs[par].free])
                            for cc in range(2):
                                n = 2 * t + cc
                                hp = 64 * par
                                tp = PE.mm(bs[par].ap[64 * cc:64 * cc + 64, j * 128:j * 128 + 128],
                                           qd[hp:hp + 64, j, n * 64:n * 64 + 64], S[hp:hp + 64, n, j, :], False, True,
                                           sig=True)
                    G = XN[:, t, 0:512]
                    for par in range(2):
                        a = VE.cp(G.rearrange("p (j a d) -> p j a d", j=2, a=2)[:, :, par, :],
                                  bs[par].ap[:, 0:256].rearrange("p (j d) -> p j d", j=2), tp)
                        bs[par].done(a)
                    g = Bank(B, 0, G, None)
                    g.done = lambda *x: None
                    tg = head_norm(g, a, rg[:, t, :], O[:, t, 512:1024], 4, SQ, 44 + 4 * t)
                OT = HT
                tf = to_features(lambda t, k: O[:, t, k * 128:(k + 1) * 128], OT,
                                 lambda k: None if k < 4 else V("g_gla"), lambda k: None, [to, tg])
                gr = AdaRow(wm, 2048, 0, T["b_mod"][:, 2048:3072], T["g_post_mix"], 0)
                while not gr.step():
                    pass
                Y = XN
                out_proj([(T["w_out"][0], 0, 8)], OT, tf,
                         lambda t, half, p, tp: AC.act(Y[:, t, half * 512:half * 512 + 512], p, ACT.Copy, after=tp))
                post_norm(Y, 0, AC.last, O[:, 0, :], gr.tok)
            barrier()
            m2 = AdaCols(wm, 3072, 0, bm + 24, vat["g_pre_ffn"], 1)
            while not m2.step():
                pass
            moe(m2)

        def moe(m2):
            wgu, wd = T["w_gate_up"][0], T["w_down"][0]
            ph = ExitStack()
            with ph:
                XN = sb("XN2", [128, 2, D], c=ph)
                HT = sb("HT2", [128, 8, 256], c=ph)
                RW = sb("RW", [128, 8, 32], c=ph)
                RB = sb("RB", [128, 32], c=ph)
                BD = sb("BD", [32, D], c=ph)
                lr = loads("router")
                lr.go(PO, RW[:, :, :], T["router_w"][0].rearrange("(k p) e -> p k e", p=128))
                lr.go(PO, RB[:, :], T["router_b"].broadcast_to([128, 32]))
                lr.go(PO, BD[:, :], T["b_down"][0])
                h = norm_mod(XN, HT, 1, m2.tok, None)
                lg = sb("lg", [128, 2, 32], c=ph)
                G = sb("G", [128, 2, 32], c=ph)
                rk = sb("rk", [128, 2, 32], c=ph)
                sl = sb("sl", [128, 2, 32], c=ph)
                m8 = sb("m8", [128, 2, 8], c=ph)
                w4 = sb("w4", [128, 4, 32], c=ph)
                c4 = sb("c4", [128, 2, 4], c=ph)
                one32 = C("ones", 0, 32)
                for t in range(2):
                    b = B.take()
                    tp = PE.mms(b.ap[:, 0:32], [(HT[:, k, t * 128:t * 128 + 128], RW[:, k, :]) for k in range(8)],
                                [h, lr.tok, b.free])
                    a = VE.tt(lg[:, t, :], b.ap[:, 0:32], RB[:, :], ADD, [tp, lr.tok, VE.last])
                    b.done(a)
                    a = VE.do(lambda e, t=t: e.max(m8[:, t, :], lg[:, t, :]), a)
                    gt, eq, cs, x = (w4[:, i, :] for i in range(4))
                    a1 = VE.ts(gt, lg[:, t, :], m8[:, t, 3:4], ALU.is_gt, after=a)
                    a2 = VE.ts(eq, lg[:, t, :], m8[:, t, 3:4], ALU.is_equal)
                    VE.red(c4[:, t, 0:1], gt, ADD, a1)
                    a3 = VE.scan(cs, one32, eq, 0.0, MUL, ADD, a2)
                    a3 = VE.ts(x, cs, c4[:, t, 0:1], ADD, 4.5, ALU.is_lt, a3)
                    a3 = VE.tt(x, x, eq, MUL, a3)
                    a3 = VE.tt(sl[:, t, :], x, gt, ADD, a3)
                    n1 = VE.ts(c4[:, t, 1:2], m8[:, t, 0:1], -1.0, MUL)
                    e1 = AC.act(x, lg[:, t, :], ACT.Exp, bias=c4[:, t, 1:2], after=[a3, n1])
                    a3 = VE.ttr(G[:, t, :], x, sl[:, t, :], MUL, ADD, 0.0, c4[:, t, 2:3], e1)
                    a3 = VE.rec(c4[:, t, 3:4], c4[:, t, 2:3], a3)
                    a3 = VE.ts(G[:, t, :], G[:, t, :], c4[:, t, 3:4], MUL, after=a3)
                tG = a3
                cnt = sb("cnt", [128, 32], c=ph)
                flag = sb("flag", [128, 2], I32, c=ph)
                mxc = sb("mxc", [128, 2], c=ph)
                b = B.take()
                PE.mm(b.ap[:, 0:32], C("SU"), sl[:, 0, :], True, True, [tG, b.free])
                PE.mms(b.ap[:, 32:64], [(ones, sl[:, 0, :]), (C("SU"), sl[:, 1, :])])
                tp = PE.mms(b.ap[:, 64:96], [(ones, sl[:, 0, :]), (ones, sl[:, 1, :])])
                for t in range(2):
                    a = VE.stt(rk[:, t, :], b.ap[:, 32 * t:32 * t + 32], 1.0, sl[:, t, :], ADD, MUL, tp)
                    a = VE.ts(rk[:, t, :], rk[:, t, :], -1.0, ADD, after=a)
                trk = a
                a = VE.red(mxc[:, 0:1], b.ap[:, 64:96], MAX)
                b.done(a)
                a = VE.ts(mxc[:, 1:2], mxc[:, 0:1], -1.0 if flip else float(CAP) + 0.5, ALU.is_gt, after=a)
                tflag = VE.cp(flag[:, 0:1], mxc[:, 1:2], a)
                ACCM = sb("ACCM", [128, 2, D], c=ph)
                GT = sb("GT", [32, 256], c=ph)
                b = B.take()
                for t in range(2):
                    tp = PE.tr(b.ap[0:32, t * 128:t * 128 + 128], G[:, t, :], ident, [tG, b.free], sig=True)
                a = VE.cp(GT[:, :], b.ap[0:32, 0:256], tp)
                b.done(a)
                ta = None
                for t in range(2):
                    for hf in range(2):
                        b = B.take()
                        tp = PE.mm(b.ap, GT[:, t * 128:t * 128 + 128], BD[:, hf * 512:hf * 512 + 512], True, True,
                                   [a, b.free, lr.tok], sig=True)
                        ta = VE.cp(ACCM[:, t, hf * 512:hf * 512 + 512], b.ap, tp)
                        b.done(ta)
                PG = sb("PG", [128, 2, 2, 128], c=ph)
                PGT = sb("PGT", [128, 256], c=ph)
                XE = sb("XE", [128, 8, 128], c=ph)
                BR = sb("BR", [1, 2, 2048], c=ph)
                BB = sb("BB", [128, 2048], c=ph)
                T1 = sb("T1", [128, 512], c=ph)
                T2 = sb("T2", [128, 256], c=ph)
                A_ = HT[:, 0:4, :].rearrange("p k t -> p (k t)")
                Y = HT[:, 4:8, :].rearrange("p k t -> p (k t)")
                AT = sb("AT2", [128, 8, 128], c=ph)
                iota = C("iota")
                hold = {"br": [None, None], "bb": None, "xe": None, "pg": None, "pgt": None, "at": None, "y": None,
                        "acc": [ta]}
                lbr = [Loads(sem("s_br0")), Loads(sem("s_br1"))]

                def expert(e, blk):
                    i = e % 2
                    lbr[i].go(AC, BR[0:1, i, :], T["b_gate_up"][0:1, e, :], hold["br"][i])
                    bt = PO.do(lambda g, i=i: g.partition_broadcast(BB[:, :], BR[0:1, i, :], 128),
                               [lbr[i].tok, hold["bb"]])
                    hold["br"][i] = bt
                    for t in range(2):
                        s1 = rk[:, t, e:e + 1]
                        src = iota
                        VE.ts(PG[:, 0, t, :], src, float(blk * CAP), ADD, s1, ALU.is_equal, [trk, hold["pg"]])
                    pg = VE.last
                    for t in range(2):
                        pg2 = VE.ts(PG[:, 1, t, :], PG[:, 0, t, :], G[:, t, e:e + 1], MUL, after=pg)
                    xt = []
                    for k in range(0, 8, 4):
                        b = B.take()
                        for j in range(4):
                            f = (k + j) * 128
                            tp = PE.mms(b.ap[:, j * 128:j * 128 + 128],
                                        [(XN[:, t, f:f + 128], PG[:, 0, t, :]) for t in range(2)], [pg, b.free],
                                        sig=j == 3)
                        fr = []
                        for j in range(4):
                            fr.append(AC.act(XE[:, k + j, :], b.ap[:, j * 128:j * 128 + 128], ACT.Identity,
                                             bias=MOD[:, 2, k + j:k + j + 1], scale=MOD[:, 3, k + j:k + j + 1],
                                             after=[tp, hold["xe"]]))
                        b.done(fr[-1])
                        xt += fr
                    b = B.take()
                    for t in range(2):
                        tp = PE.tr(b.ap[:, t * 128:t * 128 + 128], PG[:, 1, t, :], ident, [pg2, b.free], sig=True)
                    hold["pg"] = tp
                    tpg = AC.act(PGT[:, :], b.ap[:, 0:256], ACT.Copy, after=[tp, hold["pgt"]])
                    b.done(tpg)
                    at_ = []
                    for q in range(4):
                        w = wtile(wgu[e], q * 512, 512)
                        b = B.take()
                        tp = PE.mms(b.ap, [(XE[:, k, :], w.ap[:, k, :]) for k in range(8)], [w.tok, b.free, xt])
                        w.done(tp)
                        x = VE.tt(T1[:, :], b.ap, BB[:, q * 512:q * 512 + 512], ADD, [tp, bt, VE.last])
                        b.done(x)
                        v = T1[:, :].rearrange("p (n a) -> p n a", a=2)
                        x1 = VE.ts(v[:, :, 0], v[:, :, 0], 7.0, MIN, after=[x])
                        x2 = AC.act(T2[:, :], v[:, :, 0], ACT.Sigmoid, scale=1.702, after=[x1, VE.last])
                        x3 = VE.ts(v[:, :, 1], v[:, :, 1], 7.0, MIN, -7.0, MAX)
                        x3 = VE.stt(v[:, :, 1], v[:, :, 1], 1.0, v[:, :, 0], ADD, MUL, x3)
                        x3 = VE.tt(A_[:, q * 256:q * 256 + 256], v[:, :, 1], T2[:, :], MUL, [x2, x3, hold["at"]])
                        at_.append(x3)
                    hold["bb"] = x3
                    hold["xe"] = tp
                    for k in range(0, 8, 4):
                        b = B.take()
                        for j in range(4):
                            tp = PE.tr(b.ap[:, j * 128:j * 128 + 128], A_[:, (k + j) * 128:(k + j) * 128 + 128], ident,
                                       [at_, b.free], sig=j == 3)
                        x = AC.act(AT[:, k:k + 4, :].rearrange("p k n -> p (k n)"), b.ap, ACT.Copy,
                                   after=[tp, hold["y"]])
                        b.done(x)
                    hold["at"] = tp
                    for hf in range(2):
                        w = wtile(wd[e], hf * 512, 512)
                        b = B.take()
                        tp = PE.mms(b.ap, [(AT[:, k, :], w.ap[:, k, :]) for k in range(8)], [w.tok, b.free, x])
                        w.done(tp)
                        yt = AC.act(Y[:, hf * 512:hf * 512 + 512], b.ap, ACT.Copy, after=[tp, hold["pgt"]])
                        b.done(yt)
                    hold["y"] = tp
                    na = []
                    for t in range(2):
                        for hf in range(2):
                            b = B.take()
                            tp = PE.mm(b.ap, PGT[:, t * 128:t * 128 + 128], Y[:, hf * 512:hf * 512 + 512], True, True,
                                       [yt, tpg, b.free], sig=True)
                            a = VE.tt(ACCM[:, t, hf * 512:hf * 512 + 512], ACCM[:, t, hf * 512:hf * 512 + 512], b.ap,
                                      ADD, [tp, hold["acc"]])
                            b.done(a)
                            na.append(a)
                    hold["pgt"] = tp
                    hold["acc"] = na

                for e in range(E_N):
                    expert(e, 1 if flip else 0)
                    background(1)
                barrier()
                queues = (PE, AC, VE, PO, SP)
                toks = [q.last for q in (PE, AC, VE, PO)]
                keep = [(q.sem, q.n) for q in queues]
                ring_keep = (list(ring.uses), [x for x in ring.sems], ring.k)
                for q, nm in zip(queues, ("pe", "act", "dve", "pool", "sp")):
                    q.raw(lambda e, seen, outer, q=q: enter(e, seen))

                def enter(e, seen):
                    kept = dict(seen)
                    for s_, v_ in [tflag] + toks:
                        if seen.get(s_.name, 0) < v_:
                            e.wait_ge(s_, v_)
                            kept[s_.name] = v_
                    seen.update(kept)
                    reg = e.value_load(flag[0:1, 0:1], min_val=0, max_val=1)
                    g = e.If(reg == 1)
                    g.__enter__()
                    return (g, kept)

                for q, nm in zip(queues, ("pe", "act", "dve", "pool", "sp")):
                    q.sem, q.n = sem(f"s_{nm}_more"), 0
                    q.pend = []
                ring.sems = [sem(f"s_wm{i}") for i in range(NS)]
                ring.uses = [0] * NS
                ring.free = [toks[0]] * NS
                oldlbr = lbr[:]
                lbr[0], lbr[1] = Loads(sem("s_brm0")), Loads(sem("s_brm1"))
                B.free = [None] * 8
                hold.update({"br": [None, None], "bb": None, "xe": None, "pg": None, "pgt": None, "at": None, "y": None,
                             "acc": None})
                for e in range(E_N):
                    expert(e, 0 if flip else 1)
                ends = [q.last for q in (PE, AC, VE, PO)]

                def leave(e, seen, outer):
                    for s_, v_ in ends:
                        if seen.get(s_.name, 0) < v_:
                            e.wait_ge(s_, v_)
                    g, kept = outer
                    g.__exit__(None, None, None)
                    seen.clear()
                    seen.update(kept)
                    return None

                for q, k in zip(queues, keep):
                    q.raw(leave)
                    q.sem, q.n = k
                ring.uses, ring.sems, ring.k = ring_keep
                ring.free = [toks[0]] * NS
                B.free = [None] * 8
                post_norm(ACCM, 1, toks, XN[:, 0, :], rows[1].tok)
            barrier()

        def bc(ap, n):
            return ap.unsqueeze(1).broadcast_to([128, n, ap.shape[1]])

        def ex(ap, n):
            return ap.unsqueeze(2).broadcast_to([128, ap.shape[1], n])

        def heads(ap, n):
            return ap.rearrange("p (h d) -> p h d", h=n)

        def second():
            wi = T["w_in_2"][0]
            with ExitStack() as ph:
                XN = sb("XN3", [128, 2, D], c=ph)
                HT = sb("HT3", [128, 8, 256], c=ph)
                O = sb("O3", [128, 2, D], c=ph)
                h = norm_mod(XN, HT, 2, mods[2].tok, None)
                zd = sb("zd", [128, 2, 512], c=ph)
                CO = sb("CO", [128, 12, 256], c=ph)
                BG = sb("BG", [128, 2, 8], c=ph)
                AD = sb("AD", [128, 8], c=ph)
                zm = sb("zm", [128, 2, 512], c=ph)
                ld = loads("decay")
                ld.go(PO, AD[:, 0:4], T["a_log_2"].broadcast_to([128, 4]))
                ld.go(PO, AD[:, 4:8], T["dt_bias_2"].broadcast_to([128, 4]))
                pm = ExitStack()
                qm = sb("qm", [128, 4, 256], c=pm)
                km = sb("km", [128, 4, 256], c=pm)
                vm = sb("vm", [128, 2, 512], c=pm)
                cb = ExitStack()
                CI = sb("CI", [128, 2, 4, 260], c=cb)
                ct = [None, None]
                z = VE.mset(CI[:, :, :, 0:3], 0.0)
                for g in range(3):
                    i = g % 2
                    cw = []

                    def put(j, p, tp, i=i):
                        return AC.act(CI[:, i, j, 3:259], p, ACT.Copy, after=[tp, ct[i], z])
                    feats(wtile(wi, 512 * g, 512), 4, HT, h, put)
                    a = AC.last
                    for j in range(4):
                        f = 4 * g + j
                        VE.ts(CO[:, f, :], CI[:, i, j, 0:256], V("conv_w_2", f), MUL, after=a)
                        for k in range(1, 4):
                            ct[i] = VE.stt(CO[:, f, :], CI[:, i, j, k:k + 256], V("conv_w_2", 12 * k + f),
                                           CO[:, f, :], MUL, ADD)
                    cof = CO[:, 4 * g:4 * g + 4, :].rearrange("p j t -> p (j t)")
                    tco = AC.act(cof, cof, ACT.Silu, after=ct[i])
                w = wtile(wi, 1536, 520)
                bytoks(w, 0, 512, HT, h, lambda t, p, tp: AC.act(zd[:, t, :], p, ACT.Silu, after=tp), done=False)
                b = B.take()
                for t in range(2):
                    tp = toks_(w, 512, 8, HT, t, b, 8 * t, h)
                w.done(tp)
                bg = BG[:, :, :]
                a = VE.cp(bg, b.ap[:, 0:16].rearrange("p (t c) -> p t c", t=2), tp)
                b.done(a)
                sp = st[:, 0:8].rearrange("p (t c) -> p t c", t=2)
                a1 = AC.act(BG[:, :, 0:4], BG[:, :, 0:4], ACT.Sigmoid, after=a)
                a2 = VE.tt(BG[:, :, 4:8], BG[:, :, 4:8], AD[:, 4:8].unsqueeze(1).broadcast_to([128, 2, 4]), ADD, ld.tok)
                a2 = AC.act(sp, BG[:, :, 4:8], ACT.Abs, after=a2)
                a2 = AC.act(sp, sp, ACT.Exp, scale=-1.0)
                a2 = AC.act(sp, sp, ACT.Ln, bias=1.0)
                a3 = AC.act(AD[:, 0:4], AD[:, 0:4], ACT.Exp, after=ld.tok)
                a2 = VE.stt(BG[:, :, 4:8], BG[:, :, 4:8], 0.0, sp, MAX, ADD, [a2, a3])
                a2 = VE.stt(BG[:, :, 4:8], BG[:, :, 4:8], -1.0, AD[:, 0:4].unsqueeze(1).broadcast_to([128, 2, 4]), MUL, MUL)
                tbg = [a1, a2]
                feats(wtile(wi, 2056, 512), 4, HT, h, lambda j, p, tp: AC.act(qm[:, j, :], p, ACT.Copy, scale=0.125, after=tp))
                feats(wtile(wi, 2568, 512), 4, HT, h, lambda j, p, tp: AC.act(km[:, j, :], p, ACT.Copy, after=tp))
                bytoks(wtile(wi, 3080, 512), 0, 512, HT, h, lambda t, p, tp: AC.act(vm[:, t, :], p, ACT.Copy, after=tp))
                bytoks(wtile(wi, 3592, 512), 0, 512, HT, h, lambda t, p, tp: AC.act(zm[:, t, :], p, ACT.Silu, after=tp))
                cb.close()
                barrier()
                with ExitStack() as pa:
                    to = softmax_attn(pa, qm, km, vm, lambda t: C(f"CB{t}"), lambda t: O[:, t, 512:1024], [AC.last])
                for t in range(2):
                    VE.tt(O[:, t, 512:1024], O[:, t, 512:1024], zm[:, t, :], MUL)
                pm.close()
                barrier()
                pd = ExitStack()
                SQ = XN[:, 1, :]
                for g in range(2):
                    cof = CO[:, 4 * g:4 * g + 4, :].rearrange("p j t -> p (j t)")
                    a = AC.act(SQ[:, :], cof, ACT.Square)
                    bs = [B.take(), B.take()]
                    for i in range(2):
                        tp = PE.mm(bs[i].ap, ones, SQ[:, 512 * i:512 * i + 512], True, True, [a, bs[i].free], sig=True)
                    for i in range(2):
                        a = AC.act(SQ[:, 512 * i:512 * i + 512], bs[i].ap, ACT.Ln, bias=EPSC[:, :], after=tp)
                        bs[i].done(a)
                    a = AC.act(SQ[:, :], SQ[:, :], ACT.Exp, scale=-0.5)
                    tn = VE.stt(cof, cof, float(128 ** -0.5) if g == 0 else 1.0, SQ[:, :], MUL, MUL, a)
                    AC.pend = AC.pend + [tn]
                qT, kT, vT = CO[:, 0:4, :], CO[:, 4:8, :], CO[:, 8:12, :]
                GC = sb("GC", [128, 2, 4, 4], c=pd)
                per = {}
                b = B.take()
                for t in range(2):
                    PE.mm(b.ap[:, 8 * t:8 * t + 4], C("U64"), BG[:, t, 4:8], True, True, [tbg, b.free])
                    tp = PE.mm(b.ap[:, 8 * t + 4:8 * t + 8], C("B64"), BG[:, t, 4:8], True, True, sig=True)
                for t in range(2):
                    a = VE.cp(GC[:, t, 0, :], b.ap[:, 8 * t:8 * t + 4], tp)
                    a2 = VE.tt(GC[:, t, 2, :], b.ap[:, 8 * t + 4:8 * t + 8], GC[:, t, 0, :], SUB, a)
                    a = AC.act(GC[:, t, 1, :], GC[:, t, 0, :], ACT.Exp, after=a2)
                    a = AC.act(GC[:, t, 2, :], GC[:, t, 2, :], ACT.Exp)
                    a = VE.stt(GC[:, t, 1, :], GC[:, t, 1, :], -1.0, BG[:, t, 0:4], MUL, MUL, a)
                b.done(a)
                W5, W6 = XN[:, 0, 0:512], XN[:, 0, 512:1024]
                for t in range(2):
                    p = per[t] = {n: sb(f"d{n}{t}", [128, 512], c=pd)
                                  for n in ("eR", "aT", "qk", "U", "T", "Y", "kg", "vb")}
                    p["vn"], p["wT"], p["qg"], p["kb"] = p["Y"], p["T"], p["aT"], O[:, t, 0:512]
                    tok = slice(t * 128, t * 128 + 128)
                    a = VE.tt(heads(W5, 4), bc(C("U64"), 4), ex(BG[:, t, 4:8], 128), MUL, PE.last)
                    a = VE.tt(heads(W6, 4), bc(ident, 4), ex(BG[:, t, 0:4], 128), MUL)
                    b, b2 = B.take(), B.take()
                    PE.mm(b.ap, ones, W5, True, True, [a, b.free])
                    tp = PE.mm(b2.ap, ones, W6, True, True, [b2.free], sig=True)
                    a = AC.act(p["eR"][:, :], b.ap, ACT.Exp, after=tp)
                    a = VE.tt(heads(W5, 4), heads(b.ap, 4), ex(GC[:, t, 0, :], 128), SUB, [a, tp])
                    b.done(a)
                    a = VE.ts(W5, W5, 0.0, MIN)
                    a = AC.act(W5, W5, ACT.Exp, after=a)
                    a = VE.tt(heads(W6, 4), heads(W5, 4), bc(C("SU64"), 4), MUL, [a, tp])
                    a = VE.tt(W6, W6, b2.ap, MUL)
                    b2.done(a)
                    a = VE.tt(heads(W5, 4), heads(W5, 4), bc(C("U64"), 4), MUL)
                    b, b2 = B.take(), B.take()
                    for hd in range(4):
                        hc = slice(hd * 128, hd * 128 + 128)
                        PE.mm(b.ap[:, hc], kT[:, hd, tok], kT[:, hd, tok], True, True, [tn, b.free])
                    for hd in range(4):
                        hc = slice(hd * 128, hd * 128 + 128)
                        tp = PE.mm(b2.ap[:, hc], kT[:, hd, tok], qT[:, hd, tok], True, True, [b2.free], sig=True)
                    a = VE.tt(p["aT"][:, :], b.ap, W6, MUL, tp)
                    b.done(a)
                    a = VE.tt(p["qk"][:, :], b2.ap, W5, MUL)
                    b2.done(a)
                    a = VE.tt(heads(W5, 4), heads(p["aT"][:, :], 4), bc(C("H1"), 4), MUL)
                    a = VE.tt(heads(p["U"][:, :], 4), bc(ident, 4), heads(W5, 4), SUB)
                    b = B.take()
                    for hd in range(4):
                        hc = slice(hd * 128, hd * 128 + 128)
                        tp = PE.tr(b.ap[:, hc], p["U"][:, hc], ident, [a, b.free], sig=hd == 3)
                    p["tU"] = p["tT"] = AC.act(p["T"][:, :], b.ap, ACT.Copy, after=tp)
                    b.done(p["tT"])
                    b, b2 = B.take(), B.take()
                    for hd in range(4):
                        hc = slice(hd * 128, hd * 128 + 128)
                        PE.tr(b.ap[:, hc], kT[:, hd, tok], ident, [tn, b.free])
                    for hd in range(4):
                        hc = slice(hd * 128, hd * 128 + 128)
                        tp = PE.tr(b2.ap[:, hc], vT[:, hd, tok], ident, [tco, b2.free], sig=hd == 3)
                    VE.tt(heads(p["kb"], 4), heads(b.ap, 4), ex(GC[:, t, 1, :], 128), MUL, tp)
                    a = VE.tt(heads(p["kg"][:, :], 4), heads(b.ap, 4), ex(GC[:, t, 2, :], 128), MUL)
                    b.done(a)
                    a = VE.tt(heads(p["vb"][:, :], 4), heads(b2.ap, 4), ex(BG[:, t, 0:4], 128), MUL)
                    b2.done(a)
                    p["tk"] = a
                for L in (2, 4, 8, 16, 32):
                    for t in range(2):
                        p = per[t]
                        Wt = (W5, W6)[t]
                        a = VE.tt(heads(Wt, 4), heads(p["aT"][:, :], 4), bc(C(f"H{L}"), 4), MUL, [PE.last])
                        b = B.take()
                        for hd in range(4):
                            hc = slice(hd * 128, hd * 128 + 128)
                            tp = PE.mm(b.ap[:, hc], Wt[:, hc], p["T"][:, hc], True, True, [a, p["tT"], b.free], sig=hd == 3)
                        ty = AC.act(p["Y"][:, :], b.ap, ACT.Copy, after=tp)
                        b.done(ty)
                        b = B.take()
                        for hd in range(4):
                            hc = slice(hd * 128, hd * 128 + 128)
                            tp = PE.mm(b.ap[:, hc], p["Y"][:, hc], p["U"][:, hc], True, True, [ty, p["tU"], b.free],
                                       sig=hd == 3)
                        if L < 32:
                            b2 = B.take()
                            for hd in range(4):
                                hc = slice(hd * 128, hd * 128 + 128)
                                tp = PE.mm(b2.ap[:, hc], p["U"][:, hc], p["Y"][:, hc], True, True, [b2.free], sig=hd == 3)
                            p["tT"] = VE.tt(p["T"][:, :], p["T"][:, :], b2.ap, SUB, tp)
                            b2.done(p["tT"])
                        p["tU"] = VE.tt(p["U"][:, :], p["U"][:, :], b.ap, SUB, tp)
                        b.done(p["tU"])
                for t in range(2):
                    p = per[t]
                    b = B.take()
                    for hd in range(4):
                        hc = slice(hd * 128, hd * 128 + 128)
                        tp = PE.mm(b.ap[:, hc], p["kb"][:, hc], p["U"][:, hc], True, True, [p["tU"], p["tk"], b.free],
                                   sig=hd == 3)
                    a = AC.act(p["wT"][:, :], b.ap, ACT.Copy, after=tp)
                    b.done(a)
                    tok = slice(t * 128, t * 128 + 128)
                    p["tw"] = [a, VE.tt(heads(p["qg"][:, :], 4), qT[:, :, tok], heads(p["eR"][:, :], 4), MUL)]
                S = zm[:, 0, :]
                ts_ = VE.mset(S, 0.0)
                for n in range(4):
                    t, c0 = n // 2, 64 * (n % 2)
                    p = per[t]
                    rw = slice(c0, c0 + 64)
                    b = B.take()
                    for hd in range(4):
                        hc = slice(hd * 128, hd * 128 + 128)
                        cc = slice(hd * 128 + c0, hd * 128 + c0 + 64)
                        PE.mm(b.ap[rw, hc], p["U"][:, cc], p["vb"][:, hc], True, False, [p["tw"], ts_, b.free])
                        tp = PE.mm(b.ap[rw, hc], p["wT"][:, cc], S[:, hc], False, True, sig=hd == 3)
                    tv = AC.act(p["vn"][rw, :], b.ap[rw, :], ACT.Copy, after=tp)
                    b.done(tv)
                    if n % 2 == 0:
                        bo = B.take()
                    for hd in range(4):
                        hc = slice(hd * 128, hd * 128 + 128)
                        cc = slice(hd * 128 + c0, hd * 128 + c0 + 64)
                        PE.mm(bo.ap[rw, hc], p["qg"][:, cc], S[:, hc], True, False, [bo.free, ts_, tv])
                        tp = PE.mm(bo.ap[rw, hc], p["qk"][rw, cc], p["vn"][rw, hc], False, True, sig=hd == 3)
                    if n < 3:
                        b = B.take()
                        for hd in range(4):
                            hc = slice(hd * 128, hd * 128 + 128)
                            tp = PE.mm(b.ap[:, hc], p["kg"][rw, hc], p["vn"][rw, hc], True, True, b.free, sig=hd == 3)
                        for hd in range(4):
                            hc = slice(hd * 128, hd * 128 + 128)
                            ts_ = VE.stt(S[:, hc], S[:, hc], p["eR"][:, hd * 128 + c0 + 63:hd * 128 + c0 + 64],
                                         b.ap[:, hc], MUL, ADD, tp)
                        b.done(ts_)
                    if n % 2 == 1:
                        tg = head_norm(bo, tp, zd[:, t, :], O[:, t, 0:512], 4, SQ[:, 0:512], 44 + 4 * t)
                pd.close()
                barrier()
                OT = sb("OT3", [128, 8, 256], c=ph)
                tf = to_features(lambda t, k: O[:, t, k * 128:(k + 1) * 128], OT,
                                 lambda k: V("dn_norm_g_2") if k < 4 else None, lambda k: None, [tg, to])
                SG = sb("SG", [128, 2, 4, 256], c=ph)
                MX = sb("MX", [128, 8, 256], c=ph)
                sgf = [None, None]
                for half in range(2):
                    for br in range(2):
                        def put(j, p, tp, br=br):
                            return AC.act(SG[:, br, j, :], p, ACT.Sigmoid, after=[tp, sgf[br]])
                        feats(wtile(wi, 4104 + 1024 * br + 512 * half, 512), 4, HT, h, put)
                    tsg = AC.last

                    def put0(j, p, tp):
                        return VE.tt(MX[:, 4 * half + j, :], p, SG[:, 0, j, :], MUL, [tp, tsg])

                    def put1(j, p, tp):
                        return VE.tt(SG[:, 1, j, :], p, SG[:, 1, j, :], MUL, [tp, tsg])
                    feats(wtile(T["w_proj_dn_2"][0], 512 * half, 512, 0, 512), 4, OT[:, 0:4, :], tf, put0)
                    feats(wtile(T["w_proj_mb_2"][0], 512 * half, 512, 0, 512), 4, OT[:, 4:8, :], tf, put1)
                    tm = VE.tt(MX[:, 4 * half:4 * half + 4, :], MX[:, 4 * half:4 * half + 4, :], SG[:, 1, :, :], ADD)
                    sgf = [tm, tm]
                Y = XN
                out_proj([(T["w_out_2"][0], 0, 8)], MX, tm,
                         lambda t, half, p, tp: AC.act(Y[:, t, half * 512:half * 512 + 512], p, ACT.Copy, after=tp))
                post_norm(Y, 2, AC.last, O[:, 0, :], rows[2].tok)
            barrier()

        def add_gated(slot, tmp, tok):
            def put(t, half, p, tp):
                hs = slice(half * 512, half * 512 + 512)
                a = VE.tt(tmp[:, t, hs], p, GR[:, slot, hs], MUL, [tp, tok])
                VE.tt(X[:, t, hs], X[:, t, hs], tmp[:, t, hs], ADD, a)
                return a
            return put

        def ffn(layer, slot, grslot, modtok, growtok):
            w_in, w_out = T["ffn_w_in_3"][layer], T["ffn_w_out_3"][layer]
            with ExitStack() as ph:
                XN = sb(f"XF{layer}", [128, 2, D], c=ph)
                HT = sb(f"HF{layer}", [128, 8, 256], c=ph)
                A = sb(f"AF{layer}", [128, FT, 256], c=ph)
                CI = sb(f"CF{layer}", [128, 2, 4, 258], c=ph)
                z = VE.mset(CI[:, :, :, 0:2], 0.0)
                h = norm_mod(XN, HT, slot, modtok, None)
                hold = [None, None]
                for g in range(6):
                    n = 4 if g < 5 else 2
                    i = g % 2

                    def put(j, p, tp, i=i):
                        return AC.act(CI[:, i, j, 2:258], p, ACT.Copy, after=[tp, hold[i], z])
                    feats(wtile(w_in, 512 * g, 128 * n), n, HT, h, put)
                    a = AC.last
                    for j in range(n):
                        f = 4 * g + j
                        cw = 66 * layer + f
                        VE.ts(A[:, f, :], CI[:, i, j, 0:256], V("ffn_conv_w_3", cw), MUL,
                              V("ffn_conv_b_3", 22 * layer + f), ADD, a)
                        VE.stt(A[:, f, :], CI[:, i, j, 1:257], V("ffn_conv_w_3", cw + 22), A[:, f, :], MUL, ADD)
                        hold[i] = VE.stt(A[:, f, :], CI[:, i, j, 2:258], V("ffn_conv_w_3", cw + 44), A[:, f, :], MUL, ADD)
                    af = A[:, 4 * g:4 * g + n, :].rearrange("p j t -> p (j t)")
                    AC.act(af, af, ACT.Gelu_apprx_tanh, after=hold[i])
                    background(1)
                ta = AC.last
                for g in range(6):
                    n = 4 if g < 5 else 2

                    def put(j, p, tp, g=g):
                        return VE.tt(A[:, 4 * g + j, :], A[:, 4 * g + j, :], p, MUL, [tp, ta])
                    feats(wtile(w_in, FFN + 512 * g, 128 * n), n, HT, h, put)
                out_proj([(w_out, 0, 8), (w_out, 1024, 8), (w_out, 2048, 6)], A, VE.last, add_gated(grslot, XN, growtok))
            barrier()

        def even(modtok, growtok):
            wi = T["even_w_in_3"][0]
            with ExitStack() as ph:
                XN = sb("XE3", [128, 2, D], c=ph)
                HT = sb("HE3", [128, 8, 256], c=ph)
                h = norm_mod(XN, HT, 3, modtok, None)
                names = ("qa", "ka", "lf", "bcu", "qb", "kb")
                qa, ka, lf, bcu, qb, kb = (sb("e" + n, [128, 4, 256], c=ph) for n in names)
                ia, ga, vb = (sb("e" + n, [128, 2, 512], c=ph) for n in ("ia", "ga", "vb"))
                fl = lambda x: x[:, :, :].rearrange("p j t -> p (j t)")
                feats(wtile(wi, 0, 512), 4, HT, h, lambda j, p, tp: AC.act(qa[:, j, :], p, ACT.Copy, after=tp))
                feats(wtile(wi, 512, 512), 4, HT, h, lambda j, p, tp: AC.act(lf[:, j, :], p, ACT.Copy, after=tp))
                bytoks(wtile(wi, 1024, 512), 0, 512, HT, h, lambda t, p, tp: AC.act(ia[:, t, :], p, ACT.Copy, after=tp))
                bytoks(wtile(wi, 1536, 512), 0, 512, HT, h, lambda t, p, tp: AC.act(ga[:, t, :], p, ACT.Silu, after=tp))
                feats(wtile(wi, 2048, 512), 4, HT, h,
                      lambda j, p, tp: AC.act(qb[:, j, :], p, ACT.Copy, scale=float(128 ** -0.5), after=tp))
                feats(wtile(wi, 2560, 512), 4, HT, h, lambda j, p, tp: AC.act(kb[:, j, :], p, ACT.Copy, after=tp))
                bytoks(wtile(wi, 3072, 512), 0, 512, HT, h, lambda t, p, tp: AC.act(vb[:, t, :], p, ACT.Copy, after=tp))
                AC.act(fl(ka), fl(lf), ACT.Sigmoid, scale=-1.0)
                AC.act(fl(bcu), fl(lf), ACT.Abs)
                AC.act(fl(bcu), fl(bcu), ACT.Exp, scale=-1.0)
                a = AC.act(fl(bcu), fl(bcu), ACT.Ln, bias=1.0)
                VE.stt(fl(lf), fl(lf), 0.0, fl(bcu), MIN, SUB, a)
                for j in range(4):
                    tb = VE.scan(bcu[:, j, :], C("R128"), lf[:, j, :], 0.0, MUL, ADD)
                Et, QL, KL = lf, XN[:, 0, :], XN[:, 1, :]
                SC = sb("SC", [128, 2, 512], c=ph)
                z = VE.mset(SC[:, :, :], 0.0)
                free = None
                for L in (0, 1, 2, 4, 8, 16, 32, 64):
                    if L:
                        v = fl(bcu).rearrange("p (n l) -> p n l", l=2 * L)
                        ev = fl(Et).rearrange("p (n l) -> p n l", l=2 * L)
                        n = 1024 // (2 * L)
                        bm = v[:, :, L - 1:L].broadcast_to([128, n, L])
                        VE.tt(ev[:, :, 0:L], bm, v[:, :, 0:L], SUB, [AC.last, PO.last if PO.n else None])
                        a = VE.tt(ev[:, :, L:2 * L], v[:, :, L:2 * L], bm, SUB)
                        a = AC.act(fl(Et), fl(Et), ACT.Exp, after=a)
                        t1 = VE.tt(QL, fl(qa), fl(Et), MUL, [a, free])
                        t2 = PO.tt(KL, fl(ka), fl(Et), MUL, [a, free])
                        ql, kl, m = heads(QL, 4), heads(KL, 4), C(f"H{L}")
                    else:
                        t1 = t2 = AC.last
                        ql, kl, m = qa[:, :, :], ka[:, :, :], ident
                    for t in range(2):
                        b = B.take()
                        tok = slice(t * 128, t * 128 + 128)
                        for hd in range(4):
                            tp = PE.mm(b.ap[:, hd * 128:hd * 128 + 128], kl[:, hd, tok], ql[:, hd, tok], True, True,
                                       [t1, t2, b.free], sig=hd == 3)
                        a = VE.cpred(heads(SC[:, t, :], 4), bc(m.bitcast(U32), 4), heads(b.ap, 4), tp)
                        b.done(a)
                    free = tp
                tsc = a
                K1, Q1, KT, S0 = (sb("e" + n, [128, 512], c=ph) for n in ("K1", "Q1", "KT", "S0"))
                a = VE.tt(heads(K1[:, :], 4), bcu[:, :, 127:128].broadcast_to([128, 4, 128]), bcu[:, :, 0:128], SUB)
                AC.act(K1[:, :], K1[:, :], ACT.Exp, after=a)
                a = AC.act(heads(Q1[:, :], 4), bcu[:, :, 128:256], ACT.Exp)
                VE.tt(heads(K1[:, :], 4), heads(K1[:, :], 4), ka[:, :, 0:128], MUL, a)
                a = VE.tt(heads(Q1[:, :], 4), heads(Q1[:, :], 4), qa[:, :, 128:256], MUL)
                b = B.take()
                for hd in range(4):
                    hc = slice(hd * 128, hd * 128 + 128)
                    tp = PE.tr(b.ap[:, hc], K1[:, hc], ident, [a, b.free], sig=hd == 3)
                a = AC.act(KT[:, :], b.ap, ACT.Copy, after=tp)
                b.done(a)
                b = B.take()
                for hd in range(4):
                    hc = slice(hd * 128, hd * 128 + 128)
                    tp = PE.mm(b.ap[:, hc], KT[:, hc], ia[:, 0, hc], True, True, [a, b.free], sig=hd == 3)
                ts0 = AC.act(S0[:, :], b.ap, ACT.Copy, after=tp)
                b.done(ts0)
                O = sb("OE", [128, 2, 512], c=ph)
                for t in range(2):
                    b = B.take()
                    for hd in range(4):
                        hc = slice(hd * 128, hd * 128 + 128)
                        tp = PE.mm(b.ap[:, hc], SC[:, t, hc], ia[:, t, hc], True, t == 0, [tsc, ts0, b.free], sig=True)
                        if t == 1:
                            tp = PE.mm(b.ap[:, hc], Q1[:, hc], S0[:, hc], False, True, sig=True)
                    tg = head_norm(b, tp, ga[:, t, :], O[:, t, :], 4, XN[:, 0, 0:512], 44 + 4 * t)
                ZS = sb("ZS", [128, 4, 384], c=ph)
                LK = XN[:, :, :].rearrange("p a d -> p (a d)")[:, 0:1536].rearrange("p (h t) -> p h t", h=4)
                for hd in range(4):
                    b = B.take()
                    PE.mm(b.ap[:, 0:256], kb[:, hd, 0:128], qb[:, hd, :], True, True, [tg, b.free])
                    tp = PE.mm(b.ap[:, 256:384], kb[:, hd, 128:256], qb[:, hd, 128:256], True, True, sig=True)
                    a = AC.act(ZS[:, hd, :], b.ap[:, 0:384], ACT.Copy, after=tp)
                    b.done(a)
                AC.act(fl(LK), fl(ZS), ACT.Abs)
                AC.act(fl(LK), fl(LK), ACT.Exp, scale=-1.0)
                a = AC.act(fl(LK), fl(LK), ACT.Ln, bias=1.0)
                a = VE.stt(fl(LK), fl(ZS), 0.0, fl(LK), MAX, ADD, a)
                a = VE.ts(fl(LK), fl(LK), -1.0, MUL)
                for c0 in (0, 256):
                    tl = VE.tt(LK[:, :, c0:c0 + 128], LK[:, :, c0:c0 + 128], bc(C("SU"), 4), MUL)
                for hd in range(4):
                    b = B.take()
                    PE.mm(b.ap[:, 0:256], C("LF"), LK[:, hd, 0:256], True, False, [tl, b.free])
                    PE.mm(b.ap[:, 128:256], ones, LK[:, hd, 256:384], False, True)
                    tp = PE.mm(b.ap[:, 256:384], C("LF"), LK[:, hd, 256:384], True, True, sig=True)
                    a = VE.tt(ZS[:, hd, :], ZS[:, hd, :], b.ap[:, 0:384], ADD, tp)
                    b.done(a)
                for c0 in (0, 256):
                    a = VE.tt(ZS[:, :, c0:c0 + 128], ZS[:, :, c0:c0 + 128], bc(C("NM"), 4), ADD)
                tz = AC.act(fl(ZS), fl(ZS), ACT.Exp, after=a)
                OT = HT
                for hd in range(4):
                    hc = slice(hd * 128, hd * 128 + 128)
                    b = B.take()
                    PE.mm(b.ap[:, 0:256], vb[:, 0, hc], ZS[:, hd, 0:256], True, False, [tz, b.free])
                    tp = PE.mm(b.ap[:, 128:256], vb[:, 1, hc], ZS[:, hd, 256:384], False, True, sig=True)
                    to = AC.act(OT[:, 4 + hd, :], b.ap[:, 0:256], ACT.Copy, after=tp)
                    b.done(to)
                tf = to_features(lambda t, k: O[:, t, k * 128:(k + 1) * 128], OT,
                                 lambda k: V("hgrn_norm_g_3", k), lambda k: None, tg, 4)
                out_proj([(T["even_w_out_3"][0], 0, 8)], OT, [tf, to], add_gated(3, XN, growtok))
            barrier()

        def odd(modtok, growtok):
            wi = T["odd_w_in_3"][0]
            with ExitStack() as ph:
                XN = sb("XO3", [128, 2, D], c=ph)
                HT = sb("HO3", [128, 8, 256], c=ph)
                h = norm_mod(XN, HT, 5, modtok, None)
                CO = sb("COo", [128, 8, 256], c=ph)
                CI = sb("CIo", [128, 4, 260], c=ph)
                VX = sb("VX", [128, 2, 8, 129], c=ph)
                OG = sb("OG", [128, 2, D], c=ph)
                E8 = sb("E8", [8, 6, 256], c=ph)
                GBI = sb("GBI", [8, 2], c=ph)
                CCM = sb("CCM", [128, 2, 16], c=ph)
                lg = loads("gateb")
                gsrc = T["odd_gate_b_3"].rearrange("a (g p) -> (a g) p", p=8)
                for g in range(2):
                    lg.go(PO, GBI[:, g:g + 1], gsrc[g, :].rearrange("(p o) -> p o", o=1))
                z = VE.mset(CI[:, :, 0:3], 0.0)
                z = VE.mset(VX[:, :, :, 128:129], 1.0)
                z = VE.mset(E8[:, 5, :], 1.0)
                w = wtile(wi, 3072, 16)
                b = B.take()
                for g in range(2):
                    tp = PE.mms(b.ap[0:8, 256 * g:256 * g + 256],
                                [(w.ap[:, k, 8 * g:8 * g + 8], HT[:, k, :]) for k in range(8)], [w.tok, b.free, h])
                w.done(tp)
                ig, lf, bs_, cm, nm, one = (E8[:, i, :] for i in range(6))
                VE.ts(ig, b.ap[0:8, 0:256], GBI[:, 0:1], ADD, after=[tp, lg.tok])
                a = VE.ts(lf, b.ap[0:8, 256:512], GBI[:, 1:2], ADD)
                b.done(a)
                a = AC.act(bs_, lf, ACT.Abs, after=a)
                a = AC.act(bs_, bs_, ACT.Exp, scale=-1.0)
                a = AC.act(bs_, bs_, ACT.Ln, bias=1.0)
                VE.stt(lf, lf, 0.0, bs_, MIN, SUB, a)
                VE.scan(bs_, one, lf, 0.0, MUL, ADD)
                VE.tt(ig, ig, bs_, SUB)
                VE.scan(cm, one, ig, 0.0, MUL, MAX)
                a = VE.stt(nm, bs_, -1.0, cm, MUL, SUB)
                b = B.take()
                for t in range(2):
                    tk = slice(t * 128, t * 128 + 128)
                    PE.tr(b.ap[:, 16 * t:16 * t + 8], ig[:, tk], ident[0:8, 0:8], [a, b.free])
                    tp = PE.tr(b.ap[:, 16 * t + 8:16 * t + 16], nm[:, tk], ident[0:8, 0:8], sig=True)
                a = VE.cp(CCM[:, :, :], b.ap[:, 0:32].rearrange("p (t c) -> p t c", t=2), tp)
                b.done(a)
                tcm = AC.act(CCM[:, :, 8:16], CCM[:, :, 8:16], ACT.Exp, after=a)
                ct = None
                for g in range(2):
                    feats(wtile(wi, 512 * g, 512), 4, HT, h,
                          lambda j, p, tp: AC.act(CI[:, j, 3:259], p, ACT.Copy, after=[tp, ct, z]))
                    a = AC.last
                    for j in range(4):
                        f = 4 * g + j
                        VE.ts(CO[:, f, :], CI[:, j, 0:256], V("odd_conv_w_3", f), MUL, V("odd_conv_b_3", f), ADD, a)
                        for k in range(1, 4):
                            ct = VE.stt(CO[:, f, :], CI[:, j, k:k + 256], V("odd_conv_w_3", 8 * k + f), CO[:, f, :], MUL, ADD)
                    cof = CO[:, 4 * g:4 * g + 4, :].rearrange("p j t -> p (j t)")
                    tco = AC.act(cof, cof, ACT.Silu, after=ct)
                for hf in range(2):
                    bytoks(wtile(wi, 1024 + 512 * hf, 512), 0, 512, HT, h,
                           lambda t, p, tp: AC.act(VX[:, t, 4 * hf:4 * hf + 4, 0:128], heads(p, 4), ACT.Copy, after=[tp, z]))
                tv = AC.last
                for hf in range(2):
                    bytoks(wtile(wi, 2048 + 512 * hf, 512), 0, 512, HT, h,
                           lambda t, p, tp: AC.act(OG[:, t, 512 * hf:512 * hf + 512], p, ACT.Sigmoid, after=tp))
                O = sb("OO", [128, 2, D], c=ph)
                W = sb("WO", [128, 4, 384], c=ph)
                dn = sb("dn", [128, 8], c=ph)
                fw = None
                for g in range(2):
                    for i in range(4):
                        hd = 4 * g + i
                        b = B.take()
                        tp = PE.mm(b.ap[:, 0:256], SEL[0:8, hd * 128:hd * 128 + 128], cm, True, True, [tcm, b.free], sig=True)
                        VE.ts(W[:, i, 0:256], b.ap[:, 0:256], CCM[:, 0, hd:hd + 1], SUB, 0.0, MAX, [tp, fw])
                        a = VE.ts(W[:, i, 256:384], b.ap[:, 128:256], CCM[:, 1, hd:hd + 1], SUB, 0.0, MAX)
                        b.done(a)
                    wf = W[:, :, :].rearrange("p i t -> p (i t)")
                    a = AC.act(wf, wf, ACT.Exp, scale=-1.0, after=a)
                    for c0 in (0, 256):
                        te = VE.tt(W[:, :, c0:c0 + 128], W[:, :, c0:c0 + 128], bc(C("UF"), 4), MUL, a)
                    for i in (0, 2, 1, 3):
                        hd = 4 * g + i
                        hp = slice(64 * (hd % 2), 64 * (hd % 2) + 64)
                        b = B.take()
                        PE.mm(b.ap[:, 0:256], CO[hp, 4 + hd // 2, 0:128], CO[hp, hd // 2, :], True, True, [tco, b.free])
                        tp = PE.mm(b.ap[:, 256:384], CO[hp, 4 + hd // 2, 128:256], CO[hp, hd // 2, 128:256], True, True, sig=True)
                        tw = VE.stt(W[:, i, :], b.ap[:, 0:384], 0.125, W[:, i, :], MUL, MUL, [tp, te])
                        b.done(tw)
                    for t in range(2):
                        for i in range(0, 4, 2):
                            b = B.take()
                            for j in range(2):
                                hd = 4 * g + i + j
                                o = b.ap[:, 129 * j:129 * j + 129]
                                prs = [(W[:, i + j, t * 128:t * 128 + 128], VX[:, 0, hd, :])]
                                if t:
                                    prs.append((W[:, i + j, 256:384], VX[:, 1, hd, :]))
                                tp = PE.mms(o, prs, [tw, tv, b.free])
                            h0 = 4 * g + i
                            bv = b.ap[:, 0:258].rearrange("p (j c) -> p j c", j=2)
                            a = AC.act(dn[:, 0:2], bv[:, :, 128], ACT.Abs, after=[tp, VE.last])
                            VE.tt(dn[:, 0:2], dn[:, 0:2], CCM[:, t, 8 + h0:8 + h0 + 2], MAX, a)
                            VE.rec(dn[:, 0:2], dn[:, 0:2])
                            a = VE.tt(heads(O[:, t, h0 * 128:h0 * 128 + 256], 2), bv[:, :, 0:128], ex(dn[:, 0:2], 128), MUL)
                            b.done(a)
                    fw = tp
                for t in range(2):
                    v = Bank(B, 0, O[:, t, :], None)
                    v.done = lambda *x: None
                    tg = head_norm(v, VE.last, OG[:, t, :], O[:, t, :], 8, XN[:, 0, :], 44 + 8 * t)
                OT = HT
                tf = to_features(lambda t, k: O[:, t, k * 128:(k + 1) * 128], OT,
                                 lambda k: V("odd_norm_g_3", k), lambda k: None, [tg, PE.last])
                out_proj([(T["odd_w_out_3"][0], 0, 8)], OT, tf, add_gated(0, XN, growtok))
            barrier()

        def third():
            even(mods[3].tok, rows[3].tok)
            ffn(0, 4, 4, mods[4].tok, rows[4].tok)
            odd(mods[5].tok, rows[5].tok)
            background(4)
            ffn(1, 6, 1, mods[6].tok, rows[6].tok)
            lf = loads("final")
            lf.go(PO, GB[:, :], T["final_g_3"].rearrange("(a d) -> a d", a=1).broadcast_to([128, D]))
            with ExitStack() as ph:
                SQ = sb("SQF", [128, D], c=ph)
                t = rstd(lambda i: X[:, i, :], 2, D, SQ[:, :], st[:, 0:2], None)
                for i in range(2):
                    VE.stt(X[:, i, :], X[:, i, :], st[:, i:i + 1], GB[:, :], MUL, MUL, [t, lf.tok])
            barrier()

        a2, b2_, a3, b3 = T["w_ada_2"][0], T["b_ada_2"], T["ada_w_3"], T["ada_b_3"]
        v2, v3 = vat["b_ada_2"], vat["ada_b_3"]
        mods = {2: AdaCols(a2, 0, 8, v2, vat["g_pre_2"], 2)}
        rows = {1: AdaRow(T["w_mod"][0], 5120, 0, T["b_mod"][:, 5120:6144], T["g_post_ffn"], 1),
                2: AdaRow(a2, 2048, 8, b2_[:, 2048:3072], T["g_post_2"], 2)}
        for l in range(2):
            nm, nf = vat["norm_mix_g_3"] + 8 * l, vat["norm_ffn_g_3"] + 8 * l
            mods[3 + 2 * l] = AdaCols(a3[l], 0, 16, v3 + 48 * l, nm, 3 + 2 * l)
            mods[4 + 2 * l] = AdaCols(a3[l], 3072, 16, v3 + 48 * l + 24, nf, 4 + 2 * l)
            rows[3 + 2 * l] = AdaRow(a3[l], 2048, 16, b3[l:l + 1, 2048:3072], None, 3 if l == 0 else 0)
            rows[4 + 2 * l] = AdaRow(a3[l], 5120, 16, b3[l:l + 1, 5120:6144], None, 4 if l == 0 else 1)
        if "1" in parts:
            pending.append(rows[1])
        if "2" in parts:
            pending += [mods[2], rows[2]]
        if "3" in parts:
            pending += [mods[3], rows[3], mods[4], rows[4], mods[5], rows[5], mods[6], rows[6]]
        hold_last = [pending.pop()] if "3" in parts else []
        for p in parts:
            if p == "1":
                first()
            if p == "2":
                background(40)
                pending += hold_last
                hold_last = []
                second()
            if p == "3":
                background(40)
                pending += hold_last
                hold_last = []
                third()

        lo = loads("out")
        lo.go(AC, out.rearrange("a (t p) d -> p (a t) d", p=128), X[:, :, :], [VE.last])
        AC.raw(lambda e, seen, outer: e.wait_ge(lo.sem, lo.n))

        with nc.Block() as block:
            @block.tensor
            def _(eng):
                PE.emit(eng)

            @block.scalar
            def _(eng):
                AC.emit(eng)

            @block.vector
            def _(eng):
                VE.emit(eng)

            @block.gpsimd
            def _(eng):
                PO.emit(eng)

            @block.sync
            def _(eng):
                SP.emit(eng)


def make(nc, shapes, parts="123", flip=False):
    T = {}
    for name, shape in shapes.items():
        T[name] = nc.dram_tensor(f"in_{name}", shape, F32, kind="ExternalInput").ap()
    out = nc.dram_tensor("out_0", (1, 256, 1024), F32, kind="ExternalOutput").ap()
    build(nc, T, out, parts, flip)


def kernel(**inputs):
    import concourse.bacc as bacc
    from concourse.bass_utils import run_bass_kernel_spmd as run
    arrays = {}
    for name, a in inputs.items():
        arrays[name] = np.ascontiguousarray(a)
    arrays["consts"] = const_table()[1]
    arrays["sel"] = sel_table()
    nc = bacc.Bacc("TRN2", target_bir_lowering=False, num_devices=1)
    make(nc, {n: a.shape for n, a in arrays.items()})
    r = run(nc, [{f"in_{n}": a for n, a in arrays.items()}], core_ids=[0])
    return r.results[0]["out_0"]
```

```python
from contextlib import ExitStack

import numpy as np

import concourse.bass as bass
from concourse import mybir

ALU = mybir.AluOpType
ACT = mybir.ActivationFunctionType
F32 = mybir.dt.float32
U32 = mybir.dt.uint32
I32 = mybir.dt.int32
AX = mybir.AxisListType
ADD, SUB, MUL, MAX, MIN = ALU.add, ALU.subtract, ALU.mult, ALU.max, ALU.min

D = 1024
EPS = 1e-6
NEG = -1e30
E_N = 32
FFN = 2816
FT = FFN // 128



def const_table():
    p = np.arange(128)[:, None]
    f = np.arange(128)[None, :]
    same = (p // 64) == (f // 64)
    c = {}
    c["ident"] = p == f
    c["ones"] = np.ones((128, 128))
    c["U64"] = (p <= f) & same
    c["SU64"] = (p < f) & same
    c["UF"] = p <= f
    c["LF"] = p >= f
    c["SU"] = p < f
    c["B64"] = same
    c["NM"] = np.where(p < f, 0.0, NEG)
    for L in (1, 2, 4, 8, 16, 32, 64):
        c[f"H{L}"] = (p // (2 * L) == f // (2 * L)) & (p % (2 * L) < L) & (f % (2 * L) >= L)
    k = np.arange(256)[None, :]
    for t in (0, 1):
        d = (t * 128 + p) - k
        n = (d <= 128) * 1 + (d % 4 == 0) * 1 + (d % 16 == 0) * 1
        dil = np.where((d >= 0) & (n > 0), np.log(np.maximum(n, 1)), NEG)
        cau = np.where(d >= 0, 0.0, NEG)
        c[f"AB{t}"] = dil[:, :128 * (t + 1)]
        c[f"CB{t}"] = cau[:, :128 * (t + 1)]
    half = 32
    inv = (np.float32(10000.0) ** (-np.arange(half, dtype=np.float32) / np.float32(half))).astype(np.float32)
    ang = (np.arange(256, dtype=np.float32)[:, None] * inv[None, :]).astype(np.float32)
    for n, v in (("cos", np.cos(ang)), ("sin", np.sin(ang))):
        v = v.reshape(2, 128, half).transpose(1, 0, 2).reshape(128, 64)
        c[n] = v
        c[n + "q"] = v * 0.125
    c["iota"] = np.broadcast_to(np.arange(128)[None, :], (128, 128))
    t = np.arange(256)[None, :]
    c["R64"] = np.broadcast_to((t % 64 != 0), (128, 256))
    c["R128"] = np.broadcast_to((t % 128 != 0), (128, 256))
    at, cols, n = {}, [], 0
    for name, v in c.items():
        v = np.ascontiguousarray(v, dtype=np.float32)
        at[name] = (n, n + v.shape[1])
        n += v.shape[1]
        cols.append(v)
    return at, np.concatenate(cols, axis=1)


def sel_table():
    s = np.zeros((8, 8, 128), np.float32)
    for h in range(8):
        s[h, h, :] = 1.0
    return s.reshape(8, 1024)


VECS = [("c", 8), ("c_2", 8), ("c_3", 8), ("g_pre_mix", 8), ("g_pre_ffn", 8), ("g_pre_2", 8),
        ("norm_mix_g_3", 16), ("norm_ffn_g_3", 16), ("b_mod", 48), ("b_ada_2", 24), ("ada_b_3", 96),
        ("b_gate", 2), ("g_gla", 1), ("dn_norm_g_2", 1), ("hgrn_norm_g_3", 4), ("odd_norm_g_3", 8),
        ("conv_w_2", 48), ("odd_conv_w_3", 32), ("odd_conv_b_3", 8), ("ffn_conv_w_3", 132), ("ffn_conv_b_3", 44)]




def flat(x, out):
    if x is None:
        return out
    if isinstance(x, tuple):
        out.append(x)
    else:
        for y in x:
            flat(y, out)
    return out


class Queue:

    def __init__(self, sem, chain):
        self.sem, self.n, self.ops, self.pend, self.chain = sem, 0, [], [], chain

    @property
    def last(self):
        return (self.sem, self.n)

    def do(self, fn, after=None, sig=True):
        waits = flat(after, list(self.pend))
        if self.chain and self.n:
            waits.append(self.last)
        self.pend = []
        if sig:
            self.n += 1
        self.ops.append((waits, fn, (self.sem, 1) if sig else None))
        return self.last if sig else None

    def dma(self, out, in_, sem, after=None):
        waits = flat(after, list(self.pend))
        self.pend = []
        self.ops.append((waits, lambda e: e.dma_start(out, in_), (sem, 16)))

    def raw(self, fn):
        self.ops.append((None, fn, None))

    def emit(self, eng):
        seen = {}
        outer = None
        for waits, fn, inc in self.ops:
            if waits is None:
                outer = fn(eng, seen, outer)
                continue
            for sem, val in waits:
                if seen.get(sem.name, 0) < val:
                    eng.wait_ge(sem, val)
                    seen[sem.name] = val
            ins = fn(eng)
            if inc:
                ins.then_inc(inc[0], inc[1])

    def tt(self, out, a, b, op, after=None):
        return self.do(lambda e: e.tensor_tensor(out, a, b, op), after)

    def ts(self, out, a, s1, op0, s2=None, op1=None, after=None):
        if op1 is None:
            return self.do(lambda e: e.tensor_scalar(out, a, s1, None, op0), after)
        return self.do(lambda e: e.tensor_scalar(out, a, s1, s2, op0, op1), after)

    def stt(self, out, a, s, b, op0, op1, after=None):
        return self.do(lambda e: e.scalar_tensor_tensor(out=out, in0=a, scalar=s, in1=b, op0=op0, op1=op1), after)

    def ttr(self, out, a, b, op0, op1, init, acc, after=None):
        return self.do(lambda e: e.tensor_tensor_reduce(out, a, b, 1.0, init, op0, op1, acc), after)

    def cp(self, out, a, after=None):
        return self.do(lambda e: e.tensor_copy(out, a), after)

    def red(self, out, a, op, after=None):
        return self.do(lambda e: e.tensor_reduce(out, a, AX.X, op), after)

    def rec(self, out, a, after=None):
        return self.do(lambda e: e.reciprocal(out, a), after)

    def scan(self, out, a, b, init, op0, op1, after=None):
        return self.do(lambda e: e.tensor_tensor_scan(out, a, b, init, op0, op1), after)

    def cpred(self, out, mask, data, after=None):
        return self.do(lambda e: e.copy_predicated(out, mask, data), after)

    def mset(self, out, v, after=None):
        return self.do(lambda e: e.memset(out, v), after)

    def act(self, out, a, func, bias=None, scale=None, acc=None, after=None):
        kw = {}
        if bias is not None:
            kw["bias"] = bias
        if scale is not None:
            kw["scale"] = scale
        if acc is not None:
            kw["accum_out"] = acc
        return self.do(lambda e: e.activation(out, a, func, **kw), after)

    def mm(self, out, lhsT, rhs, start, stop, after=None, sig=False):
        return self.do(lambda e: e.matmul(out, lhsT, rhs, start=start, stop=stop, skip_group_check=True), after, sig)

    def mms(self, out, pairs, after=None, sig=True, start=True, stop=True):
        n = len(pairs)
        tok = None
        for i, (a, b) in enumerate(pairs):
            tok = self.mm(out, a, b, start and i == 0, stop and i == n - 1, after if i == 0 else None,
                          sig and i == n - 1)
        return tok

    def tr(self, out, in_, ident, after=None, sig=False):
        return self.do(lambda e: e.transpose(out, in_, ident), after, sig)


class Banks:

    def __init__(self, ps):
        self.ps, self.k, self.free = ps, 0, [None] * 8

    def take(self):
        i = self.k % 8
        self.k += 1
        return Bank(self, i, self.ps[:, i, :], self.free[i])


class Bank:
    def __init__(self, banks, i, ap, free):
        self.banks, self.i, self.ap, self.free = banks, i, ap, free

    def done(self, *toks):
        self.banks.free[self.i] = list(toks)


class Loads:

    def __init__(self, sem):
        self.sem, self.n = sem, 0

    def go(self, q, out, in_, after=None):
        q.dma(out, in_, self.sem, after)
        self.n += 16

    @property
    def tok(self):
        return (self.sem, self.n)


class Weights:

    def __init__(self, q, tiles, sems):
        self.q, self.tiles, self.sems = q, tiles, sems
        self.k, self.uses = 0, [0] * len(tiles)
        self.free = [None] * len(tiles)

    def load(self, src, kc, n):
        i = self.k % len(self.tiles)
        self.k += 1
        assert self.uses[i] == 0 or self.free[i] is not None
        ap = self.tiles[i][:, 0:kc * n].rearrange("p (k n) -> p k n", k=kc)
        self.q.dma(ap, src, self.sems[i], self.free[i])
        self.uses[i] += 1
        self.free[i] = None
        return Tile(self, i, ap, (self.sems[i], 16 * self.uses[i]))


class Tile:
    def __init__(self, ring, i, ap, tok):
        self.ring, self.i, self.ap, self.tok = ring, i, ap, tok

    def done(self, *toks):
        self.ring.free[self.i] = list(toks)


def build(nc, T, out, parts="123", flip=False):
    at, _ = const_table()
    vat, n = {}, 0
    for name, r in VECS:
        vat[name] = n
        n += r
    NV = -(-n // 128)
    ctx = ExitStack()
    with ctx:
        def sem(name):
            return ctx.enter_context(nc.semaphore(name))

        nsb = [0]

        def sb(name, shape, dt=F32, c=None):
            nsb[0] += 1
            return (c or ctx).enter_context(nc.sbuf_tensor(f"{name}_{nsb[0]}", shape, dt))

        PE, AC, VE, PO, SP = (
            Queue(sem(f"s_{x}"), x in ("act", "dve", "pool")) for x in ("pe", "act", "dve", "pool", "sp"))
        ps = ctx.enter_context(nc.psum_tensor("ps", [128, 8, 512], F32))
        B = Banks(ps)
        NS = 4
        SLOT = 8 * 520
        ring = Weights(SP, [sb(f"w{i}", [128, SLOT]) for i in range(NS)], [sem(f"s_w{i}") for i in range(NS)])

        CT = sb("CT", [128, max(b for _, b in at.values())])
        SEL = sb("SEL", [8, 1024])
        VT = sb("VT", [128, NV * 128])
        CS = sb("CS", [128, 24])
        EPSC = sb("EPSC", [128, 1])
        X = sb("X", [128, 2, D])
        MOD = sb("MOD", [128, 14, 8])
        GR = sb("GR", [128, 5, D])
        AC2 = sb("AC2", [128, 4, 512])
        ROW = sb("ROW", [1, D])
        GB = sb("GB", [128, D])
        st = sb("st", [128, 64])

        def C(name, a=0, b=None):
            lo, hi = at[name]
            return CT[:, lo + a:(hi if b is None else lo + b)]

        def V(name, j=0, k=1):
            return VT[:, vat[name] + j:vat[name] + j + k]

        ident = C("ident")
        ones = C("ones")

        def barrier():
            toks = [q.last for q in (PE, AC, VE, PO) if q.n]
            for q in (PE, AC, VE, PO):
                q.pend = q.pend + toks

        nsem = [0]

        def loads(name):
            nsem[0] += 1
            return Loads(sem(f"s_l{nsem[0]}_{name}"))

        with ExitStack() as ph:
            VR = sb("VR", [128, NV, 128], c=ph)
            lc = loads("const")
            lc.go(AC, CT[:, :], T["consts"])
            lc.go(AC, SEL[:, :], T["sel"])
            lx = loads("x")
            lx.go(AC, X[:, :, :], T["x"].rearrange("a (t p) d -> p (a t) d", p=128))
            lv = loads("vecs")
            VR0 = VE.mset(VR[:, NV - 1, :], 0.0)
            for name, r in VECS:
                a = T[name]
                names = " ".join(f"a{i}" for i in range(len(a.shape)))
                src = a.rearrange(f"{names} -> ({names})").rearrange("(r q) -> r q", q=128)
                done = 0
                while done < r:
                    g = vat[name] + done
                    k = min(r - done, 128 - g % 128)
                    lv.go(AC, VR[g % 128:g % 128 + k, g // 128, :], src[done:done + k, :],
                          VR0 if g // 128 == NV - 1 else None)
                    done += k
            VE.mset(EPSC[:, :], EPS)
            b0, b1 = B.take(), B.take()
            for i in range(NV):
                b = b0 if i < 4 else b1
                PE.tr(b.ap[:, (i % 4) * 128:(i % 4) * 128 + 128], VR[:, i, :], ident,
                      [lc.tok, lv.tok, VR0], sig=True)
            t0 = VE.cp(VT[:, 0:512], b0.ap, PE.last)
            t1 = VE.cp(VT[:, 512:NV * 128], b1.ap[:, 0:NV * 128 - 512], PE.last)
            b0.done(t0)
            b1.done(t1)
            AC.act(CS[:, :], VT[:, 0:24], ACT.Silu, after=[t0, lx.tok])
        barrier()

        accfree = [None, None]
        nacc = [0]

        def ada_acc(src, c0, ccol):
            i = nacc[0] % 2
            nacc[0] += 1
            w = ring.load(src[:, c0:c0 + 512].rearrange("(k p) n -> p k n", p=128), 8, 512)
            toks = [None, None]
            for k in range(8):
                acc = AC2[:, 2 * i + k % 2, :]
                if k < 2:
                    toks[k] = VE.ts(acc, w.ap[:, k, :], CS[:, ccol + k:ccol + k + 1], MUL,
                                    after=[w.tok, accfree[i]])
                else:
                    toks[k % 2] = VE.stt(acc, w.ap[:, k, :], CS[:, ccol + k:ccol + k + 1], acc, MUL, ADD,
                                         after=[toks[k % 2]])
            w.done(toks[1])
            return i, VE.tt(AC2[:, 2 * i, :], AC2[:, 2 * i, :], AC2[:, 2 * i + 1, :], ADD, toks)

        class AdaCols:
            n = 4

            def __init__(self, src, c0, ccol, bias, g, slot):
                self.a = (src, c0, ccol, bias, g, slot)
                self.tok = []

            def start(self, j):
                return ada_acc(self.a[0], self.a[1] + 512 * j, self.a[2])

            def finish(self, j, i, toks):
                src, c0, ccol, bias, g, slot = self.a
                b = B.take()
                for f in range(4):
                    tp = PE.mm(b.ap[:, f:f + 1], AC2[:, 2 * i, f * 128:(f + 1) * 128], ones[:, 0:1], True, True,
                               [toks, b.free], sig=f == 3)
                accfree[i] = tp
                o = MOD[:, 2 * slot + j // 2, 4 * (j % 2):4 * (j % 2) + 4]
                bv = VT[:, bias + 4 * j:bias + 4 * j + 4]
                if j < 2:
                    t = VE.tt(o, b.ap[:, 0:4], bv, ADD, tp)
                    b.done(t)
                else:
                    t = VE.stt(o, b.ap[:, 0:4], 1.0, bv, ADD, ADD, tp)
                    b.done(t)
                    t = VE.tt(o, o, VT[:, g + 4 * (j - 2):g + 4 * (j - 2) + 4], MUL, t)
                self.tok.append(t)

        rowfree = [None]
        gbfree = [None]

        class AdaRow:
            n = 2

            def __init__(self, src, c0, ccol, bias, gpost, slot):
                self.a = (src, c0, ccol, bias, gpost, slot)
                self.tok = []

            def start(self, j):
                src, c0, ccol, bias, gpost, slot = self.a
                if j == 0:
                    self.l = loads("row")
                    self.l.go(PO, ROW[0:1, :], bias, rowfree[0])
                    if gpost is not None:
                        self.l.go(PO, GB[:, :], gpost.broadcast_to([128, D]), gbfree[0])
                return ada_acc(src, c0 + 512 * j, ccol)

            def finish(self, j, i, toks):
                src, c0, ccol, bias, gpost, slot = self.a
                b = B.take()
                PE.mm(b.ap, ones, AC2[:, 2 * i, :], True, False, [toks, b.free])
                tp = PE.mm(b.ap, ones[0:1, :], ROW[0:1, 512 * j:512 * j + 512], False, True, self.l.tok, sig=True)
                accfree[i] = rowfree[0] = tp
                o = GR[:, slot, 512 * j:512 * j + 512]
                if gpost is not None:
                    t = VE.tt(o, b.ap, GB[:, 512 * j:512 * j + 512], MUL, [tp, self.l.tok])
                    gbfree[0] = t
                else:
                    t = VE.cp(o, b.ap, tp)
                b.done(t)
                self.tok.append(t)

        pending, inflight, bgon = [], [], [False]

        def background(n=1):
            for _ in range(n):
                if inflight:
                    o, j, i, toks = inflight.pop()
                    o.finish(j, i, toks)
                if pending:
                    o, j = pending.pop(0)
                    i, toks = o.start(j)
                    inflight.append((o, j, i, toks))

        def need(o):
            while len(o.tok) < o.n:
                background(1)
            return o.tok

        def rstd(ins, n, width, scratch, dst, after):
            for i in range(n):
                t = AC.act(scratch, ins(i), ACT.Square, acc=st[:, 32 + i:33 + i], after=[after])
            t = AC.act(st[:, 40:40 + n], st[:, 32:32 + n], ACT.Sqrt, bias=EPSC[:, :], scale=1.0 / width, after=t)
            return VE.rec(dst, st[:, 40:40 + n], t)

        def to_features(src, dst, scale, shift, after, ncols=8):
            toks = []
            for k in range(0, ncols, 2):
                b = B.take()
                m = min(2, ncols - k)
                for j in range(m):
                    for t in range(2):
                        tp = PE.tr(b.ap[:, j * 256 + t * 128:j * 256 + t * 128 + 128], src(t, k + j), ident,
                                   [after, b.free], sig=(j == m - 1 and t == 1))
                fr = []
                for j in range(m):
                    o, i_ = dst[:, k + j, :], b.ap[:, j * 256:j * 256 + 256]
                    s_, b_ = scale(k + j), shift(k + j)
                    dve = (k // 2) % 2
                    if s_ is None:
                        fr.append(VE.cp(o, i_, tp) if dve else AC.act(o, i_, ACT.Copy, after=tp))
                    elif b_ is None:
                        fr.append(VE.ts(o, i_, s_, MUL, after=tp) if dve else
                                  AC.act(o, i_, ACT.Copy, scale=s_, after=tp))
                    elif dve:
                        fr.append(VE.ts(o, i_, s_, MUL, b_, ADD, tp))
                    else:
                        fr.append(AC.act(o, i_, ACT.Identity, bias=b_, scale=s_, after=tp))
                b.done(*fr)
                toks += fr
            return toks

        def norm_mod(XN, HT, slot, modtok, after):
            t = rstd(lambda i: X[:, i, :], 2, D, XN[:, 0, :], st[:, 0:2], after)
            a = VE.ts(XN[:, 0, :], X[:, 0, :], st[:, 0:1], MUL, after=t)
            b = VE.ts(XN[:, 1, :], X[:, 1, :], st[:, 1:2], MUL)
            return to_features(lambda t_, k: XN[:, t_, k * 128:(k + 1) * 128], HT,
                               lambda k: MOD[:, 2 * slot + 1, k:k + 1], lambda k: MOD[:, 2 * slot, k:k + 1],
                               [a, b, modtok])

        def wtile(src, c0, n, r0=0, rows=1024):
            if bgon[0]:
                background(1)
            return ring.load(src[r0:r0 + rows, c0:c0 + n].rearrange("(k p) n -> p k n", p=128), rows // 128, n)

        def feat(w, c, m, HT, b, col, after):
            kc = w.ap.shape[1]
            return PE.mms(b.ap[0:m, col:col + 256], [(w.ap[:, k, c:c + m], HT[:, k, :]) for k in range(kc)],
                          [w.tok, b.free, after])

        def toks_(w, c, n, HT, t, b, col, after, start=True, stop=True, k0=0):
            kc = w.ap.shape[1]
            return PE.mms(b.ap[:, col:col + n],
                          [(HT[:, k0 + k, t * 128:(t + 1) * 128], w.ap[:, k, c:c + n]) for k in range(kc)],
                          [w.tok, b.free, after], start=start, stop=stop)

        def feats(w, ntile, HT, after, put):
            for j in range(0, ntile, 2):
                b = B.take()
                fr = []
                for i in range(min(2, ntile - j)):
                    tp = feat(w, (j + i) * 128, 128, HT, b, i * 256, after)
                for i in range(min(2, ntile - j)):
                    fr.append(put(j + i, b.ap[:, i * 256:i * 256 + 256], tp))
                b.done(*fr)
            w.done(tp)

        def bytoks(w, c, n, HT, after, put, done=True):
            for t in range(2):
                b = B.take()
                tp = toks_(w, c, n, HT, t, b, 0, after)
                b.done(put(t, b.ap[:, 0:n], tp))
            if done:
                w.done(tp)

        def out_proj(srcs, OT, after, put):
            for half in range(2):
                bs = [B.take(), B.take()]
                n = len(srcs)
                for s, (src, r0, kc) in enumerate(srcs):
                    w = wtile(src, half * 512, 512, r0, kc * 128)
                    for t in range(2):
                        tp = toks_(w, 0, 512, OT, t, bs[t], 0, after, start=s == 0, stop=s == n - 1, k0=r0 // 128)
                        if s == n - 1:
                            bs[t].tok = tp
                    w.done(tp)
                for t in range(2):
                    bs[t].done(put(t, half, bs[t].ap, bs[t].tok))

        def post_norm(Y, slot, after, scratch, modtok):
            t = rstd(lambda i: Y[:, i, :], 2, D, scratch, st[:, 2:4], after)
            for i in range(2):
                a = VE.stt(Y[:, i, :], Y[:, i, :], st[:, 2 + i:3 + i], GR[:, slot, :], MUL, MUL, [t, modtok])
                a = VE.tt(X[:, i, :], X[:, i, :], Y[:, i, :], ADD, a)
            return a

        def softmax_attn(ph, qT, kT, v, mask, O, after):
            SB = sb("att_s", [128, 8, 384], c=ph)
            PT = sb("att_p", [128, 4, 256], c=ph)
            pv = [None] * 4
            mx = sb("att_m", [128, 4, 8], c=ph)
            for t in range(2):
                nk = 128 * (t + 1)
                c0 = 0 if t == 0 else 128
                stok = {}
                for g in range(2):
                    bs = [B.take(), B.take()]
                    for par in range(2):
                        for i in range(2):
                            h = 4 * g + 2 * i + par
                            hp = 64 * par
                            stok[h] = PE.mm(bs[par].ap[:, i * 256:i * 256 + nk],
                                            qT[hp:hp + 64, h // 2, t * 128:t * 128 + 128],
                                            kT[hp:hp + 64, h // 2, 0:nk], True, True, [bs[par].free, after], sig=True)
                    mt = {}
                    sall = PE.last
                    for par in range(2):
                        for i in range(2):
                            h = 4 * g + 2 * i + par
                            mt[h] = VE.ttr(SB[:, h, c0:c0 + nk], bs[par].ap[:, i * 256:i * 256 + nk], mask(t), ADD, MAX,
                                           -3e38, mx[:, 0 + t, h:h + 1], sall)
                        bs[par].done(mt[4 * g + 2 + par])
                nt = VE.ts(mx[:, t, :], mx[:, t, :], -1.0, MUL, after=VE.last)
                bo = B.take()
                for h in range(0, 8, 2):
                    b = B.take()
                    for i in range(2):
                        et = AC.act(SB[:, h + i, c0:c0 + nk], SB[:, h + i, c0:c0 + nk], ACT.Exp,
                                    bias=mx[:, t, h + i:h + i + 1], acc=mx[:, 2 + t, h + i:h + i + 1], after=nt)
                        for k in range(t + 1):
                            tp = PE.tr(b.ap[:, i * 256 + k * 128:i * 256 + k * 128 + 128],
                                       SB[:, h + i, c0 + k * 128:c0 + k * 128 + 128], ident, [et, b.free],
                                       sig=(i == 1 and k == t))
                    ct = VE.cp(PT[:, h % 4:h % 4 + 2, 0:nk],
                               b.ap.rearrange("p (i n) -> p i n", i=2)[:, :, 0:nk], [tp, pv[h % 4]])
                    b.done(ct)
                    for i in range(2):
                        tp = PE.mms(bo.ap[:, (h + i) * 64:(h + i) * 64 + 64],
                                    [(PT[:, (h + i) % 4, k * 128:k * 128 + 128], v[:, k, (h + i) * 64:(h + i) * 64 + 64])
                                     for k in range(t + 1)], [ct, bo.free])
                    pv[h % 4] = tp
                rt = VE.rec(mx[:, 2 + t, :], mx[:, 2 + t, :], et)
                ot = VE.tt(O(t).rearrange("p (h d) -> p h d", h=8), bo.ap.rearrange("p (h d) -> p h d", h=8),
                           mx[:, 2 + t, :].unsqueeze(2).broadcast_to([128, 8, 64]), MUL, [rt, tp])
                bo.done(ot)
            return ot

        def head_norm(b, tp, gate, O, nh, SQ, col):
            r = st[:, col:col + nh]
            a = AC.act(SQ, b.ap, ACT.Square, after=tp)
            a = VE.red(r, SQ.rearrange("p (h d) -> p h d", h=nh), ADD, a)
            a = AC.act(r, r, ACT.Sqrt, bias=EPSC[:, :], scale=1.0 / 128, after=a)
            a = VE.rec(r, r, a)
            a = VE.tt(O.rearrange("p (h d) -> p h d", h=nh), b.ap.rearrange("p (h d) -> p h d", h=nh),
                      r.unsqueeze(2).broadcast_to([128, nh, 128]), MUL, a)
            b.done(a)
            return VE.tt(O, O, gate, MUL, [a])

        def first():
            wi = T["w_in"][0]
            need(mods[0])
            bgon[0] = True
            with ExitStack() as ph:
                XN = sb("XN", [128, 2, D], c=ph)
                HT = sb("HT", [128, 8, 256], c=ph)
                h = norm_mod(XN, HT, 0, mods[0].tok, None)
                qT = sb("qT", [128, 4, 256], c=ph)
                kT = sb("kT", [128, 4, 256], c=ph)
                va = sb("va", [128, 2, 512], c=ph)
                R, tm = XN[:, :, 0:512], XN[:, :, 512:768]

                def rope(w, dst, cn, sn):
                    toks = []

                    def put(t, p, tp):
                        x = p.rearrange("p (h a d) -> p h a d", h=8, a=2)
                        o = R[:, t, :].rearrange("p (h a d) -> p h a d", h=8, a=2)
                        cs = C(cn, 32 * t, 32 * t + 32).unsqueeze(1).broadcast_to([128, 8, 32])
                        sn_ = C(sn, 32 * t, 32 * t + 32).unsqueeze(1).broadcast_to([128, 8, 32])
                        u = tm[:, t, :].rearrange("p (h d) -> p h d", h=8)
                        VE.tt(o[:, :, 0, :], x[:, :, 0, :], cs, MUL, tp)
                        a = VE.tt(u, x[:, :, 1, :], sn_, MUL)
                        a = VE.tt(o[:, :, 0, :], o[:, :, 0, :], u, SUB, a)
                        VE.tt(o[:, :, 1, :], x[:, :, 1, :], cs, MUL)
                        a = VE.tt(u, x[:, :, 0, :], sn_, MUL, a)
                        toks.append(VE.tt(o[:, :, 1, :], o[:, :, 1, :], u, ADD, a))
                        return a
                    bytoks(w, 0, 512, HT, h, put)
                    r = to_features(lambda t, k: R[:, t, k * 128:(k + 1) * 128], dst, lambda k: None, lambda k: None,
                                    toks, 4)
                    VE.pend = VE.pend + [PE.last]
                    return r

                tq = rope(wtile(wi, 0, 512), qT, "cosq", "sinq")
                tk = rope(wtile(wi, 512, 512), kT, "cos", "sin")
                bytoks(wtile(wi, 1024, 512), 0, 512, HT, h, lambda t, p, tp: AC.act(va[:, t, :], p, ACT.Copy, after=tp))
                tv = AC.last
                qg = sb("qg", [128, 2, 256], c=ph)
                kg = sb("kg", [128, 2, 256], c=ph)
                vg = sb("vg", [128, 2, 512], c=ph)
                rg = sb("rg", [128, 2, 512], c=ph)
                la = sb("la", [128, 2, 256], c=ph)
                bb = sb("bb", [128, 2, 256], c=ph)
                glr = sb("glr", [16, 256], c=ph)
                wlr = sb("wlr", [16, 256], c=ph)
                lw = loads("wlr")
                lw.go(PO, wlr[:, :], T["w_gate_lr"][0])

                def put_qk(j, p, tp):
                    if j < 2:
                        return AC.act(qg[:, j, :], p, ACT.Copy, scale=0.125, after=tp)
                    return AC.act(kg[:, j - 2, :], p, ACT.Copy, after=tp)
                feats(wtile(wi, 1536, 512), 4, HT, h, put_qk)
                bytoks(wtile(wi, 2048, 512), 0, 512, HT, h, lambda t, p, tp: AC.act(vg[:, t, :], p, ACT.Copy, after=tp))
                bytoks(wtile(wi, 2560, 512), 0, 512, HT, h, lambda t, p, tp: AC.act(rg[:, t, :], p, ACT.Silu, after=tp))
                w = wtile(wi, 3072, 16)
                b = B.take()
                tp = feat(w, 0, 16, HT, b, 0, h)
                w.done(tp)
                a = VE.cp(glr[:, :], b.ap[0:16, 0:256], tp)
                b.done(a)
                b = B.take()
                for j in range(2):
                    tp = PE.mm(b.ap[:, j * 256:j * 256 + 256], wlr[:, j * 128:j * 128 + 128], glr[:, :], True, True,
                               [a, lw.tok, b.free], sig=True)
                fr = [VE.ts(la[:, j, :], b.ap[:, j * 256:j * 256 + 256], V("b_gate", j), ADD, after=tp) for j in range(2)]
                b.done(*fr)
                laf, bbf = la[:, :, :].rearrange("p a t -> p (a t)"), bb[:, :, :].rearrange("p a t -> p (a t)")
                a = AC.act(bbf, laf, ACT.Abs, after=fr)
                a = AC.act(bbf, bbf, ACT.Exp, scale=-1.0, after=a)
                a = AC.act(bbf, bbf, ACT.Ln, bias=1.0, after=a)
                a = VE.stt(laf, laf, 0.0, bbf, MIN, SUB, a)
                for j in range(2):
                    a2 = VE.scan(bb[:, j, :], C("R64"), la[:, j, :], 0.0, MUL, ADD, a)
                qd = sb("qd", [128, 2, 256], c=ph)
                ki = sb("ki", [128, 2, 256], c=ph)
                ke = sb("ke", [128, 2, 256], c=ph)
                al = sb("al", [128, 2, 4], c=ph)
                qdf, kif, kef = (x[:, :, :].rearrange("p a t -> p (a t)") for x in (qd, ki, ke))
                qgf, kgf = (x[:, :, :].rearrange("p a t -> p (a t)") for x in (qg, kg))
                bl = bb[:, :, :].rearrange("p a (n c) -> p (a n) c", c=64)
                x1 = AC.act(qdf, bbf, ACT.Exp, scale=1.0 / 16, after=a2)
                x2 = AC.act(kif, bbf, ACT.Exp, scale=-1.0 / 16, after=a2)
                x3 = VE.tt(ke[:, :, :].rearrange("p a (n c) -> p (a n) c", c=64),
                           bl[:, :, 63:64].broadcast_to([128, 8, 64]), bl, SUB, a2)
                x4 = AC.act(kef, kef, ACT.Exp, scale=1.0 / 16, after=x3)
                x5 = AC.act(al[:, :, :].rearrange("p a n -> p (a n)"), bl[:, :, 63], ACT.Exp, scale=1.0 / 16, after=a2)
                x1 = VE.tt(qdf, qdf, qgf, MUL, [x1, AC.last])
                x2 = VE.tt(kif, kif, kgf, MUL, x2)
                x4 = VE.tt(kef, kef, kgf, MUL, x4)
                O = sb("O", [128, 2, D], c=ph)
                with ExitStack() as pa:
                    to = softmax_attn(pa, qT, kT, va, lambda t: C(f"AB{t}"), lambda t: O[:, t, 0:512], [tq, tk, tv])
                barrier()
                keT = sb("keT", [128, 2, 256], c=ph)
                b = B.take()
                for j in range(2):
                    for t in range(2):
                        tp = PE.tr(b.ap[:, t * 256 + j * 128:t * 256 + j * 128 + 128], ke[:, j, t * 128:t * 128 + 128],
                                   ident, [x4, b.free], sig=True)
                a = AC.act(keT[:, :, :].rearrange("p a t -> p (a t)"), b.ap, ACT.Copy, after=tp)
                b.done(a)
                tke = a
                AT = sb("AT", [128, 8, 128], c=ph)
                z = VE.mset(AT[:, :, :], 0.0)
                att = []
                for t in range(2):
                    bs = [B.take(), B.take()]
                    for par in range(2):
                        for j in range(2):
                            hp = 64 * par
                            tp = PE.mm(bs[par].ap[:, j * 128:j * 128 + 128], ki[hp:hp + 64, j, t * 128:t * 128 + 128],
                                       qd[hp:hp + 64, j, t * 128:t * 128 + 128], True, True, [x1, x2, bs[par].free], sig=True)
                    for par in range(2):
                        for j in range(2):
                            a = VE.cpred(AT[:, t * 4 + 2 * j + par, :], C("U64").bitcast(U32),
                                         bs[par].ap[:, j * 128:j * 128 + 128], [z, tp])
                        bs[par].done(a)
                    att.append(a)
                S = sb("S", [128, 4, 2, 128], c=ph)
                sz = VE.mset(S[:, 0, :, :], 0.0)
                stk = [sz]
                for n in range(3):
                    t, c0 = n // 2, 64 * (n % 2)
                    bs = [B.take(), B.take()]
                    for j in range(2):
                        for par in range(2):
                            tp = PE.mm(bs[par].ap[64 * par:64 * par + 64, j * 128:j * 128 + 128],
                                       keT[c0:c0 + 64, t, j * 128 + 64 * par:j * 128 + 64 * par + 64],
                                       vg[c0:c0 + 64, t, (2 * j + par) * 128:(2 * j + par) * 128 + 128], True, True,
                                       [tke, bs[par].free], sig=True)
                    nw = []
                    for par in range(2):
                        for j in range(2):
                            hs = slice(64 * par, 64 * par + 64)
                            nw.append(VE.stt(S[hs, n + 1, j, :], S[hs, n, j, :], al[hs, j, n:n + 1],
                                             bs[par].ap[hs, j * 128:j * 128 + 128], MUL, ADD, [tp, x5, stk[-1]]))
                        bs[par].done(nw[-1])
                    stk.append(nw)
                SQ = XN[:, 0, 512:1024]
                for t in range(2):
                    bs = [B.take(), B.take()]
                    for par in range(2):
                        for j in range(2):
                            hd = 2 * j + par
                            o = bs[par].ap[:, j * 128:j * 128 + 128]
                            PE.mm(o, AT[:, t * 4 + hd, :], vg[:, t, hd * 128:hd * 128 + 128], True, False,
                                  [att[t], stk, bs[par].free])
                            for cc in range(2):
                                n = 2 * t + cc
                                hp = 64 * par
                                tp = PE.mm(bs[par].ap[64 * cc:64 * cc + 64, j * 128:j * 128 + 128],
                                           qd[hp:hp + 64, j, n * 64:n * 64 + 64], S[hp:hp + 64, n, j, :], False, True,
                                           sig=True)
                    G = XN[:, t, 0:512]
                    for par in range(2):
                        a = VE.cp(G.rearrange("p (j a d) -> p j a d", j=2, a=2)[:, :, par, :],
                                  bs[par].ap[:, 0:256].rearrange("p (j d) -> p j d", j=2), tp)
                        bs[par].done(a)
                    g = Bank(B, 0, G, None)
                    g.done = lambda *x: None
                    tg = head_norm(g, a, rg[:, t, :], O[:, t, 512:1024], 4, SQ, 44 + 4 * t)
                OT = HT
                tf = to_features(lambda t, k: O[:, t, k * 128:(k + 1) * 128], OT,
                                 lambda k: None if k < 4 else V("g_gla"), lambda k: None, [to, tg])
                need(rows[0])
                Y = XN
                out_proj([(T["w_out"][0], 0, 8)], OT, tf,
                         lambda t, half, p, tp: AC.act(Y[:, t, half * 512:half * 512 + 512], p, ACT.Copy, after=tp))
                post_norm(Y, 0, AC.last, O[:, 0, :], rows[0].tok)
            barrier()
            need(mods[1])
            bgon[0] = False
            moe(mods[1])

        def moe(m2):
            wgu, wd = T["w_gate_up"][0], T["w_down"][0]
            ph = ExitStack()
            with ph:
                XN = sb("XN2", [128, 2, D], c=ph)
                HT = sb("HT2", [128, 8, 256], c=ph)
                RW = sb("RW", [128, 8, 32], c=ph)
                RB = sb("RB", [128, 32], c=ph)
                BD = sb("BD", [32, D], c=ph)
                lr = loads("router")
                lr.go(PO, RW[:, :, :], T["router_w"][0].rearrange("(k p) e -> p k e", p=128))
                lr.go(PO, RB[:, :], T["router_b"].broadcast_to([128, 32]))
                lr.go(PO, BD[:, :], T["b_down"][0])
                h = norm_mod(XN, HT, 1, m2.tok, None)
                lg = sb("lg", [128, 2, 32], c=ph)
                G = sb("G", [128, 2, 32], c=ph)
                rk = sb("rk", [128, 2, 32], c=ph)
                sl = sb("sl", [128, 2, 32], c=ph)
                m8 = sb("m8", [128, 2, 8], c=ph)
                w4 = sb("w4", [128, 4, 32], c=ph)
                c4 = sb("c4", [128, 2, 4], c=ph)
                one32 = C("ones", 0, 32)
                for t in range(2):
                    b = B.take()
                    tp = PE.mms(b.ap[:, 0:32], [(HT[:, k, t * 128:t * 128 + 128], RW[:, k, :]) for k in range(8)],
                                [h, lr.tok, b.free])
                    a = VE.tt(lg[:, t, :], b.ap[:, 0:32], RB[:, :], ADD, [tp, lr.tok, VE.last])
                    b.done(a)
                    a = VE.do(lambda e, t=t: e.max(m8[:, t, :], lg[:, t, :]), a)
                    gt, eq, cs, x = (w4[:, i, :] for i in range(4))
                    a1 = VE.ts(gt, lg[:, t, :], m8[:, t, 3:4], ALU.is_gt, after=a)
                    a2 = VE.ts(eq, lg[:, t, :], m8[:, t, 3:4], ALU.is_equal)
                    VE.red(c4[:, t, 0:1], gt, ADD, a1)
                    a3 = VE.scan(cs, one32, eq, 0.0, MUL, ADD, a2)
                    a3 = VE.ts(x, cs, c4[:, t, 0:1], ADD, 4.5, ALU.is_lt, a3)
                    a3 = VE.tt(x, x, eq, MUL, a3)
                    a3 = VE.tt(sl[:, t, :], x, gt, ADD, a3)
                    n1 = VE.ts(c4[:, t, 1:2], m8[:, t, 0:1], -1.0, MUL)
                    e1 = AC.act(x, lg[:, t, :], ACT.Exp, bias=c4[:, t, 1:2], after=[a3, n1])
                    a3 = VE.ttr(G[:, t, :], x, sl[:, t, :], MUL, ADD, 0.0, c4[:, t, 2:3], e1)
                    a3 = VE.rec(c4[:, t, 3:4], c4[:, t, 2:3], a3)
                    a3 = VE.ts(G[:, t, :], G[:, t, :], c4[:, t, 3:4], MUL, after=a3)
                tG = a3
                cnt = sb("cnt", [128, 32], c=ph)
                flag = sb("flag", [128, 33], I32, c=ph)
                mxc = sb("mxc", [128, 33], c=ph)
                b = B.take()
                PE.mm(b.ap[:, 0:32], C("SU"), sl[:, 0, :], True, True, [tG, b.free])
                PE.mms(b.ap[:, 32:64], [(ones, sl[:, 0, :]), (C("SU"), sl[:, 1, :])])
                tp = PE.mms(b.ap[:, 64:96], [(ones, sl[:, 0, :]), (ones, sl[:, 1, :])])
                for t in range(2):
                    a = VE.stt(rk[:, t, :], b.ap[:, 32 * t:32 * t + 32], 1.0, sl[:, t, :], ADD, MUL, tp)
                    a = VE.ts(rk[:, t, :], rk[:, t, :], -1.0, ADD, after=a)
                trk = a
                a = VE.red(mxc[:, 32:33], b.ap[:, 64:96], MAX)
                a = VE.ts(mxc[:, 0:32], b.ap[:, 64:96], -1.0 if flip else 64.5, ALU.is_gt)
                b.done(a)
                a = VE.ts(mxc[:, 32:33], mxc[:, 32:33], -1.0 if flip else 128.5, ALU.is_gt)
                tflag = VE.cp(flag[:, :], mxc[:, :])
                ACCM = sb("ACCM", [128, 2, D], c=ph)
                GT = sb("GT", [32, 256], c=ph)
                b = B.take()
                for t in range(2):
                    tp = PE.tr(b.ap[0:32, t * 128:t * 128 + 128], G[:, t, :], ident, [tG, b.free], sig=True)
                a = VE.cp(GT[:, :], b.ap[0:32, 0:256], tp)
                b.done(a)
                ta = None
                for t in range(2):
                    for hf in range(2):
                        b = B.take()
                        tp = PE.mm(b.ap, GT[:, t * 128:t * 128 + 128], BD[:, hf * 512:hf * 512 + 512], True, True,
                                   [a, b.free, lr.tok], sig=True)
                        ta = VE.cp(ACCM[:, t, hf * 512:hf * 512 + 512], b.ap, tp)
                        b.done(ta)
                PG = sb("PG", [128, 2, 2, 128], c=ph)
                PGT = sb("PGT", [128, 2, 256], c=ph)
                XE = sb("XE", [128, 2, 8, 128], c=ph)
                BR = sb("BR", [33, 2048], c=ph)
                BB = sb("BB", [128, 2048], c=ph)
                T1 = sb("T1", [128, 512], c=ph)
                T2 = sb("T2", [128, 256], c=ph)
                AT = sb("AT2", [128, 8, 128], c=ph)
                A_ = HT[:, 0:4, :].rearrange("p k t -> p (k t)")
                Y = HT[:, 4:8, :].rearrange("p k t -> p (k t)")
                iota = C("iota")
                hold = {"br": None, "bb": None, "xe": [None, None], "pg": None, "pgt": [None, None], "at": None,
                        "y": None, "sc": None, "acc": ta}
                lbr = Loads(sem("s_br"))

                def gather(es, i, base, dup=False):
                    for j, e in enumerate(es):
                        lbr.go(AC, BR[32 * j:32 * j + 1, :], T["b_gate_up"][0:1, e, :], hold["br"])
                    PO.pend = flat(hold["bb"], list(PO.pend))
                    for j in reversed(range(len(es))):
                        m = 128 if j == len(es) - 1 else 64
                        bt = PO.do(lambda g, j=j, m=m: g.partition_broadcast(BB[0:m, :], BR[32 * j:32 * j + 1, :], m),
                                   lbr.tok)
                    hold["br"] = bt
                    if base is None:
                        shape = [128, 2, 2, 64]
                        v = [PG[:, x, :, :].rearrange("p t (e s) -> p t e s", e=2) for x in range(2)]
                        io = iota[:, 0:64].unsqueeze(1).unsqueeze(1).broadcast_to(shape)
                        VE.tt(v[0], io, rk[:, :, es[0]:es[0] + 2].unsqueeze(3).broadcast_to(shape), ALU.is_equal,
                              [trk, hold["pg"]])
                        pg = VE.tt(v[1], v[0], G[:, :, es[0]:es[0] + 2].unsqueeze(3).broadcast_to(shape), MUL)
                    else:
                        io = iota[:, 0:64].unsqueeze(1).broadcast_to([128, 2, 64]) if dup else iota
                        for t in range(2):
                            VE.ts(PG[:, 0, t, :].rearrange("p (e s) -> p e s", e=2) if dup else PG[:, 0, t, :], io, float(base), ADD, rk[:, t, es[0]:es[0] + 1], ALU.is_equal,
                                  [trk, hold["pg"]])
                            pg = VE.ts(PG[:, 1, t, :], PG[:, 0, t, :], G[:, t, es[0]:es[0] + 1], MUL)
                    xt = []
                    for k in range(0, 8, 4):
                        b = B.take()
                        for j in range(4):
                            f = (k + j) * 128
                            tp = PE.mms(b.ap[:, j * 128:j * 128 + 128],
                                        [(XN[:, t, f:f + 128], PG[:, 0, t, :]) for t in range(2)], [pg, b.free],
                                        sig=j == 3)
                        for j in range(4):
                            xt = AC.act(XE[:, i, k + j, :], b.ap[:, j * 128:j * 128 + 128], ACT.Identity,
                                        bias=MOD[:, 2, k + j:k + j + 1], scale=MOD[:, 3, k + j:k + j + 1],
                                        after=[tp, hold["xe"][i]])
                        b.done(xt)
                    b = B.take()
                    for t in range(2):
                        tp = PE.tr(b.ap[:, t * 128:t * 128 + 128], PG[:, 1, t, :], ident, [pg, b.free], sig=t == 1)
                    hold["pg"] = tp
                    tpg = AC.act(PGT[:, i, :], b.ap[:, 0:256], ACT.Copy, after=[tp, hold["pgt"][i]])
                    b.done(tpg)
                    return es, i, bt, xt, tpg

                def stream(es, src, c, lhs, b, after):
                    ws = [wtile(src[e], c * 512, 512) for e in es]
                    m = 128 // len(es)
                    for k in range(8):
                        for j, w in enumerate(ws):
                            tp = PE.mm(b.ap[j * m:j * m + m, :], lhs[:, k, j * m:j * m + m], w.ap[:, k, :], k == 0, k == 7,
                                       [w.tok, b.free, after], sig=k == 7)
                    for w in ws:
                        w.done(tp)
                    return tp

                def glu(out_):
                    v = T1[:, :].rearrange("p (n a) -> p n a", a=2)
                    a = VE.ts(v[:, :, 0], v[:, :, 0], 7.0, MIN)
                    a2 = AC.act(T2[:, :], v[:, :, 0], ACT.Sigmoid, scale=1.702, after=a)
                    VE.ts(v[:, :, 1], v[:, :, 1], 7.0, MIN, -7.0, MAX)
                    VE.stt(v[:, :, 1], v[:, :, 1], 1.0, v[:, :, 0], ADD, MUL)
                    return VE.tt(out_, v[:, :, 1], T2[:, :], MUL, [a2, hold["at"]])

                def gate_up(x):
                    es, i, bt, xt, _ = x
                    for q in range(4):
                        b = B.take()
                        tp = stream(es, wgu, q, XE[:, i], b, xt)
                        a = VE.tt(T1[:, :], b.ap, BB[:, q * 512:q * 512 + 512], ADD, [tp, bt])
                        b.done(a)
                        a = glu(A_[:, q * 256:q * 256 + 256])
                    hold["bb"] = a
                    hold["xe"][i] = tp
                    return a

                def down(x, ta_):
                    es = x[0]
                    for k in range(0, 8, 4):
                        b = B.take()
                        for j in range(4):
                            tp = PE.tr(b.ap[:, j * 128:j * 128 + 128], A_[:, (k + j) * 128:(k + j) * 128 + 128], ident,
                                       [ta_, b.free], sig=j == 3)
                        a = AC.act(AT[:, k:k + 4, :].rearrange("p k n -> p (k n)"), b.ap, ACT.Copy, after=[tp, hold["y"]])
                        b.done(a)
                    hold["at"] = tp
                    for hf in range(2):
                        b = B.take()
                        tp = stream(es, wd, hf, AT, b, a)
                        ty = AC.act(Y[:, hf * 512:hf * 512 + 512], b.ap, ACT.Copy, after=[tp, hold["sc"]])
                        b.done(ty)
                    hold["y"] = tp
                    return ty

                def halves(e, base):
                    es, i, bt, xt, tpg = gather((e,), 0, base, dup=True)
                    for q in range(0, 4, 2):
                        ws = [wtile(wgu[e], (q + j) * 512, 512) for j in range(2)]
                        b = B.take()
                        for k in range(8):
                            for j, w in enumerate(ws):
                                tp = PE.mm(b.ap[64 * j:64 * j + 64, :], XE[:, i, k, 64 * j:64 * j + 64], w.ap[:, k, :],
                                           k == 0, k == 7, [w.tok, b.free, xt], sig=k == 7)
                        for w in ws:
                            w.done(tp)
                        for j in range(2):
                            hs = slice(64 * j, 64 * j + 64)
                            a = VE.tt(T1[hs, :], b.ap[hs, :], BB[hs, (q + j) * 512:(q + j) * 512 + 512], ADD, [tp, bt])
                        b.done(a)
                        a = glu(A_[:, q * 128:q * 128 + 256])
                    hold["bb"] = a
                    hold["xe"][i] = tp
                    b = B.take()
                    for k in range(4):
                        tp = PE.tr(b.ap[:, k * 128:k * 128 + 128], A_[:, k * 128:k * 128 + 128], ident, [a, b.free], sig=k == 3)
                    hold["at"] = tp
                    a = AC.act(AT[:, 0:4, :].rearrange("p k n -> p (k n)"), b.ap, ACT.Copy, after=[tp, hold["y"]])
                    b.done(a)
                    ws = [wtile(wd[e], j * 512, 512) for j in range(2)]
                    b = B.take()
                    for k in range(8):
                        q, c = k // 2, k % 2
                        for j, w in enumerate(ws):
                            tp = PE.mm(b.ap[64 * j:64 * j + 64, :], AT[:, 2 * (q // 2) + c, 64 * (q % 2):64 * (q % 2) + 64],
                                       w.ap[:, k, :], k == 0, k == 7, [w.tok, b.free, a], sig=k == 7)
                    for w in ws:
                        w.done(tp)
                    hold["y"] = tp
                    ty = AC.act(Y[:, 0:512], b.ap, ACT.Copy, after=[tp, hold["sc"]])
                    b.done(ty)
                    for t in range(2):
                        for hf in range(2):
                            hs = slice(64 * hf, 64 * hf + 64)
                            b = B.take()
                            tp = PE.mm(b.ap, PGT[hs, i, t * 128:t * 128 + 128], Y[hs, 0:512], True, True,
                                       [ty, tpg, b.free], sig=True)
                            hold["acc"] = VE.tt(ACCM[:, t, hf * 512:hf * 512 + 512], ACCM[:, t, hf * 512:hf * 512 + 512],
                                                b.ap, ADD, tp)
                            b.done(hold["acc"])
                    hold["sc"] = tp
                    hold["pgt"][i] = tp

                def scatter(x, ty):
                    i, tpg = x[1], x[4]
                    for t in range(2):
                        for hf in range(2):
                            b = B.take()
                            tp = PE.mm(b.ap, PGT[:, i, t * 128:t * 128 + 128], Y[:, hf * 512:hf * 512 + 512], True, True,
                                       [ty, tpg, b.free], sig=True)
                            hold["acc"] = VE.tt(ACCM[:, t, hf * 512:hf * 512 + 512], ACCM[:, t, hf * 512:hf * 512 + 512],
                                                b.ap, ADD, tp)
                            b.done(hold["acc"])
                    hold["sc"] = tp
                    hold["pgt"][i] = tp

                x = gather((0, 1), 0, None)
                for pr in range(E_N // 2):
                    a = gate_up(x)
                    nx = gather((2 * pr + 2, 2 * pr + 3), (pr + 1) % 2, None) if pr < E_N // 2 - 1 else None
                    y = down(x, a)
                    scatter(x, y)
                    x = nx
                    if pr < 7:
                        background(1)
                queues = (PE, AC, VE, PO, SP)

                def branch(bit, body):
                    ends = [q.last for q in queues[:4]]
                    start = [q.n for q in queues]
                    uses = list(ring.uses)
                    nbr = lbr.n
                    for q in queues:
                        def enter(e, seen, outer, q=q):
                            for s_, v_ in [tflag]:
                                if seen.get(s_.name, 0) < v_:
                                    e.wait_ge(s_, v_)
                                    seen[s_.name] = v_
                            kept = dict(seen)
                            reg = e.value_load(flag[0:1, bit:bit + 1], min_val=0, max_val=1)
                            g = e.If(reg == 1)
                            g.__enter__()
                            if q is not SP:
                                for s_, v_ in ends:
                                    e.wait_ge(s_, v_)
                                    seen[s_.name] = max(v_, seen.get(s_.name, 0))
                            return (g, kept)
                        q.raw(enter)
                    B.free = [None] * 8
                    body()
                    toks = [q.last for q in queues[:4]]
                    more = {q.sem.name: [(q.sem, q.n - s_)] for q, s_ in zip(queues, start)}
                    more[SP.sem.name] = [(s_, 16 * (u1 - u0)) for s_, u1, u0 in zip(ring.sems, ring.uses, uses)]
                    more[AC.sem.name] += [(lbr.sem, lbr.n - nbr)]
                    before = {q.sem.name: [t_] for q, t_ in zip(queues, ends)}
                    before[SP.sem.name] = [(s_, 16 * u) for s_, u in zip(ring.sems, uses)]
                    before[AC.sem.name] = [ends[1], (lbr.sem, nbr)]
                    for q in queues:
                        def leave(e, seen, outer, q=q):
                            if q is not SP:
                                for s_, v_ in toks:
                                    if seen.get(s_.name, 0) < v_:
                                        e.wait_ge(s_, v_)
                            g, kept = outer
                            g.__exit__(None, None, None)
                            with e.Else():
                                for s_, v_ in before[q.sem.name]:
                                    if v_:
                                        e.wait_ge(s_, v_)
                                for s_, n_ in more[q.sem.name]:
                                    if n_:
                                        e.sem_inc(s_, n_)
                            seen.clear()
                            seen.update(kept)
                            return None
                        q.raw(leave)
                    for q in queues[:4]:
                        q.pend = q.pend + toks
                    ring.free = [toks[0]] * NS
                    B.free = [None] * 8

                def alone(e, base):
                    x = gather((e,), 0, base)
                    scatter(x, down(x, gate_up(x)))

                barrier()
                for e in range(E_N):
                    branch(e, lambda: halves(e, 64))

                def rest():
                    for e in range(E_N):
                        alone(e, 128)
                branch(E_N, rest)
                toks = [VE.last]
                post_norm(ACCM, 1, toks, XN[:, 0, :], need(rows[1]))
            barrier()

        def bc(ap, n):
            return ap.unsqueeze(1).broadcast_to([128, n, ap.shape[1]])

        def ex(ap, n):
            return ap.unsqueeze(2).broadcast_to([128, ap.shape[1], n])

        def heads(ap, n):
            return ap.rearrange("p (h d) -> p h d", h=n)

        def second():
            wi = T["w_in_2"][0]
            with ExitStack() as ph:
                XN = sb("XN3", [128, 2, D], c=ph)
                HT = sb("HT3", [128, 8, 256], c=ph)
                O = sb("O3", [128, 2, D], c=ph)
                bgon[0] = True
                h = norm_mod(XN, HT, 2, need(mods[2]), None)
                zd = sb("zd", [128, 2, 512], c=ph)
                CO = sb("CO", [128, 12, 256], c=ph)
                BG = sb("BG", [128, 2, 8], c=ph)
                AD = sb("AD", [128, 8], c=ph)
                zm = sb("zm", [128, 2, 512], c=ph)
                ld = loads("decay")
                ld.go(PO, AD[:, 0:4], T["a_log_2"].broadcast_to([128, 4]))
                ld.go(PO, AD[:, 4:8], T["dt_bias_2"].broadcast_to([128, 4]))
                pm = ExitStack()
                qm = sb("qm", [128, 4, 256], c=pm)
                km = sb("km", [128, 4, 256], c=pm)
                vm = sb("vm", [128, 2, 512], c=pm)
                cb = ExitStack()
                CI = sb("CI", [128, 2, 4, 260], c=cb)
                ct = [None, None]
                z = VE.mset(CI[:, :, :, 0:3], 0.0)
                for g in range(3):
                    i = g % 2
                    cw = []

                    def put(j, p, tp, i=i):
                        return AC.act(CI[:, i, j, 3:259], p, ACT.Copy, after=[tp, ct[i], z])
                    feats(wtile(wi, 512 * g, 512), 4, HT, h, put)
                    a = AC.last
                    for j in range(4):
                        f = 4 * g + j
                        VE.ts(CO[:, f, :], CI[:, i, j, 0:256], V("conv_w_2", f), MUL, after=a)
                        for k in range(1, 4):
                            ct[i] = VE.stt(CO[:, f, :], CI[:, i, j, k:k + 256], V("conv_w_2", 12 * k + f),
                                           CO[:, f, :], MUL, ADD)
                    cof = CO[:, 4 * g:4 * g + 4, :].rearrange("p j t -> p (j t)")
                    tco = AC.act(cof, cof, ACT.Silu, after=ct[i])
                w = wtile(wi, 1536, 520)
                bytoks(w, 0, 512, HT, h, lambda t, p, tp: AC.act(zd[:, t, :], p, ACT.Silu, after=tp), done=False)
                b = B.take()
                for t in range(2):
                    tp = toks_(w, 512, 8, HT, t, b, 8 * t, h)
                w.done(tp)
                bg = BG[:, :, :]
                a = VE.cp(bg, b.ap[:, 0:16].rearrange("p (t c) -> p t c", t=2), tp)
                b.done(a)
                sp = st[:, 0:8].rearrange("p (t c) -> p t c", t=2)
                a1 = AC.act(BG[:, :, 0:4], BG[:, :, 0:4], ACT.Sigmoid, after=a)
                a2 = VE.tt(BG[:, :, 4:8], BG[:, :, 4:8], AD[:, 4:8].unsqueeze(1).broadcast_to([128, 2, 4]), ADD, ld.tok)
                a2 = AC.act(sp, BG[:, :, 4:8], ACT.Abs, after=a2)
                a2 = AC.act(sp, sp, ACT.Exp, scale=-1.0)
                a2 = AC.act(sp, sp, ACT.Ln, bias=1.0)
                a3 = AC.act(AD[:, 0:4], AD[:, 0:4], ACT.Exp, after=ld.tok)
                a2 = VE.stt(BG[:, :, 4:8], BG[:, :, 4:8], 0.0, sp, MAX, ADD, [a2, a3])
                a2 = VE.stt(BG[:, :, 4:8], BG[:, :, 4:8], -1.0, AD[:, 0:4].unsqueeze(1).broadcast_to([128, 2, 4]), MUL, MUL)
                tbg = [a1, a2]
                feats(wtile(wi, 2056, 512), 4, HT, h, lambda j, p, tp: AC.act(qm[:, j, :], p, ACT.Copy, scale=0.125, after=tp))
                feats(wtile(wi, 2568, 512), 4, HT, h, lambda j, p, tp: AC.act(km[:, j, :], p, ACT.Copy, after=tp))
                bytoks(wtile(wi, 3080, 512), 0, 512, HT, h, lambda t, p, tp: AC.act(vm[:, t, :], p, ACT.Copy, after=tp))
                bytoks(wtile(wi, 3592, 512), 0, 512, HT, h, lambda t, p, tp: AC.act(zm[:, t, :], p, ACT.Silu, after=tp))
                cb.close()
                barrier()
                with ExitStack() as pa:
                    to = softmax_attn(pa, qm, km, vm, lambda t: C(f"CB{t}"), lambda t: O[:, t, 512:1024], [AC.last])
                for t in range(2):
                    VE.tt(O[:, t, 512:1024], O[:, t, 512:1024], zm[:, t, :], MUL)
                pm.close()
                barrier()
                pd = ExitStack()
                SQ = XN[:, 1, :]
                for g in range(2):
                    cof = CO[:, 4 * g:4 * g + 4, :].rearrange("p j t -> p (j t)")
                    a = AC.act(SQ[:, :], cof, ACT.Square)
                    bs = [B.take(), B.take()]
                    for i in range(2):
                        tp = PE.mm(bs[i].ap, ones, SQ[:, 512 * i:512 * i + 512], True, True, [a, bs[i].free], sig=True)
                    for i in range(2):
                        a = AC.act(SQ[:, 512 * i:512 * i + 512], bs[i].ap, ACT.Ln, bias=EPSC[:, :], after=tp)
                        bs[i].done(a)
                    a = AC.act(SQ[:, :], SQ[:, :], ACT.Exp, scale=-0.5)
                    tn = VE.stt(cof, cof, float(128 ** -0.5) if g == 0 else 1.0, SQ[:, :], MUL, MUL, a)
                    AC.pend = AC.pend + [tn]
                qT, kT, vT = CO[:, 0:4, :], CO[:, 4:8, :], CO[:, 8:12, :]
                GC = sb("GC", [128, 2, 4, 4], c=pd)
                per = {}
                b = B.take()
                for t in range(2):
                    PE.mm(b.ap[:, 8 * t:8 * t + 4], C("U64"), BG[:, t, 4:8], True, True, [tbg, b.free])
                    tp = PE.mm(b.ap[:, 8 * t + 4:8 * t + 8], C("B64"), BG[:, t, 4:8], True, True, sig=True)
                for t in range(2):
                    a = VE.cp(GC[:, t, 0, :], b.ap[:, 8 * t:8 * t + 4], tp)
                    a2 = VE.tt(GC[:, t, 2, :], b.ap[:, 8 * t + 4:8 * t + 8], GC[:, t, 0, :], SUB, a)
                    a = AC.act(GC[:, t, 1, :], GC[:, t, 0, :], ACT.Exp, after=a2)
                    a = AC.act(GC[:, t, 2, :], GC[:, t, 2, :], ACT.Exp)
                    a = VE.stt(GC[:, t, 1, :], GC[:, t, 1, :], -1.0, BG[:, t, 0:4], MUL, MUL, a)
                b.done(a)
                W5, W6 = XN[:, 0, 0:512], XN[:, 0, 512:1024]
                for t in range(2):
                    p = per[t] = {n: sb(f"d{n}{t}", [128, 512], c=pd)
                                  for n in ("eR", "aT", "qk", "U", "T", "Y", "kg", "vb")}
                    p["vn"], p["wT"], p["qg"], p["kb"] = p["Y"], p["T"], p["aT"], O[:, t, 0:512]
                    tok = slice(t * 128, t * 128 + 128)
                    a = VE.tt(heads(W5, 4), bc(C("U64"), 4), ex(BG[:, t, 4:8], 128), MUL, PE.last)
                    a = VE.tt(heads(W6, 4), bc(ident, 4), ex(BG[:, t, 0:4], 128), MUL)
                    b, b2 = B.take(), B.take()
                    PE.mm(b.ap, ones, W5, True, True, [a, b.free])
                    tp = PE.mm(b2.ap, ones, W6, True, True, [b2.free], sig=True)
                    a = AC.act(p["eR"][:, :], b.ap, ACT.Exp, after=tp)
                    a = VE.tt(heads(W5, 4), heads(b.ap, 4), ex(GC[:, t, 0, :], 128), SUB, [a, tp])
                    b.done(a)
                    a = VE.ts(W5, W5, 0.0, MIN)
                    a = AC.act(W5, W5, ACT.Exp, after=a)
                    a = VE.tt(heads(W6, 4), heads(W5, 4), bc(C("SU64"), 4), MUL, [a, tp])
                    a = VE.tt(W6, W6, b2.ap, MUL)
                    b2.done(a)
                    a = VE.tt(heads(W5, 4), heads(W5, 4), bc(C("U64"), 4), MUL)
                    b, b2 = B.take(), B.take()
                    for hd in range(4):
                        hc = slice(hd * 128, hd * 128 + 128)
                        PE.mm(b.ap[:, hc], kT[:, hd, tok], kT[:, hd, tok], True, True, [tn, b.free])
                    for hd in range(4):
                        hc = slice(hd * 128, hd * 128 + 128)
                        tp = PE.mm(b2.ap[:, hc], kT[:, hd, tok], qT[:, hd, tok], True, True, [b2.free], sig=True)
                    a = VE.tt(p["aT"][:, :], b.ap, W6, MUL, tp)
                    b.done(a)
                    a = VE.tt(p["qk"][:, :], b2.ap, W5, MUL)
                    b2.done(a)
                    a = VE.tt(heads(W5, 4), heads(p["aT"][:, :], 4), bc(C("H1"), 4), MUL)
                    a = VE.tt(heads(p["U"][:, :], 4), bc(ident, 4), heads(W5, 4), SUB)
                    b = B.take()
                    for hd in range(4):
                        hc = slice(hd * 128, hd * 128 + 128)
                        tp = PE.tr(b.ap[:, hc], p["U"][:, hc], ident, [a, b.free], sig=hd == 3)
                    p["tU"] = p["tT"] = AC.act(p["T"][:, :], b.ap, ACT.Copy, after=tp)
                    b.done(p["tT"])
                    b, b2 = B.take(), B.take()
                    for hd in range(4):
                        hc = slice(hd * 128, hd * 128 + 128)
                        PE.tr(b.ap[:, hc], kT[:, hd, tok], ident, [tn, b.free])
                    for hd in range(4):
                        hc = slice(hd * 128, hd * 128 + 128)
                        tp = PE.tr(b2.ap[:, hc], vT[:, hd, tok], ident, [tco, b2.free], sig=hd == 3)
                    VE.tt(heads(p["kb"], 4), heads(b.ap, 4), ex(GC[:, t, 1, :], 128), MUL, tp)
                    a = VE.tt(heads(p["kg"][:, :], 4), heads(b.ap, 4), ex(GC[:, t, 2, :], 128), MUL)
                    b.done(a)
                    a = VE.tt(heads(p["vb"][:, :], 4), heads(b2.ap, 4), ex(BG[:, t, 0:4], 128), MUL)
                    b2.done(a)
                    p["tk"] = a
                for L in (2, 4, 8, 16, 32):
                    for t in range(2):
                        p = per[t]
                        Wt = (W5, W6)[t]
                        a = VE.tt(heads(Wt, 4), heads(p["aT"][:, :], 4), bc(C(f"H{L}"), 4), MUL, [PE.last])
                        b = B.take()
                        for hd in range(4):
                            hc = slice(hd * 128, hd * 128 + 128)
                            tp = PE.mm(b.ap[:, hc], Wt[:, hc], p["T"][:, hc], True, True, [a, p["tT"], b.free], sig=hd == 3)
                        ty = AC.act(p["Y"][:, :], b.ap, ACT.Copy, after=tp)
                        b.done(ty)
                        b = B.take()
                        for hd in range(4):
                            hc = slice(hd * 128, hd * 128 + 128)
                            tp = PE.mm(b.ap[:, hc], p["Y"][:, hc], p["U"][:, hc], True, True, [ty, p["tU"], b.free],
                                       sig=hd == 3)
                        if L < 32:
                            b2 = B.take()
                            for hd in range(4):
                                hc = slice(hd * 128, hd * 128 + 128)
                                tp = PE.mm(b2.ap[:, hc], p["U"][:, hc], p["Y"][:, hc], True, True, [b2.free], sig=hd == 3)
                            p["tT"] = VE.tt(p["T"][:, :], p["T"][:, :], b2.ap, SUB, tp)
                            b2.done(p["tT"])
                        p["tU"] = VE.tt(p["U"][:, :], p["U"][:, :], b.ap, SUB, tp)
                        b.done(p["tU"])
                for t in range(2):
                    p = per[t]
                    b = B.take()
                    for hd in range(4):
                        hc = slice(hd * 128, hd * 128 + 128)
                        tp = PE.mm(b.ap[:, hc], p["kb"][:, hc], p["U"][:, hc], True, True, [p["tU"], p["tk"], b.free],
                                   sig=hd == 3)
                    a = AC.act(p["wT"][:, :], b.ap, ACT.Copy, after=tp)
                    b.done(a)
                    tok = slice(t * 128, t * 128 + 128)
                    p["tw"] = [a, VE.tt(heads(p["qg"][:, :], 4), qT[:, :, tok], heads(p["eR"][:, :], 4), MUL)]
                S = zm[:, 0, :]
                ts_ = VE.mset(S, 0.0)
                for n in range(4):
                    t, c0 = n // 2, 64 * (n % 2)
                    p = per[t]
                    rw = slice(c0, c0 + 64)
                    b = B.take()
                    for hd in range(4):
                        hc = slice(hd * 128, hd * 128 + 128)
                        cc = slice(hd * 128 + c0, hd * 128 + c0 + 64)
                        PE.mm(b.ap[rw, hc], p["U"][:, cc], p["vb"][:, hc], True, False, [p["tw"], ts_, b.free])
                        tp = PE.mm(b.ap[rw, hc], p["wT"][:, cc], S[:, hc], False, True, sig=hd == 3)
                    tv = AC.act(p["vn"][rw, :], b.ap[rw, :], ACT.Copy, after=tp)
                    b.done(tv)
                    if n % 2 == 0:
                        bo = B.take()
                    for hd in range(4):
                        hc = slice(hd * 128, hd * 128 + 128)
                        cc = slice(hd * 128 + c0, hd * 128 + c0 + 64)
                        PE.mm(bo.ap[rw, hc], p["qg"][:, cc], S[:, hc], True, False, [bo.free, ts_, tv])
                        tp = PE.mm(bo.ap[rw, hc], p["qk"][rw, cc], p["vn"][rw, hc], False, True, sig=hd == 3)
                    if n < 3:
                        b = B.take()
                        for hd in range(4):
                            hc = slice(hd * 128, hd * 128 + 128)
                            tp = PE.mm(b.ap[:, hc], p["kg"][rw, hc], p["vn"][rw, hc], True, True, b.free, sig=hd == 3)
                        for hd in range(4):
                            hc = slice(hd * 128, hd * 128 + 128)
                            ts_ = VE.stt(S[:, hc], S[:, hc], p["eR"][:, hd * 128 + c0 + 63:hd * 128 + c0 + 64],
                                         b.ap[:, hc], MUL, ADD, tp)
                        b.done(ts_)
                    if n % 2 == 1:
                        tg = head_norm(bo, tp, zd[:, t, :], O[:, t, 0:512], 4, SQ[:, 0:512], 44 + 4 * t)
                pd.close()
                barrier()
                OT = sb("OT3", [128, 8, 256], c=ph)
                tf = to_features(lambda t, k: O[:, t, k * 128:(k + 1) * 128], OT,
                                 lambda k: V("dn_norm_g_2") if k < 4 else None, lambda k: None, [tg, to])
                SG = sb("SG", [128, 2, 4, 256], c=ph)
                MX = sb("MX", [128, 8, 256], c=ph)
                sgf = [None, None]
                for half in range(2):
                    for br in range(2):
                        def put(j, p, tp, br=br):
                            return AC.act(SG[:, br, j, :], p, ACT.Sigmoid, after=[tp, sgf[br]])
                        feats(wtile(wi, 4104 + 1024 * br + 512 * half, 512), 4, HT, h, put)
                    tsg = AC.last

                    def put0(j, p, tp):
                        return VE.tt(MX[:, 4 * half + j, :], p, SG[:, 0, j, :], MUL, [tp, tsg])

                    def put1(j, p, tp):
                        return VE.tt(SG[:, 1, j, :], p, SG[:, 1, j, :], MUL, [tp, tsg])
                    feats(wtile(T["w_proj_dn_2"][0], 512 * half, 512, 0, 512), 4, OT[:, 0:4, :], tf, put0)
                    feats(wtile(T["w_proj_mb_2"][0], 512 * half, 512, 0, 512), 4, OT[:, 4:8, :], tf, put1)
                    tm = VE.tt(MX[:, 4 * half:4 * half + 4, :], MX[:, 4 * half:4 * half + 4, :], SG[:, 1, :, :], ADD)
                    sgf = [tm, tm]
                Y = XN
                out_proj([(T["w_out_2"][0], 0, 8)], MX, tm,
                         lambda t, half, p, tp: AC.act(Y[:, t, half * 512:half * 512 + 512], p, ACT.Copy, after=tp))
                post_norm(Y, 2, AC.last, O[:, 0, :], need(rows[2]))
            barrier()

        def add_gated(slot, tmp, tok):
            tok = tok()

            def put(t, half, p, tp):
                hs = slice(half * 512, half * 512 + 512)
                a = VE.tt(tmp[:, t, hs], p, GR[:, slot, hs], MUL, [tp, tok])
                VE.tt(X[:, t, hs], X[:, t, hs], tmp[:, t, hs], ADD, a)
                return a
            return put

        def ffn(layer, slot, grslot, modtok, growtok):
            w_in, w_out = T["ffn_w_in_3"][layer], T["ffn_w_out_3"][layer]
            with ExitStack() as ph:
                XN = sb(f"XF{layer}", [128, 2, D], c=ph)
                HT = sb(f"HF{layer}", [128, 8, 256], c=ph)
                A = sb(f"AF{layer}", [128, FT, 256], c=ph)
                CI = sb(f"CF{layer}", [128, 2, 4, 258], c=ph)
                z = VE.mset(CI[:, :, :, 0:2], 0.0)
                h = norm_mod(XN, HT, slot, modtok, None)
                hold = [None, None]
                for g in range(6):
                    n = 4 if g < 5 else 2
                    i = g % 2

                    def put(j, p, tp, i=i):
                        return AC.act(CI[:, i, j, 2:258], p, ACT.Copy, after=[tp, hold[i], z])
                    feats(wtile(w_in, 512 * g, 128 * n), n, HT, h, put)
                    a = AC.last
                    for j in range(n):
                        f = 4 * g + j
                        cw = 66 * layer + f
                        VE.ts(A[:, f, :], CI[:, i, j, 0:256], V("ffn_conv_w_3", cw), MUL,
                              V("ffn_conv_b_3", 22 * layer + f), ADD, a)
                        VE.stt(A[:, f, :], CI[:, i, j, 1:257], V("ffn_conv_w_3", cw + 22), A[:, f, :], MUL, ADD)
                        hold[i] = VE.stt(A[:, f, :], CI[:, i, j, 2:258], V("ffn_conv_w_3", cw + 44), A[:, f, :], MUL, ADD)
                    af = A[:, 4 * g:4 * g + n, :].rearrange("p j t -> p (j t)")
                    AC.act(af, af, ACT.Gelu_apprx_tanh, after=hold[i])
                ta = AC.last
                for g in range(6):
                    n = 4 if g < 5 else 2

                    def put(j, p, tp, g=g):
                        return VE.tt(A[:, 4 * g + j, :], A[:, 4 * g + j, :], p, MUL, [tp, ta])
                    feats(wtile(w_in, FFN + 512 * g, 128 * n), n, HT, h, put)
                out_proj([(w_out, 0, 8), (w_out, 1024, 8), (w_out, 2048, 6)], A, VE.last, add_gated(grslot, XN, growtok))
            barrier()

        def even(modtok, growtok):
            wi = T["even_w_in_3"][0]
            with ExitStack() as ph:
                XN = sb("XE3", [128, 2, D], c=ph)
                HT = sb("HE3", [128, 8, 256], c=ph)
                h = norm_mod(XN, HT, 3, modtok, None)
                names = ("qa", "ka", "lf", "bcu", "qb", "kb")
                qa, ka, lf, bcu, qb, kb = (sb("e" + n, [128, 4, 256], c=ph) for n in names)
                ia, ga, vb = (sb("e" + n, [128, 2, 512], c=ph) for n in ("ia", "ga", "vb"))
                fl = lambda x: x[:, :, :].rearrange("p j t -> p (j t)")
                feats(wtile(wi, 0, 512), 4, HT, h, lambda j, p, tp: AC.act(qa[:, j, :], p, ACT.Copy, after=tp))
                feats(wtile(wi, 512, 512), 4, HT, h, lambda j, p, tp: AC.act(lf[:, j, :], p, ACT.Copy, after=tp))
                bytoks(wtile(wi, 1024, 512), 0, 512, HT, h, lambda t, p, tp: AC.act(ia[:, t, :], p, ACT.Copy, after=tp))
                bytoks(wtile(wi, 1536, 512), 0, 512, HT, h, lambda t, p, tp: AC.act(ga[:, t, :], p, ACT.Silu, after=tp))
                feats(wtile(wi, 2048, 512), 4, HT, h,
                      lambda j, p, tp: AC.act(qb[:, j, :], p, ACT.Copy, scale=float(128 ** -0.5), after=tp))
                feats(wtile(wi, 2560, 512), 4, HT, h, lambda j, p, tp: AC.act(kb[:, j, :], p, ACT.Copy, after=tp))
                bytoks(wtile(wi, 3072, 512), 0, 512, HT, h, lambda t, p, tp: AC.act(vb[:, t, :], p, ACT.Copy, after=tp))
                AC.act(fl(ka), fl(lf), ACT.Sigmoid, scale=-1.0)
                AC.act(fl(bcu), fl(lf), ACT.Abs)
                AC.act(fl(bcu), fl(bcu), ACT.Exp, scale=-1.0)
                a = AC.act(fl(bcu), fl(bcu), ACT.Ln, bias=1.0)
                VE.stt(fl(lf), fl(lf), 0.0, fl(bcu), MIN, SUB, a)
                for j in range(4):
                    tb = VE.scan(bcu[:, j, :], C("R128"), lf[:, j, :], 0.0, MUL, ADD)
                Et, QL, KL = lf, XN[:, 0, :], XN[:, 1, :]
                SC = sb("SC", [128, 2, 512], c=ph)
                z = VE.mset(SC[:, :, :], 0.0)
                free = None
                for L in (0, 1, 2, 4, 8, 16, 32, 64):
                    if L:
                        v = fl(bcu).rearrange("p (n l) -> p n l", l=2 * L)
                        ev = fl(Et).rearrange("p (n l) -> p n l", l=2 * L)
                        n = 1024 // (2 * L)
                        bm = v[:, :, L - 1:L].broadcast_to([128, n, L])
                        VE.tt(ev[:, :, 0:L], bm, v[:, :, 0:L], SUB, [AC.last, PO.last if PO.n else None])
                        a = VE.tt(ev[:, :, L:2 * L], v[:, :, L:2 * L], bm, SUB)
                        a = AC.act(fl(Et), fl(Et), ACT.Exp, after=a)
                        t1 = VE.tt(QL, fl(qa), fl(Et), MUL, [a, free])
                        t2 = PO.tt(KL, fl(ka), fl(Et), MUL, [a, free])
                        ql, kl, m = heads(QL, 4), heads(KL, 4), C(f"H{L}")
                    else:
                        t1 = t2 = AC.last
                        ql, kl, m = qa[:, :, :], ka[:, :, :], ident
                    for t in range(2):
                        b = B.take()
                        tok = slice(t * 128, t * 128 + 128)
                        for hd in range(4):
                            tp = PE.mm(b.ap[:, hd * 128:hd * 128 + 128], kl[:, hd, tok], ql[:, hd, tok], True, True,
                                       [t1, t2, b.free], sig=hd == 3)
                        a = VE.cpred(heads(SC[:, t, :], 4), bc(m.bitcast(U32), 4), heads(b.ap, 4), tp)
                        b.done(a)
                    free = tp
                tsc = a
                K1, Q1, KT, S0 = (sb("e" + n, [128, 512], c=ph) for n in ("K1", "Q1", "KT", "S0"))
                a = VE.tt(heads(K1[:, :], 4), bcu[:, :, 127:128].broadcast_to([128, 4, 128]), bcu[:, :, 0:128], SUB)
                AC.act(K1[:, :], K1[:, :], ACT.Exp, after=a)
                a = AC.act(heads(Q1[:, :], 4), bcu[:, :, 128:256], ACT.Exp)
                VE.tt(heads(K1[:, :], 4), heads(K1[:, :], 4), ka[:, :, 0:128], MUL, a)
                a = VE.tt(heads(Q1[:, :], 4), heads(Q1[:, :], 4), qa[:, :, 128:256], MUL)
                b = B.take()
                for hd in range(4):
                    hc = slice(hd * 128, hd * 128 + 128)
                    tp = PE.tr(b.ap[:, hc], K1[:, hc], ident, [a, b.free], sig=hd == 3)
                a = AC.act(KT[:, :], b.ap, ACT.Copy, after=tp)
                b.done(a)
                b = B.take()
                for hd in range(4):
                    hc = slice(hd * 128, hd * 128 + 128)
                    tp = PE.mm(b.ap[:, hc], KT[:, hc], ia[:, 0, hc], True, True, [a, b.free], sig=hd == 3)
                ts0 = AC.act(S0[:, :], b.ap, ACT.Copy, after=tp)
                b.done(ts0)
                O = sb("OE", [128, 2, 512], c=ph)
                for t in range(2):
                    b = B.take()
                    for hd in range(4):
                        hc = slice(hd * 128, hd * 128 + 128)
                        tp = PE.mm(b.ap[:, hc], SC[:, t, hc], ia[:, t, hc], True, t == 0, [tsc, ts0, b.free], sig=True)
                        if t == 1:
                            tp = PE.mm(b.ap[:, hc], Q1[:, hc], S0[:, hc], False, True, sig=True)
                    tg = head_norm(b, tp, ga[:, t, :], O[:, t, :], 4, XN[:, 0, 0:512], 44 + 4 * t)
                ZS = sb("ZS", [128, 4, 384], c=ph)
                LK = XN[:, :, :].rearrange("p a d -> p (a d)")[:, 0:1536].rearrange("p (h t) -> p h t", h=4)
                for hd in range(4):
                    b = B.take()
                    PE.mm(b.ap[:, 0:256], kb[:, hd, 0:128], qb[:, hd, :], True, True, [tg, b.free])
                    tp = PE.mm(b.ap[:, 256:384], kb[:, hd, 128:256], qb[:, hd, 128:256], True, True, sig=True)
                    a = AC.act(ZS[:, hd, :], b.ap[:, 0:384], ACT.Copy, after=tp)
                    b.done(a)
                AC.act(fl(LK), fl(ZS), ACT.Abs)
                AC.act(fl(LK), fl(LK), ACT.Exp, scale=-1.0)
                a = AC.act(fl(LK), fl(LK), ACT.Ln, bias=1.0)
                a = VE.stt(fl(LK), fl(ZS), 0.0, fl(LK), MAX, ADD, a)
                a = VE.ts(fl(LK), fl(LK), -1.0, MUL)
                for c0 in (0, 256):
                    tl = VE.tt(LK[:, :, c0:c0 + 128], LK[:, :, c0:c0 + 128], bc(C("SU"), 4), MUL)
                for hd in range(4):
                    b = B.take()
                    PE.mm(b.ap[:, 0:256], C("LF"), LK[:, hd, 0:256], True, False, [tl, b.free])
                    PE.mm(b.ap[:, 128:256], ones, LK[:, hd, 256:384], False, True)
                    tp = PE.mm(b.ap[:, 256:384], C("LF"), LK[:, hd, 256:384], True, True, sig=True)
                    a = VE.tt(ZS[:, hd, :], ZS[:, hd, :], b.ap[:, 0:384], ADD, tp)
                    b.done(a)
                for c0 in (0, 256):
                    a = VE.tt(ZS[:, :, c0:c0 + 128], ZS[:, :, c0:c0 + 128], bc(C("NM"), 4), ADD)
                tz = AC.act(fl(ZS), fl(ZS), ACT.Exp, after=a)
                OT = HT
                for hd in range(4):
                    hc = slice(hd * 128, hd * 128 + 128)
                    b = B.take()
                    PE.mm(b.ap[:, 0:256], vb[:, 0, hc], ZS[:, hd, 0:256], True, False, [tz, b.free])
                    tp = PE.mm(b.ap[:, 128:256], vb[:, 1, hc], ZS[:, hd, 256:384], False, True, sig=True)
                    to = AC.act(OT[:, 4 + hd, :], b.ap[:, 0:256], ACT.Copy, after=tp)
                    b.done(to)
                tf = to_features(lambda t, k: O[:, t, k * 128:(k + 1) * 128], OT,
                                 lambda k: V("hgrn_norm_g_3", k), lambda k: None, tg, 4)
                out_proj([(T["even_w_out_3"][0], 0, 8)], OT, [tf, to], add_gated(3, XN, growtok))
            barrier()

        def odd(modtok, growtok):
            wi = T["odd_w_in_3"][0]
            with ExitStack() as ph:
                XN = sb("XO3", [128, 2, D], c=ph)
                HT = sb("HO3", [128, 8, 256], c=ph)
                h = norm_mod(XN, HT, 5, modtok, None)
                CO = sb("COo", [128, 8, 256], c=ph)
                CI = sb("CIo", [128, 4, 260], c=ph)
                VX = sb("VX", [128, 2, 8, 129], c=ph)
                OG = sb("OG", [128, 2, D], c=ph)
                E8 = sb("E8", [8, 6, 256], c=ph)
                GBI = sb("GBI", [8, 2], c=ph)
                CCM = sb("CCM", [128, 2, 16], c=ph)
                lg = loads("gateb")
                gsrc = T["odd_gate_b_3"].rearrange("a (g p) -> (a g) p", p=8)
                for g in range(2):
                    lg.go(PO, GBI[:, g:g + 1], gsrc[g, :].rearrange("(p o) -> p o", o=1))
                z = VE.mset(CI[:, :, 0:3], 0.0)
                z = VE.mset(VX[:, :, :, 128:129], 1.0)
                z = VE.mset(E8[:, 5, :], 1.0)
                w = wtile(wi, 3072, 16)
                b = B.take()
                for g in range(2):
                    tp = PE.mms(b.ap[0:8, 256 * g:256 * g + 256],
                                [(w.ap[:, k, 8 * g:8 * g + 8], HT[:, k, :]) for k in range(8)], [w.tok, b.free, h])
                w.done(tp)
                ig, lf, bs_, cm, nm, one = (E8[:, i, :] for i in range(6))
                VE.ts(ig, b.ap[0:8, 0:256], GBI[:, 0:1], ADD, after=[tp, lg.tok])
                a = VE.ts(lf, b.ap[0:8, 256:512], GBI[:, 1:2], ADD)
                b.done(a)
                a = AC.act(bs_, lf, ACT.Abs, after=a)
                a = AC.act(bs_, bs_, ACT.Exp, scale=-1.0)
                a = AC.act(bs_, bs_, ACT.Ln, bias=1.0)
                VE.stt(lf, lf, 0.0, bs_, MIN, SUB, a)
                VE.scan(bs_, one, lf, 0.0, MUL, ADD)
                VE.tt(ig, ig, bs_, SUB)
                VE.scan(cm, one, ig, 0.0, MUL, MAX)
                a = VE.stt(nm, bs_, -1.0, cm, MUL, SUB)
                b = B.take()
                for t in range(2):
                    tk = slice(t * 128, t * 128 + 128)
                    PE.tr(b.ap[:, 16 * t:16 * t + 8], ig[:, tk], ident[0:8, 0:8], [a, b.free])
                    tp = PE.tr(b.ap[:, 16 * t + 8:16 * t + 16], nm[:, tk], ident[0:8, 0:8], sig=True)
                a = VE.cp(CCM[:, :, :], b.ap[:, 0:32].rearrange("p (t c) -> p t c", t=2), tp)
                b.done(a)
                tcm = AC.act(CCM[:, :, 8:16], CCM[:, :, 8:16], ACT.Exp, after=a)
                ct = None
                for g in range(2):
                    feats(wtile(wi, 512 * g, 512), 4, HT, h,
                          lambda j, p, tp: AC.act(CI[:, j, 3:259], p, ACT.Copy, after=[tp, ct, z]))
                    a = AC.last
                    for j in range(4):
                        f = 4 * g + j
                        VE.ts(CO[:, f, :], CI[:, j, 0:256], V("odd_conv_w_3", f), MUL, V("odd_conv_b_3", f), ADD, a)
                        for k in range(1, 4):
                            ct = VE.stt(CO[:, f, :], CI[:, j, k:k + 256], V("odd_conv_w_3", 8 * k + f), CO[:, f, :], MUL, ADD)
                    cof = CO[:, 4 * g:4 * g + 4, :].rearrange("p j t -> p (j t)")
                    tco = AC.act(cof, cof, ACT.Silu, after=ct)
                for hf in range(2):
                    bytoks(wtile(wi, 1024 + 512 * hf, 512), 0, 512, HT, h,
                           lambda t, p, tp: AC.act(VX[:, t, 4 * hf:4 * hf + 4, 0:128], heads(p, 4), ACT.Copy, after=[tp, z]))
                tv = AC.last
                for hf in range(2):
                    bytoks(wtile(wi, 2048 + 512 * hf, 512), 0, 512, HT, h,
                           lambda t, p, tp: AC.act(OG[:, t, 512 * hf:512 * hf + 512], p, ACT.Sigmoid, after=tp))
                O = sb("OO", [128, 2, D], c=ph)
                W = sb("WO", [128, 4, 384], c=ph)
                dn = sb("dn", [128, 8], c=ph)
                fw = None
                for g in range(2):
                    for i in range(4):
                        hd = 4 * g + i
                        b = B.take()
                        tp = PE.mm(b.ap[:, 0:256], SEL[0:8, hd * 128:hd * 128 + 128], cm, True, True, [tcm, b.free], sig=True)
                        VE.ts(W[:, i, 0:256], b.ap[:, 0:256], CCM[:, 0, hd:hd + 1], SUB, 0.0, MAX, [tp, fw])
                        a = VE.ts(W[:, i, 256:384], b.ap[:, 128:256], CCM[:, 1, hd:hd + 1], SUB, 0.0, MAX)
                        b.done(a)
                    wf = W[:, :, :].rearrange("p i t -> p (i t)")
                    a = AC.act(wf, wf, ACT.Exp, scale=-1.0, after=a)
                    for c0 in (0, 256):
                        te = VE.tt(W[:, :, c0:c0 + 128], W[:, :, c0:c0 + 128], bc(C("UF"), 4), MUL, a)
                    for i in (0, 2, 1, 3):
                        hd = 4 * g + i
                        hp = slice(64 * (hd % 2), 64 * (hd % 2) + 64)
                        b = B.take()
                        PE.mm(b.ap[:, 0:256], CO[hp, 4 + hd // 2, 0:128], CO[hp, hd // 2, :], True, True, [tco, b.free])
                        tp = PE.mm(b.ap[:, 256:384], CO[hp, 4 + hd // 2, 128:256], CO[hp, hd // 2, 128:256], True, True, sig=True)
                        tw = VE.stt(W[:, i, :], b.ap[:, 0:384], 0.125, W[:, i, :], MUL, MUL, [tp, te])
                        b.done(tw)
                    for t in range(2):
                        for i in range(0, 4, 2):
                            b = B.take()
                            for j in range(2):
                                hd = 4 * g + i + j
                                o = b.ap[:, 129 * j:129 * j + 129]
                                prs = [(W[:, i + j, t * 128:t * 128 + 128], VX[:, 0, hd, :])]
                                if t:
                                    prs.append((W[:, i + j, 256:384], VX[:, 1, hd, :]))
                                tp = PE.mms(o, prs, [tw, tv, b.free])
                            h0 = 4 * g + i
                            bv = b.ap[:, 0:258].rearrange("p (j c) -> p j c", j=2)
                            a = AC.act(dn[:, 0:2], bv[:, :, 128], ACT.Abs, after=[tp, VE.last])
                            VE.tt(dn[:, 0:2], dn[:, 0:2], CCM[:, t, 8 + h0:8 + h0 + 2], MAX, a)
                            VE.rec(dn[:, 0:2], dn[:, 0:2])
                            a = VE.tt(heads(O[:, t, h0 * 128:h0 * 128 + 256], 2), bv[:, :, 0:128], ex(dn[:, 0:2], 128), MUL)
                            b.done(a)
                    fw = tp
                for t in range(2):
                    v = Bank(B, 0, O[:, t, :], None)
                    v.done = lambda *x: None
                    tg = head_norm(v, VE.last, OG[:, t, :], O[:, t, :], 8, XN[:, 0, :], 44 + 8 * t)
                OT = HT
                tf = to_features(lambda t, k: O[:, t, k * 128:(k + 1) * 128], OT,
                                 lambda k: V("odd_norm_g_3", k), lambda k: None, [tg, PE.last])
                out_proj([(T["odd_w_out_3"][0], 0, 8)], OT, tf, add_gated(0, XN, growtok))
            barrier()

        def third():
            bgon[0] = True
            even(need(mods[3]), lambda: need(rows[3]))
            ffn(0, 4, 4, need(mods[4]), lambda: need(rows[4]))
            odd(need(mods[5]), lambda: need(rows[5]))
            ffn(1, 6, 1, need(mods[6]), lambda: need(rows[6]))
            lf = loads("final")
            lf.go(PO, GB[:, :], T["final_g_3"].rearrange("(a d) -> a d", a=1).broadcast_to([128, D]))
            with ExitStack() as ph:
                SQ = sb("SQF", [128, D], c=ph)
                t = rstd(lambda i: X[:, i, :], 2, D, SQ[:, :], st[:, 0:2], None)
                for i in range(2):
                    VE.stt(X[:, i, :], X[:, i, :], st[:, i:i + 1], GB[:, :], MUL, MUL, [t, lf.tok])
            barrier()

        a2, b2_, a3, b3 = T["w_ada_2"][0], T["b_ada_2"], T["ada_w_3"], T["ada_b_3"]
        v2, v3 = vat["b_ada_2"], vat["ada_b_3"]
        wm = T["w_mod"][0]
        mods = {0: AdaCols(wm, 0, 0, vat["b_mod"], vat["g_pre_mix"], 0),
                1: AdaCols(wm, 3072, 0, vat["b_mod"] + 24, vat["g_pre_ffn"], 1),
                2: AdaCols(a2, 0, 8, v2, vat["g_pre_2"], 2)}
        rows = {0: AdaRow(wm, 2048, 0, T["b_mod"][:, 2048:3072], T["g_post_mix"], 0),
                1: AdaRow(T["w_mod"][0], 5120, 0, T["b_mod"][:, 5120:6144], T["g_post_ffn"], 1),
                2: AdaRow(a2, 2048, 8, b2_[:, 2048:3072], T["g_post_2"], 2)}
        for l in range(2):
            nm, nf = vat["norm_mix_g_3"] + 8 * l, vat["norm_ffn_g_3"] + 8 * l
            mods[3 + 2 * l] = AdaCols(a3[l], 0, 16, v3 + 48 * l, nm, 3 + 2 * l)
            mods[4 + 2 * l] = AdaCols(a3[l], 3072, 16, v3 + 48 * l + 24, nf, 4 + 2 * l)
            rows[3 + 2 * l] = AdaRow(a3[l], 2048, 16, b3[l:l + 1, 2048:3072], None, 3 if l == 0 else 0)
            rows[4 + 2 * l] = AdaRow(a3[l], 5120, 16, b3[l:l + 1, 5120:6144], None, 4 if l == 0 else 1)
        order = {"1": [mods[0], rows[0], mods[1], rows[1]], "2": [mods[2], rows[2]],
                 "3": [mods[3], rows[3], mods[4], rows[4], mods[5], rows[5], mods[6], rows[6]]}
        for p in parts:
            pending += [(o, j) for o in order[p] for j in range(o.n)]
        for p in parts:
            if p == "1":
                first()
            if p == "2":
                second()
            if p == "3":
                third()

        lo = loads("out")
        lo.go(AC, out.rearrange("a (t p) d -> p (a t) d", p=128), X[:, :, :], [VE.last])
        AC.raw(lambda e, seen, outer: e.wait_ge(lo.sem, lo.n))

        with nc.Block() as block:
            @block.tensor
            def _(eng):
                PE.emit(eng)

            @block.scalar
            def _(eng):
                AC.emit(eng)

            @block.vector
            def _(eng):
                VE.emit(eng)

            @block.gpsimd
            def _(eng):
                PO.emit(eng)

            @block.sync
            def _(eng):
                SP.emit(eng)


def make(nc, shapes, parts="123", flip=False):
    T = {}
    for name, shape in shapes.items():
        T[name] = nc.dram_tensor(f"in_{name}", shape, F32, kind="ExternalInput").ap()
    out = nc.dram_tensor("out_0", (1, 256, 1024), F32, kind="ExternalOutput").ap()
    build(nc, T, out, parts, flip)


def kernel(**inputs):
    import concourse.bacc as bacc
    from concourse.bass_utils import run_bass_kernel_spmd as run
    arrays = {}
    for name, a in inputs.items():
        arrays[name] = np.ascontiguousarray(a)
    arrays["consts"] = const_table()[1]
    arrays["sel"] = sel_table()
    nc = bacc.Bacc("TRN2", target_bir_lowering=False, num_devices=1)
    make(nc, {n: a.shape for n, a in arrays.items()})
    r = run(nc, [{f"in_{n}": a for n, a in arrays.items()}], core_ids=[0])
    return r.results[0]["out_0"]
```

```python
from contextlib import ExitStack

import numpy as np

import concourse.bass as bass
from concourse import mybir

ALU = mybir.AluOpType
ACT = mybir.ActivationFunctionType
F32 = mybir.dt.float32
U32 = mybir.dt.uint32
I32 = mybir.dt.int32
AX = mybir.AxisListType
ADD, SUB, MUL, MAX, MIN = ALU.add, ALU.subtract, ALU.mult, ALU.max, ALU.min

D = 1024
EPS = 1e-6
NEG = -1e30
E_N = 32
FFN = 2816
FT = FFN // 128



def const_table():
    p = np.arange(128)[:, None]
    f = np.arange(128)[None, :]
    same = (p // 64) == (f // 64)
    c = {}
    c["ident"] = p == f
    c["ones"] = np.ones((128, 128))
    c["U64"] = (p <= f) & same
    c["SU64"] = (p < f) & same
    c["UF"] = p <= f
    c["LF"] = p >= f
    c["SU"] = p < f
    c["B64"] = same
    c["NM"] = np.where(p < f, 0.0, NEG)
    for L in (1, 2, 4, 8, 16, 32, 64):
        c[f"H{L}"] = (p // (2 * L) == f // (2 * L)) & (p % (2 * L) < L) & (f % (2 * L) >= L)
    k = np.arange(256)[None, :]
    for t in (0, 1):
        d = (t * 128 + p) - k
        n = (d <= 128) * 1 + (d % 4 == 0) * 1 + (d % 16 == 0) * 1
        dil = np.where((d >= 0) & (n > 0), np.log(np.maximum(n, 1)), NEG)
        cau = np.where(d >= 0, 0.0, NEG)
        c[f"AB{t}"] = dil[:, :128 * (t + 1)]
        c[f"CB{t}"] = cau[:, :128 * (t + 1)]
    half = 32
    inv = (np.float32(10000.0) ** (-np.arange(half, dtype=np.float32) / np.float32(half))).astype(np.float32)
    ang = (np.arange(256, dtype=np.float32)[:, None] * inv[None, :]).astype(np.float32)
    for n, v in (("cos", np.cos(ang)), ("sin", np.sin(ang))):
        v = v.reshape(2, 128, half).transpose(1, 0, 2).reshape(128, 64)
        c[n] = v
        c[n + "q"] = v * 0.125
    c["iota"] = np.broadcast_to(np.arange(128)[None, :], (128, 128))
    t = np.arange(256)[None, :]
    c["R64"] = np.broadcast_to((t % 64 != 0), (128, 256))
    c["R128"] = np.broadcast_to((t % 128 != 0), (128, 256))
    at, cols, n = {}, [], 0
    for name, v in c.items():
        v = np.ascontiguousarray(v, dtype=np.float32)
        at[name] = (n, n + v.shape[1])
        n += v.shape[1]
        cols.append(v)
    return at, np.concatenate(cols, axis=1)


def sel_table():
    s = np.zeros((8, 8, 128), np.float32)
    for h in range(8):
        s[h, h, :] = 1.0
    return s.reshape(8, 1024)


VECS = [("c", 8), ("c_2", 8), ("c_3", 8), ("g_pre_mix", 8), ("g_pre_ffn", 8), ("g_pre_2", 8),
        ("norm_mix_g_3", 16), ("norm_ffn_g_3", 16), ("b_mod", 48), ("b_ada_2", 24), ("ada_b_3", 96),
        ("b_gate", 2), ("g_gla", 1), ("dn_norm_g_2", 1), ("hgrn_norm_g_3", 4), ("odd_norm_g_3", 8),
        ("conv_w_2", 48), ("odd_conv_w_3", 32), ("odd_conv_b_3", 8), ("ffn_conv_w_3", 132), ("ffn_conv_b_3", 44)]




def flat(x, out):
    if x is None:
        return out
    if isinstance(x, tuple):
        out.append(x)
    else:
        for y in x:
            flat(y, out)
    return out


class Queue:

    def __init__(self, sem, chain):
        self.sem, self.n, self.ops, self.pend, self.chain = sem, 0, [], [], chain

    @property
    def last(self):
        return (self.sem, self.n)

    def do(self, fn, after=None, sig=True):
        waits = flat(after, list(self.pend))
        if self.chain and self.n:
            waits.append(self.last)
        self.pend = []
        if sig:
            self.n += 1
        self.ops.append((waits, fn, (self.sem, 1) if sig else None))
        return self.last if sig else None

    def dma(self, out, in_, sem, after=None):
        waits = flat(after, list(self.pend))
        self.pend = []
        self.ops.append((waits, lambda e: e.dma_start(out, in_), (sem, 16)))

    def raw(self, fn):
        self.ops.append((None, fn, None))

    def emit(self, eng):
        seen = {}
        outer = None
        for waits, fn, inc in self.ops:
            if waits is None:
                outer = fn(eng, seen, outer)
                continue
            for sem, val in waits:
                if seen.get(sem.name, 0) < val:
                    eng.wait_ge(sem, val)
                    seen[sem.name] = val
            ins = fn(eng)
            if inc:
                ins.then_inc(inc[0], inc[1])

    def tt(self, out, a, b, op, after=None):
        return self.do(lambda e: e.tensor_tensor(out, a, b, op), after)

    def ts(self, out, a, s1, op0, s2=None, op1=None, after=None):
        if op1 is None:
            return self.do(lambda e: e.tensor_scalar(out, a, s1, None, op0), after)
        return self.do(lambda e: e.tensor_scalar(out, a, s1, s2, op0, op1), after)

    def stt(self, out, a, s, b, op0, op1, after=None):
        return self.do(lambda e: e.scalar_tensor_tensor(out=out, in0=a, scalar=s, in1=b, op0=op0, op1=op1), after)

    def ttr(self, out, a, b, op0, op1, init, acc, after=None):
        return self.do(lambda e: e.tensor_tensor_reduce(out, a, b, 1.0, init, op0, op1, acc), after)

    def cp(self, out, a, after=None):
        return self.do(lambda e: e.tensor_copy(out, a), after)

    def red(self, out, a, op, after=None):
        return self.do(lambda e: e.tensor_reduce(out, a, AX.X, op), after)

    def rec(self, out, a, after=None):
        return self.do(lambda e: e.reciprocal(out, a), after)

    def scan(self, out, a, b, init, op0, op1, after=None):
        return self.do(lambda e: e.tensor_tensor_scan(out, a, b, init, op0, op1), after)

    def cpred(self, out, mask, data, after=None):
        return self.do(lambda e: e.copy_predicated(out, mask, data), after)

    def mset(self, out, v, after=None):
        return self.do(lambda e: e.memset(out, v), after)

    def act(self, out, a, func, bias=None, scale=None, acc=None, after=None):
        kw = {}
        if bias is not None:
            kw["bias"] = bias
        if scale is not None:
            kw["scale"] = scale
        if acc is not None:
            kw["accum_out"] = acc
        return self.do(lambda e: e.activation(out, a, func, **kw), after)

    def mm(self, out, lhsT, rhs, start, stop, after=None, sig=False):
        return self.do(lambda e: e.matmul(out, lhsT, rhs, start=start, stop=stop, skip_group_check=True), after, sig)

    def mms(self, out, pairs, after=None, sig=True, start=True, stop=True):
        n = len(pairs)
        tok = None
        for i, (a, b) in enumerate(pairs):
            tok = self.mm(out, a, b, start and i == 0, stop and i == n - 1, after if i == 0 else None,
                          sig and i == n - 1)
        return tok

    def tr(self, out, in_, ident, after=None, sig=False):
        return self.do(lambda e: e.transpose(out, in_, ident), after, sig)


class Banks:

    def __init__(self, ps):
        self.ps, self.k, self.free = ps, 0, [None] * 8

    def take(self):
        while self.free[self.k % 8] is False:
            self.k += 1
        i = self.k % 8
        self.k += 1
        f, self.free[i] = self.free[i], False
        return Bank(self, i, self.ps[:, i, :], f)


class Bank:
    def __init__(self, banks, i, ap, free):
        self.banks, self.i, self.ap, self.free = banks, i, ap, free

    def done(self, *toks):
        self.banks.free[self.i] = list(toks)


class Loads:

    def __init__(self, sem):
        self.sem, self.n = sem, 0

    def go(self, q, out, in_, after=None):
        q.dma(out, in_, self.sem, after)
        self.n += 16

    @property
    def tok(self):
        return (self.sem, self.n)


class Weights:

    def __init__(self, q, tiles, sems):
        self.q, self.tiles, self.sems = q, tiles, sems
        self.k, self.uses = 0, [0] * len(tiles)
        self.free = [None] * len(tiles)

    def load(self, src, kc, n):
        i = self.k % len(self.tiles)
        self.k += 1
        assert self.uses[i] == 0 or self.free[i] is not None
        ap = self.tiles[i][:, 0:kc * n].rearrange("p (k n) -> p k n", k=kc)
        self.q.dma(ap, src, self.sems[i], self.free[i])
        self.uses[i] += 1
        self.free[i] = None
        return Tile(self, i, ap, (self.sems[i], 16 * self.uses[i]))


class Tile:
    def __init__(self, ring, i, ap, tok):
        self.ring, self.i, self.ap, self.tok = ring, i, ap, tok

    def done(self, *toks):
        self.ring.free[self.i] = list(toks)


def build(nc, T, out, parts="123", flip=False):
    at, _ = const_table()
    vat, n = {}, 0
    for name, r in VECS:
        vat[name] = n
        n += r
    NV = -(-n // 128)
    ctx = ExitStack()
    with ctx:
        def sem(name):
            return ctx.enter_context(nc.semaphore(name))

        nsb = [0]

        def sb(name, shape, dt=F32, c=None):
            nsb[0] += 1
            return (c or ctx).enter_context(nc.sbuf_tensor(f"{name}_{nsb[0]}", shape, dt))

        PE, AC, VE, PO, SP = (
            Queue(sem(f"s_{x}"), x in ("act", "dve", "pool")) for x in ("pe", "act", "dve", "pool", "sp"))
        ps = ctx.enter_context(nc.psum_tensor("ps", [128, 8, 512], F32))
        B = Banks(ps)
        NS = 4
        SLOT = 8 * 520
        ring = Weights(SP, [sb(f"w{i}", [128, SLOT]) for i in range(NS)], [sem(f"s_w{i}") for i in range(NS)])

        CT = sb("CT", [128, max(b for _, b in at.values())])
        SEL = sb("SEL", [8, 1024])
        VT = sb("VT", [128, NV * 128])
        CS = sb("CS", [128, 24])
        EPSC = sb("EPSC", [128, 1])
        X = sb("X", [128, 2, D])
        MOD = sb("MOD", [128, 14, 8])
        GR = sb("GR", [128, 5, D])
        AC2 = sb("AC2", [128, 4, 512])
        ROW = sb("ROW", [1, D])
        GB = sb("GB", [128, D])
        st = sb("st", [128, 64])

        def C(name, a=0, b=None):
            lo, hi = at[name]
            return CT[:, lo + a:(hi if b is None else lo + b)]

        def V(name, j=0, k=1):
            return VT[:, vat[name] + j:vat[name] + j + k]

        ident = C("ident")
        ones = C("ones")

        def barrier():
            toks = [q.last for q in (PE, AC, VE, PO) if q.n]
            for q in (PE, AC, VE, PO):
                q.pend = q.pend + toks

        nsem = [0]

        def loads(name):
            nsem[0] += 1
            return Loads(sem(f"s_l{nsem[0]}_{name}"))

        VR = GR[:, 4, 0:NV * 128].rearrange("p (n q) -> p n q", n=NV)
        VC = GR[0:24, 4, NV * 128:NV * 128 + 128]
        l1, l2, lx = loads("first"), loads("rest"), loads("x")
        lv = [loads("vecs"), loads("vecs2")]
        l1.go(AC, CT[:, 0:256], T["consts"][:, 0:256])
        for i, name in enumerate(("c", "c_2", "c_3")):
            l1.go(AC, VC[8 * i:8 * i + 8, :], T[name].rearrange("a (r q) -> (a r) q", q=128))
        VR0 = VE.mset(VR[:, NV - 1, :], 0.0)
        SP.pend = [l1.tok]
        ready = [VE.mset(EPSC[:, :], EPS)]
        lx.go(PO, X[:, :, :], T["x"].rearrange("a (t p) d -> p (a t) d", p=128))
        for i, (name, r) in enumerate(VECS):
            a = T[name]
            names = " ".join(f"a{i}" for i in range(len(a.shape)))
            src = a.rearrange(f"{names} -> ({names})").rearrange("(r q) -> r q", q=128)
            done = 0
            while done < r:
                g = vat[name] + done
                k = min(r - done, 128 - g % 128)
                lv[i % 2].go((AC, PO)[i % 2], VR[g % 128:g % 128 + k, g // 128, :], src[done:done + k, :],
                      VR0 if g // 128 == NV - 1 else None)
                done += k
        l2.go(AC, CT[:, 256:], T["consts"][:, 256:])
        l2.go(AC, SEL[:, :], T["sel"])
        b = B.take()
        tp = PE.tr(b.ap[:, 0:24], VC, ident[0:24, 0:24], l1.tok, sig=True)
        tcs = AC.act(CS[:, :], b.ap[:, 0:24], ACT.Silu, after=tp)
        b.done(tcs)

        def vectors():
            for i in range(0, NV, 4):
                b = B.take()
                m = min(4, NV - i)
                for j in range(m):
                    tp = PE.tr(b.ap[:, j * 128:j * 128 + 128], VR[:, i + j, :], ident, [lv[0].tok, lv[1].tok, VR0, b.free], sig=True)
                t = AC.act(VT[:, i * 128:(i + m) * 128], b.ap[:, 0:m * 128], ACT.Copy, after=tp)
                b.done(t)
            ready.append(t)

        accfree = [None, None]
        nacc = [0]

        def ada_acc(src, c0, ccol):
            i = nacc[0] % 2
            nacc[0] += 1
            w = ring.load(src[:, c0:c0 + 512].rearrange("(k p) n -> p k n", p=128), 8, 512)
            toks = [None, None]
            for k in range(8):
                acc = AC2[:, 2 * i + k % 2, :]
                if k < 2:
                    toks[k] = VE.ts(acc, w.ap[:, k, :], CS[:, ccol + k:ccol + k + 1], MUL,
                                    after=[w.tok, accfree[i], tcs])
                else:
                    toks[k % 2] = VE.stt(acc, w.ap[:, k, :], CS[:, ccol + k:ccol + k + 1], acc, MUL, ADD,
                                         after=[toks[k % 2]])
            w.done(toks[1])
            return i, VE.tt(AC2[:, 2 * i, :], AC2[:, 2 * i, :], AC2[:, 2 * i + 1, :], ADD, toks)

        class AdaCols:
            n = 4

            def __init__(self, src, c0, ccol, bias, g, slot):
                self.a = (src, c0, ccol, bias, g, slot)
                self.tok = []

            def start(self, j):
                return ada_acc(self.a[0], self.a[1] + 512 * j, self.a[2])

            def finish(self, j, i, toks):
                src, c0, ccol, bias, g, slot = self.a
                b = B.take()
                for f in range(4):
                    tp = PE.mm(b.ap[:, f:f + 1], AC2[:, 2 * i, f * 128:(f + 1) * 128], ones[:, 0:1], True, True,
                               [toks, b.free], sig=f == 3)
                accfree[i] = tp
                o = MOD[:, 2 * slot + j // 2, 4 * (j % 2):4 * (j % 2) + 4]
                bv = VT[:, bias + 4 * j:bias + 4 * j + 4]
                if j < 2:
                    t = VE.tt(o, b.ap[:, 0:4], bv, ADD, [tp, ready])
                    b.done(t)
                else:
                    t = VE.stt(o, b.ap[:, 0:4], 1.0, bv, ADD, ADD, [tp, ready])
                    b.done(t)
                    t = VE.tt(o, o, VT[:, g + 4 * (j - 2):g + 4 * (j - 2) + 4], MUL, t)
                self.tok.append(t)

        rowfree = [None]
        gbfree = [None]

        class AdaRow:
            n = 2

            def __init__(self, src, c0, ccol, bias, gpost, slot):
                self.a = (src, c0, ccol, bias, gpost, slot)
                self.tok = []

            def start(self, j):
                src, c0, ccol, bias, gpost, slot = self.a
                if j == 0:
                    self.l = loads("row")
                    self.l.go(PO, ROW[0:1, :], bias, rowfree[0])
                    if gpost is not None:
                        self.l.go(PO, GB[:, :], gpost.broadcast_to([128, D]), gbfree[0])
                return ada_acc(src, c0 + 512 * j, ccol)

            def finish(self, j, i, toks):
                src, c0, ccol, bias, gpost, slot = self.a
                b = B.take()
                PE.mm(b.ap, ones, AC2[:, 2 * i, :], True, False, [toks, b.free])
                tp = PE.mm(b.ap, ones[0:1, :], ROW[0:1, 512 * j:512 * j + 512], False, True, self.l.tok, sig=True)
                accfree[i] = rowfree[0] = tp
                o = GR[:, slot, 512 * j:512 * j + 512]
                if gpost is not None:
                    t = VE.tt(o, b.ap, GB[:, 512 * j:512 * j + 512], MUL, [tp, self.l.tok])
                    gbfree[0] = t
                else:
                    t = VE.cp(o, b.ap, tp)
                b.done(t)
                self.tok.append(t)

        pending, inflight, bgon = [], [], [False]

        def settle():
            for o, j, i, toks in inflight:
                o.finish(j, i, toks)
            inflight.clear()

        def background(n=1):
            for _ in range(n):
                if not pending or (isinstance(pending[0][0], AdaRow) and pending[0][1] == 0):
                    settle()
                if pending:
                    o, j = pending.pop(0)
                    i, toks = o.start(j)
                    settle()
                    inflight.append((o, j, i, toks))

        def need(o):
            while len(o.tok) < o.n:
                if any(p is o for p, _ in pending):
                    background(1)
                else:
                    settle()
            return o.tok

        def rstd(ins, n, width, scratch, dst, after):
            for i in range(n):
                t = AC.act(scratch, ins(i), ACT.Square, acc=st[:, 32 + i:33 + i], after=[after])
            t = AC.act(st[:, 40:40 + n], st[:, 32:32 + n], ACT.Sqrt, bias=EPSC[:, :], scale=1.0 / width, after=t)
            return VE.rec(dst, st[:, 40:40 + n], t)

        def to_features(src, dst, scale, shift, after, ncols=8):
            toks = []
            for k in range(0, ncols, 2):
                b = B.take()
                m = min(2, ncols - k)
                for j in range(m):
                    for t in range(2):
                        tp = PE.tr(b.ap[:, j * 256 + t * 128:j * 256 + t * 128 + 128], src(t, k + j), ident,
                                   [after, b.free], sig=(j == m - 1 and t == 1))
                fr = []
                for j in range(m):
                    o, i_ = dst[:, k + j, :], b.ap[:, j * 256:j * 256 + 256]
                    s_, b_ = scale(k + j), shift(k + j)
                    dve = (k // 2) % 2
                    if s_ is None:
                        fr.append(VE.cp(o, i_, tp) if dve else AC.act(o, i_, ACT.Copy, after=tp))
                    elif b_ is None:
                        fr.append(VE.ts(o, i_, s_, MUL, after=tp) if dve else
                                  AC.act(o, i_, ACT.Copy, scale=s_, after=tp))
                    elif dve:
                        fr.append(VE.ts(o, i_, s_, MUL, b_, ADD, tp))
                    else:
                        fr.append(AC.act(o, i_, ACT.Identity, bias=b_, scale=s_, after=tp))
                b.done(*fr)
                toks += fr
            return toks

        def norm_mod(XN, HT, slot, modtok, after):
            t = rstd(lambda i: X[:, i, :], 2, D, XN[:, 0, :], st[:, 0:2], after)
            a = VE.ts(XN[:, 0, :], X[:, 0, :], st[:, 0:1], MUL, after=t)
            b = VE.ts(XN[:, 1, :], X[:, 1, :], st[:, 1:2], MUL)
            return to_features(lambda t_, k: XN[:, t_, k * 128:(k + 1) * 128], HT,
                               lambda k: MOD[:, 2 * slot + 1, k:k + 1], lambda k: MOD[:, 2 * slot, k:k + 1],
                               [a, b, modtok])

        def wtile(src, c0, n, r0=0, rows=1024):
            if bgon[0]:
                background(1)
            return ring.load(src[r0:r0 + rows, c0:c0 + n].rearrange("(k p) n -> p k n", p=128), rows // 128, n)

        def feat(w, c, m, HT, b, col, after):
            kc = w.ap.shape[1]
            return PE.mms(b.ap[0:m, col:col + 256], [(w.ap[:, k, c:c + m], HT[:, k, :]) for k in range(kc)],
                          [w.tok, b.free, after])

        def toks_(w, c, n, HT, t, b, col, after, start=True, stop=True, k0=0):
            kc = w.ap.shape[1]
            return PE.mms(b.ap[:, col:col + n],
                          [(HT[:, k0 + k, t * 128:(t + 1) * 128], w.ap[:, k, c:c + n]) for k in range(kc)],
                          [w.tok, b.free, after], start=start, stop=stop)

        def feats(w, ntile, HT, after, put):
            for j in range(0, ntile, 2):
                b = B.take()
                fr = []
                for i in range(min(2, ntile - j)):
                    tp = feat(w, (j + i) * 128, 128, HT, b, i * 256, after)
                for i in range(min(2, ntile - j)):
                    fr.append(put(j + i, b.ap[:, i * 256:i * 256 + 256], tp))
                b.done(*fr)
            w.done(tp)

        def bytoks(w, c, n, HT, after, put, done=True):
            for t in range(2):
                b = B.take()
                tp = toks_(w, c, n, HT, t, b, 0, after)
                b.done(put(t, b.ap[:, 0:n], tp))
            if done:
                w.done(tp)

        def out_proj(srcs, OT, after, put):
            for half in range(2):
                bs = [B.take(), B.take()]
                n = len(srcs)
                for s, (src, r0, kc) in enumerate(srcs):
                    w = wtile(src, half * 512, 512, r0, kc * 128)
                    for t in range(2):
                        tp = toks_(w, 0, 512, OT, t, bs[t], 0, after, start=s == 0, stop=s == n - 1, k0=r0 // 128)
                        if s == n - 1:
                            bs[t].tok = tp
                    w.done(tp)
                for t in range(2):
                    bs[t].done(put(t, half, bs[t].ap, bs[t].tok))

        pieces, read = [], []

        def fill(n=1):
            while read:
                read.pop(0)()
            for _ in range(min(n, len(pieces))):
                read.append(pieces.pop(0)())

        def fill_rest():
            while pieces or read:
                fill()

        def later(n, src, c0, products, put):
            ws = []

            def piece(j):
                if j == 0:
                    ws.append(ring.load(src[:, c0:c0 + 512].rearrange("(k p) n -> p k n", p=128), 8, 512))
                b = B.take()
                ap, tp = products(ws[0], j, b)
                if j == n - 1:
                    ws[0].done(tp)
                return lambda: b.done(put(j, ap, tp))
            pieces.extend(lambda j=j: piece(j) for j in range(n))

        def later_feats(src, c0, HT, after, put):
            def products(w, j, b):
                return b.ap[:, 0:256], feat(w, j * 128, 128, HT, b, 0, after)
            later(4, src, c0, products, put)

        def later_toks(src, c0, HT, after, put):
            def products(w, t, b):
                return b.ap, toks_(w, 0, 512, HT, t, b, 0, after)
            later(2, src, c0, products, put)

        def post_norm(Y, slot, after, scratch, modtok):
            t = rstd(lambda i: Y[:, i, :], 2, D, scratch, st[:, 2:4], after)
            for i in range(2):
                a = VE.stt(Y[:, i, :], Y[:, i, :], st[:, 2 + i:3 + i], GR[:, slot, :], MUL, MUL, [t, modtok])
                a = VE.tt(X[:, i, :], X[:, i, :], Y[:, i, :], ADD, a)
            return a

        def softmax_attn(ph, qT, kT, v, mask, O, after, PT=None):
            SB = sb("att_s", [128, 8, 384], c=ph)
            if PT is None:
                PT = sb("att_p", [128, 4, 256], c=ph)[:, :, :]
            pv = [None] * 4
            mx = sb("att_m", [128, 4, 8], c=ph)
            for t in range(2):
                nk = 128 * (t + 1)
                c0 = 0 if t == 0 else 128
                stok = {}
                for g in range(2):
                    bs = [B.take(), B.take()]
                    for par in range(2):
                        for i in range(2):
                            h = 4 * g + 2 * i + par
                            hp = 64 * par
                            stok[h] = PE.mm(bs[par].ap[:, i * 256:i * 256 + nk],
                                            qT[hp:hp + 64, h // 2, t * 128:t * 128 + 128],
                                            kT[hp:hp + 64, h // 2, 0:nk], True, True, [bs[par].free, after], sig=True)
                    mt = {}
                    sall = PE.last
                    for par in range(2):
                        for i in range(2):
                            h = 4 * g + 2 * i + par
                            mt[h] = VE.ttr(SB[:, h, c0:c0 + nk], bs[par].ap[:, i * 256:i * 256 + nk], mask(t), ADD, MAX,
                                           -3e38, mx[:, 0 + t, h:h + 1], sall)
                        bs[par].done(mt[4 * g + 2 + par])
                nt = VE.ts(mx[:, t, :], mx[:, t, :], -1.0, MUL, after=VE.last)
                fill()
                bo = B.take()
                for h in range(0, 8, 2):
                    b = B.take()
                    for i in range(2):
                        et = AC.act(SB[:, h + i, c0:c0 + nk], SB[:, h + i, c0:c0 + nk], ACT.Exp,
                                    bias=mx[:, t, h + i:h + i + 1], acc=mx[:, 2 + t, h + i:h + i + 1], after=nt)
                        for k in range(t + 1):
                            tp = PE.tr(b.ap[:, i * 256 + k * 128:i * 256 + k * 128 + 128],
                                       SB[:, h + i, c0 + k * 128:c0 + k * 128 + 128], ident, [et, b.free],
                                       sig=(i == 1 and k == t))
                    ct = VE.cp(PT[:, h % 4:h % 4 + 2, 0:nk],
                               b.ap.rearrange("p (i n) -> p i n", i=2)[:, :, 0:nk], [tp, pv[h % 4]])
                    b.done(ct)
                    fill()
                    for i in range(2):
                        tp = PE.mms(bo.ap[:, (h + i) * 64:(h + i) * 64 + 64],
                                    [(PT[:, (h + i) % 4, k * 128:k * 128 + 128], v[:, k, (h + i) * 64:(h + i) * 64 + 64])
                                     for k in range(t + 1)], [ct, bo.free])
                    pv[h % 4] = tp
                rt = VE.rec(mx[:, 2 + t, :], mx[:, 2 + t, :], et)
                ot = VE.tt(O(t).rearrange("p (h d) -> p h d", h=8), bo.ap.rearrange("p (h d) -> p h d", h=8),
                           mx[:, 2 + t, :].unsqueeze(2).broadcast_to([128, 8, 64]), MUL, [rt, tp])
                bo.done(ot)
            return ot

        def head_norm(b, tp, gate, O, nh, SQ, col):
            r = st[:, col:col + nh]
            a = AC.act(SQ, b.ap, ACT.Square, after=tp)
            a = VE.red(r, SQ.rearrange("p (h d) -> p h d", h=nh), ADD, a)
            a = AC.act(r, r, ACT.Sqrt, bias=EPSC[:, :], scale=1.0 / 128, after=a)
            a = VE.rec(r, r, a)
            a = VE.tt(O.rearrange("p (h d) -> p h d", h=nh), b.ap.rearrange("p (h d) -> p h d", h=nh),
                      r.unsqueeze(2).broadcast_to([128, nh, 128]), MUL, a)
            b.done(a)
            return VE.tt(O, O, gate, MUL, [a])

        def first():
            wi = T["w_in"][0]
            need(mods[0])
            bgon[0] = True
            with ExitStack() as ph:
                XN = sb("XN", [128, 2, D], c=ph)
                HT = sb("HT", [128, 8, 256], c=ph)
                h = norm_mod(XN, HT, 0, mods[0].tok, None)
                qT = sb("qT", [128, 4, 256], c=ph)
                kT = sb("kT", [128, 4, 256], c=ph)
                va = sb("va", [128, 2, 512], c=ph)
                R, tm = XN[:, :, 0:512], XN[:, :, 512:768]

                def rope(w, dst, cn, sn):
                    toks = []

                    def put(t, p, tp):
                        x = p.rearrange("p (h a d) -> p h a d", h=8, a=2)
                        o = R[:, t, :].rearrange("p (h a d) -> p h a d", h=8, a=2)
                        cs = C(cn, 32 * t, 32 * t + 32).unsqueeze(1).broadcast_to([128, 8, 32])
                        sn_ = C(sn, 32 * t, 32 * t + 32).unsqueeze(1).broadcast_to([128, 8, 32])
                        u = tm[:, t, :].rearrange("p (h d) -> p h d", h=8)
                        VE.tt(o[:, :, 0, :], x[:, :, 0, :], cs, MUL, tp)
                        a = VE.tt(u, x[:, :, 1, :], sn_, MUL)
                        a = VE.tt(o[:, :, 0, :], o[:, :, 0, :], u, SUB, a)
                        VE.tt(o[:, :, 1, :], x[:, :, 1, :], cs, MUL)
                        a = VE.tt(u, x[:, :, 0, :], sn_, MUL, a)
                        toks.append(VE.tt(o[:, :, 1, :], o[:, :, 1, :], u, ADD, a))
                        return a
                    bytoks(w, 0, 512, HT, h, put)
                    r = to_features(lambda t, k: R[:, t, k * 128:(k + 1) * 128], dst, lambda k: None, lambda k: None,
                                    toks, 4)
                    VE.pend = VE.pend + [PE.last]
                    return r

                tq = rope(wtile(wi, 0, 512), qT, "cosq", "sinq")
                tk = rope(wtile(wi, 512, 512), kT, "cos", "sin")
                bytoks(wtile(wi, 1024, 512), 0, 512, HT, h, lambda t, p, tp: AC.act(va[:, t, :], p, ACT.Copy, after=tp))
                tv = AC.last
                qg = sb("qg", [128, 2, 256], c=ph)
                kg = sb("kg", [128, 2, 256], c=ph)
                vg = sb("vg", [128, 2, 512], c=ph)
                rg = sb("rg", [128, 2, 512], c=ph)
                la = sb("la", [128, 2, 256], c=ph)
                bb = sb("bb", [128, 2, 256], c=ph)
                glr = sb("glr", [16, 256], c=ph)
                wlr = sb("wlr", [16, 256], c=ph)
                lw = loads("wlr")
                lw.go(PO, wlr[:, :], T["w_gate_lr"][0])

                def put_qk(j, p, tp):
                    if j < 2:
                        return AC.act(qg[:, j, :], p, ACT.Copy, scale=0.125, after=tp)
                    return AC.act(kg[:, j - 2, :], p, ACT.Copy, after=tp)
                feats(wtile(wi, 1536, 512), 4, HT, h, put_qk)
                later_toks(wi, 2048, HT, h, lambda t, p, tp: AC.act(vg[:, t, :], p, ACT.Copy, after=tp))
                later_toks(wi, 2560, HT, h, lambda t, p, tp: AC.act(rg[:, t, :], p, ACT.Copy, after=tp))
                w = wtile(wi, 3072, 16)
                b = B.take()
                tp = feat(w, 0, 16, HT, b, 0, h)
                w.done(tp)
                a = VE.cp(glr[:, :], b.ap[0:16, 0:256], tp)
                b.done(a)
                b = B.take()
                for j in range(2):
                    tp = PE.mm(b.ap[:, j * 256:j * 256 + 256], wlr[:, j * 128:j * 128 + 128], glr[:, :], True, True,
                               [a, lw.tok, b.free], sig=True)
                fr = [VE.ts(la[:, j, :], b.ap[:, j * 256:j * 256 + 256], V("b_gate", j), ADD, after=tp) for j in range(2)]
                b.done(*fr)
                laf, bbf = la[:, :, :].rearrange("p a t -> p (a t)"), bb[:, :, :].rearrange("p a t -> p (a t)")
                a = AC.act(bbf, laf, ACT.Abs, after=fr)
                a = AC.act(bbf, bbf, ACT.Exp, scale=-1.0, after=a)
                a = AC.act(bbf, bbf, ACT.Ln, bias=1.0, after=a)
                a = VE.stt(laf, laf, 0.0, bbf, MIN, SUB, a)
                for j in range(2):
                    a2 = VE.scan(bb[:, j, :], C("R64"), la[:, j, :], 0.0, MUL, ADD, a)
                qd = sb("qd", [128, 2, 256], c=ph)
                ki = sb("ki", [128, 2, 256], c=ph)
                ke = sb("ke", [128, 2, 256], c=ph)
                al = sb("al", [128, 2, 4], c=ph)
                qdf, kif, kef = (x[:, :, :].rearrange("p a t -> p (a t)") for x in (qd, ki, ke))
                qgf, kgf = (x[:, :, :].rearrange("p a t -> p (a t)") for x in (qg, kg))
                bl = bb[:, :, :].rearrange("p a (n c) -> p (a n) c", c=64)
                x1 = AC.act(qdf, bbf, ACT.Exp, scale=1.0 / 16, after=a2)
                x2 = AC.act(kif, bbf, ACT.Exp, scale=-1.0 / 16, after=a2)
                x3 = VE.tt(ke[:, :, :].rearrange("p a (n c) -> p (a n) c", c=64),
                           bl[:, :, 63:64].broadcast_to([128, 8, 64]), bl, SUB, a2)
                x4 = AC.act(kef, kef, ACT.Exp, scale=1.0 / 16, after=x3)
                x5 = AC.act(al[:, :, :].rearrange("p a n -> p (a n)"), bl[:, :, 63], ACT.Exp, scale=1.0 / 16, after=a2)
                x1 = VE.tt(qdf, qdf, qgf, MUL, [x1, AC.last])
                x2 = VE.tt(kif, kif, kgf, MUL, x2)
                x4 = VE.tt(kef, kef, kgf, MUL, x4)
                O = sb("O", [128, 2, D], c=ph)
                with ExitStack() as pa:
                    to = softmax_attn(pa, qT, kT, va, lambda t: C(f"AB{t}"), lambda t: O[:, t, 0:512], [tq, tk, tv])
                fill_rest()
                AC.act(rg[:, :, :], rg[:, :, :], ACT.Silu)
                barrier()
                keT = sb("keT", [128, 2, 256], c=ph)
                b = B.take()
                for j in range(2):
                    for t in range(2):
                        tp = PE.tr(b.ap[:, t * 256 + j * 128:t * 256 + j * 128 + 128], ke[:, j, t * 128:t * 128 + 128],
                                   ident, [x4, b.free], sig=True)
                a = AC.act(keT[:, :, :].rearrange("p a t -> p (a t)"), b.ap, ACT.Copy, after=tp)
                b.done(a)
                tke = a
                AT = sb("AT", [128, 8, 128], c=ph)
                z = VE.mset(AT[:, :, :], 0.0)
                att = []
                for t in range(2):
                    bs = [B.take(), B.take()]
                    for par in range(2):
                        for j in range(2):
                            hp = 64 * par
                            tp = PE.mm(bs[par].ap[:, j * 128:j * 128 + 128], ki[hp:hp + 64, j, t * 128:t * 128 + 128],
                                       qd[hp:hp + 64, j, t * 128:t * 128 + 128], True, True, [x1, x2, bs[par].free], sig=True)
                    for par in range(2):
                        for j in range(2):
                            a = VE.cpred(AT[:, t * 4 + 2 * j + par, :], C("U64").bitcast(U32),
                                         bs[par].ap[:, j * 128:j * 128 + 128], [z, tp])
                        bs[par].done(a)
                    att.append(a)
                S = sb("S", [128, 4, 2, 128], c=ph)
                sz = VE.mset(S[:, 0, :, :], 0.0)
                stk = [sz]
                for n in range(3):
                    t, c0 = n // 2, 64 * (n % 2)
                    bs = [B.take(), B.take()]
                    for j in range(2):
                        for par in range(2):
                            tp = PE.mm(bs[par].ap[64 * par:64 * par + 64, j * 128:j * 128 + 128],
                                       keT[c0:c0 + 64, t, j * 128 + 64 * par:j * 128 + 64 * par + 64],
                                       vg[c0:c0 + 64, t, (2 * j + par) * 128:(2 * j + par) * 128 + 128], True, True,
                                       [tke, bs[par].free], sig=True)
                    nw = []
                    for par in range(2):
                        for j in range(2):
                            hs = slice(64 * par, 64 * par + 64)
                            nw.append(VE.stt(S[hs, n + 1, j, :], S[hs, n, j, :], al[hs, j, n:n + 1],
                                             bs[par].ap[hs, j * 128:j * 128 + 128], MUL, ADD, [tp, x5, stk[-1]]))
                        bs[par].done(nw[-1])
                    stk.append(nw)
                SQ = XN[:, 0, 512:1024]
                for t in range(2):
                    bs = [B.take(), B.take()]
                    for par in range(2):
                        for j in range(2):
                            hd = 2 * j + par
                            o = bs[par].ap[:, j * 128:j * 128 + 128]
                            PE.mm(o, AT[:, t * 4 + hd, :], vg[:, t, hd * 128:hd * 128 + 128], True, False,
                                  [att[t], stk, bs[par].free])
                            for cc in range(2):
                                n = 2 * t + cc
                                hp = 64 * par
                                tp = PE.mm(bs[par].ap[64 * cc:64 * cc + 64, j * 128:j * 128 + 128],
                                           qd[hp:hp + 64, j, n * 64:n * 64 + 64], S[hp:hp + 64, n, j, :], False, True,
                                           sig=True)
                    G = XN[:, t, 0:512]
                    for par in range(2):
                        a = VE.cp(G.rearrange("p (j a d) -> p j a d", j=2, a=2)[:, :, par, :],
                                  bs[par].ap[:, 0:256].rearrange("p (j d) -> p j d", j=2), tp)
                        bs[par].done(a)
                    g = Bank(B, 0, G, None)
                    g.done = lambda *x: None
                    tg = head_norm(g, a, rg[:, t, :], O[:, t, 512:1024], 4, SQ, 44 + 4 * t)
                OT = HT
                tf = to_features(lambda t, k: O[:, t, k * 128:(k + 1) * 128], OT,
                                 lambda k: None if k < 4 else V("g_gla"), lambda k: None, [to, tg])
                need(rows[0])
                Y = XN
                out_proj([(T["w_out"][0], 0, 8)], OT, tf,
                         lambda t, half, p, tp: AC.act(Y[:, t, half * 512:half * 512 + 512], p, ACT.Copy, after=tp))
                post_norm(Y, 0, AC.last, O[:, 0, :], rows[0].tok)
            barrier()
            need(mods[1])
            bgon[0] = False
            moe(mods[1])

        def moe(m2):
            wgu, wd = T["w_gate_up"][0], T["w_down"][0]
            ph = ExitStack()
            with ph:
                XN = sb("XN2", [128, 2, D], c=ph)
                HT = sb("HT2", [128, 8, 256], c=ph)
                RW = sb("RW", [128, 8, 32], c=ph)
                RB = sb("RB", [128, 32], c=ph)
                BD = sb("BD", [32, D], c=ph)
                lr = loads("router")
                lr.go(PO, RW[:, :, :], T["router_w"][0].rearrange("(k p) e -> p k e", p=128))
                lr.go(PO, RB[:, :], T["router_b"].broadcast_to([128, 32]))
                lr.go(PO, BD[:, :], T["b_down"][0])
                h = norm_mod(XN, HT, 1, m2.tok, None)
                lg = sb("lg", [128, 2, 32], c=ph)
                G = sb("G", [128, 2, 32], c=ph)
                rk = sb("rk", [128, 2, 32], c=ph)
                sl = sb("sl", [128, 2, 32], c=ph)
                m8 = sb("m8", [128, 2, 8], c=ph)
                w4 = sb("w4", [128, 4, 32], c=ph)
                c4 = sb("c4", [128, 2, 4], c=ph)
                one32 = C("ones", 0, 32)
                for t in range(2):
                    b = B.take()
                    tp = PE.mms(b.ap[:, 0:32], [(HT[:, k, t * 128:t * 128 + 128], RW[:, k, :]) for k in range(8)],
                                [h, lr.tok, b.free])
                    a = VE.tt(lg[:, t, :], b.ap[:, 0:32], RB[:, :], ADD, [tp, lr.tok, VE.last])
                    b.done(a)
                    a = VE.do(lambda e, t=t: e.max(m8[:, t, :], lg[:, t, :]), a)
                    gt, eq, cs, x = (w4[:, i, :] for i in range(4))
                    a1 = VE.ts(gt, lg[:, t, :], m8[:, t, 3:4], ALU.is_gt, after=a)
                    a2 = VE.ts(eq, lg[:, t, :], m8[:, t, 3:4], ALU.is_equal)
                    VE.red(c4[:, t, 0:1], gt, ADD, a1)
                    a3 = VE.scan(cs, one32, eq, 0.0, MUL, ADD, a2)
                    a3 = VE.ts(x, cs, c4[:, t, 0:1], ADD, 4.5, ALU.is_lt, a3)
                    a3 = VE.tt(x, x, eq, MUL, a3)
                    a3 = VE.tt(sl[:, t, :], x, gt, ADD, a3)
                    n1 = VE.ts(c4[:, t, 1:2], m8[:, t, 0:1], -1.0, MUL)
                    e1 = AC.act(x, lg[:, t, :], ACT.Exp, bias=c4[:, t, 1:2], after=[a3, n1])
                    a3 = VE.ttr(G[:, t, :], x, sl[:, t, :], MUL, ADD, 0.0, c4[:, t, 2:3], e1)
                    a3 = VE.rec(c4[:, t, 3:4], c4[:, t, 2:3], a3)
                    a3 = VE.ts(G[:, t, :], G[:, t, :], c4[:, t, 3:4], MUL, after=a3)
                tG = a3
                cnt = sb("cnt", [128, 32], c=ph)
                flag = sb("flag", [128, 33], I32, c=ph)
                mxc = sb("mxc", [128, 33], c=ph)
                b = B.take()
                PE.mm(b.ap[:, 0:32], C("SU"), sl[:, 0, :], True, True, [tG, b.free])
                PE.mms(b.ap[:, 32:64], [(ones, sl[:, 0, :]), (C("SU"), sl[:, 1, :])])
                tp = PE.mms(b.ap[:, 64:96], [(ones, sl[:, 0, :]), (ones, sl[:, 1, :])])
                for t in range(2):
                    a = VE.stt(rk[:, t, :], b.ap[:, 32 * t:32 * t + 32], 1.0, sl[:, t, :], ADD, MUL, tp)
                    a = VE.ts(rk[:, t, :], rk[:, t, :], -1.0, ADD, after=a)
                trk = a
                a = VE.red(mxc[:, 32:33], b.ap[:, 64:96], MAX)
                a = VE.ts(mxc[:, 0:32], b.ap[:, 64:96], -1.0 if flip else 64.5, ALU.is_gt)
                b.done(a)
                a = VE.ts(mxc[:, 32:33], mxc[:, 32:33], -1.0 if flip else 128.5, ALU.is_gt)
                tflag = VE.cp(flag[:, :], mxc[:, :])
                ACCM = sb("ACCM", [128, 2, D], c=ph)
                GT = sb("GT", [32, 256], c=ph)
                b = B.take()
                for t in range(2):
                    tp = PE.tr(b.ap[0:32, t * 128:t * 128 + 128], G[:, t, :], ident, [tG, b.free], sig=True)
                a = VE.cp(GT[:, :], b.ap[0:32, 0:256], tp)
                b.done(a)
                ta = None
                for t in range(2):
                    for hf in range(2):
                        b = B.take()
                        tp = PE.mm(b.ap, GT[:, t * 128:t * 128 + 128], BD[:, hf * 512:hf * 512 + 512], True, True,
                                   [a, b.free, lr.tok], sig=True)
                        ta = VE.cp(ACCM[:, t, hf * 512:hf * 512 + 512], b.ap, tp)
                        b.done(ta)
                PG = sb("PG", [128, 2, 2, 128], c=ph)
                PGT = sb("PGT", [128, 2, 256], c=ph)
                XE = sb("XE", [128, 2, 8, 128], c=ph)
                BR = sb("BR", [33, 2048], c=ph)
                BB = sb("BB", [128, 2048], c=ph)
                T1 = sb("T1", [128, 512], c=ph)
                T2 = sb("T2", [128, 256], c=ph)
                AT = sb("AT2", [128, 8, 128], c=ph)
                A_ = HT[:, 0:4, :].rearrange("p k t -> p (k t)")
                Y = HT[:, 4:8, :].rearrange("p k t -> p (k t)")
                iota = C("iota")
                hold = {"br": None, "bb": None, "xe": [None, None], "pg": None, "pgt": [None, None], "at": None,
                        "y": None, "sc": None, "acc": ta}
                lbr = Loads(sem("s_br"))

                def bias(es):
                    for j, e in enumerate(es):
                        lbr.go(AC, BR[32 * j:32 * j + 1, :], T["b_gate_up"][0:1, e, :], hold["br"])
                    PO.pend = flat(hold["bb"], list(PO.pend))
                    for j in reversed(range(len(es))):
                        m = 128 if j == len(es) - 1 else 64
                        bt = PO.do(lambda g, j=j, m=m: g.partition_broadcast(BB[0:m, :], BR[32 * j:32 * j + 1, :], m),
                                   lbr.tok)
                    hold["br"] = bt
                    return bt

                def gather(es, i, base, dup=False):
                    if base is None:
                        shape = [128, 2, 2, 64]
                        v = [PG[:, x, :, :].rearrange("p t (e s) -> p t e s", e=2) for x in range(2)]
                        io = iota[:, 0:64].unsqueeze(1).unsqueeze(1).broadcast_to(shape)
                        VE.tt(v[0], io, rk[:, :, es[0]:es[0] + 2].unsqueeze(3).broadcast_to(shape), ALU.is_equal,
                              [trk, hold["pg"]])
                        pg = VE.tt(v[1], v[0], G[:, :, es[0]:es[0] + 2].unsqueeze(3).broadcast_to(shape), MUL)
                    else:
                        io = iota[:, 0:64].unsqueeze(1).broadcast_to([128, 2, 64]) if dup else iota
                        for t in range(2):
                            VE.ts(PG[:, 0, t, :].rearrange("p (e s) -> p e s", e=2) if dup else PG[:, 0, t, :], io, float(base), ADD, rk[:, t, es[0]:es[0] + 1], ALU.is_equal,
                                  [trk, hold["pg"]])
                            pg = VE.ts(PG[:, 1, t, :], PG[:, 0, t, :], G[:, t, es[0]:es[0] + 1], MUL)
                    xt = []
                    for k in range(0, 8, 4):
                        b = B.take()
                        for j in range(4):
                            f = (k + j) * 128
                            tp = PE.mms(b.ap[:, j * 128:j * 128 + 128],
                                        [(XN[:, t, f:f + 128], PG[:, 0, t, :]) for t in range(2)], [pg, b.free],
                                        sig=j == 3)
                        for j in range(4):
                            xt = AC.act(XE[:, i, k + j, :], b.ap[:, j * 128:j * 128 + 128], ACT.Identity,
                                        bias=MOD[:, 2, k + j:k + j + 1], scale=MOD[:, 3, k + j:k + j + 1],
                                        after=[tp, hold["xe"][i]])
                        b.done(xt)
                    b = B.take()
                    for t in range(2):
                        tp = PE.tr(b.ap[:, t * 128:t * 128 + 128], PG[:, 1, t, :], ident, [pg, b.free], sig=t == 1)
                    hold["pg"] = tp
                    tpg = AC.act(PGT[:, i, :], b.ap[:, 0:256], ACT.Copy, after=[tp, hold["pgt"][i]])
                    b.done(tpg)
                    return es, i, xt, tpg

                def stream(es, src, c, lhs, b, after, between=None):
                    ws = [wtile(src[e], c * 512, 512) for e in es]
                    m = 128 // len(es)
                    for k in range(8):
                        if k == 4 and between is not None:
                            after = between()
                        for j, w in enumerate(ws):
                            tp = PE.mm(b.ap[j * m:j * m + m, :], lhs[:, k, j * m:j * m + m], w.ap[:, k, :], k == 0, k == 7,
                                       [w.tok, b.free, after], sig=k == 7)
                    for w in ws:
                        w.done(tp)
                    return tp

                def glu(out_):
                    v = T1[:, :].rearrange("p (n a) -> p n a", a=2)
                    a = VE.ts(v[:, :, 0], v[:, :, 0], 7.0, MIN)
                    a2 = AC.act(T2[:, :], v[:, :, 0], ACT.Sigmoid, scale=1.702, after=a)
                    VE.ts(v[:, :, 1], v[:, :, 1], 7.0, MIN, -7.0, MAX)
                    VE.stt(v[:, :, 1], v[:, :, 1], 1.0, v[:, :, 0], ADD, MUL)
                    return VE.tt(out_, v[:, :, 1], T2[:, :], MUL, [a2, hold["at"]])

                def gate_up(x, bt, then):
                    es, i, xt, _ = x
                    for q in range(4):
                        b = B.take()
                        tp = stream(es, wgu, q, XE[:, i], b, xt)
                        a = VE.tt(T1[:, :], b.ap, BB[:, q * 512:q * 512 + 512], ADD, [tp, bt])
                        b.done(a)
                        a = glu(A_[:, q * 256:q * 256 + 256])
                        then(q, a)
                    hold["bb"] = a
                    hold["xe"][i] = tp
                    return a

                def turn(k, ta_):
                    b = B.take()
                    for j in range(4):
                        tp = PE.tr(b.ap[:, j * 128:j * 128 + 128], A_[:, (k + j) * 128:(k + j) * 128 + 128], ident,
                                   [ta_, b.free], sig=j == 3)
                    hold["at"] = tp
                    a = AC.act(AT[:, k:k + 4, :].rearrange("p k n -> p (k n)"), b.ap, ACT.Copy, after=[tp, hold["y"]])
                    b.done(a)
                    return a

                def down(x, at0, ta_):
                    es = x[0]
                    at1 = []

                    def between():
                        at1.append(turn(4, ta_))
                        return at1[0]
                    for hf in range(2):
                        b = B.take()
                        tp = stream(es, wd, hf, AT, b, at0 if hf == 0 else at1[0], between if hf == 0 else None)
                        ty = AC.act(Y[:, hf * 512:hf * 512 + 512], b.ap, ACT.Copy, after=[tp, hold["sc"]])
                        b.done(ty)
                    hold["y"] = tp
                    return ty

                def halves(e, base):
                    bt = bias((e,))
                    es, i, xt, tpg = gather((e,), 0, base, dup=True)
                    for q in range(0, 4, 2):
                        ws = [wtile(wgu[e], (q + j) * 512, 512) for j in range(2)]
                        b = B.take()
                        for k in range(8):
                            for j, w in enumerate(ws):
                                tp = PE.mm(b.ap[64 * j:64 * j + 64, :], XE[:, i, k, 64 * j:64 * j + 64], w.ap[:, k, :],
                                           k == 0, k == 7, [w.tok, b.free, xt], sig=k == 7)
                        for w in ws:
                            w.done(tp)
                        for j in range(2):
                            hs = slice(64 * j, 64 * j + 64)
                            a = VE.tt(T1[hs, :], b.ap[hs, :], BB[hs, (q + j) * 512:(q + j) * 512 + 512], ADD, [tp, bt])
                        b.done(a)
                        a = glu(A_[:, q * 128:q * 128 + 256])
                    hold["bb"] = a
                    hold["xe"][i] = tp
                    b = B.take()
                    for k in range(4):
                        tp = PE.tr(b.ap[:, k * 128:k * 128 + 128], A_[:, k * 128:k * 128 + 128], ident, [a, b.free], sig=k == 3)
                    hold["at"] = tp
                    a = AC.act(AT[:, 0:4, :].rearrange("p k n -> p (k n)"), b.ap, ACT.Copy, after=[tp, hold["y"]])
                    b.done(a)
                    ws = [wtile(wd[e], j * 512, 512) for j in range(2)]
                    b = B.take()
                    for k in range(8):
                        q, c = k // 2, k % 2
                        for j, w in enumerate(ws):
                            tp = PE.mm(b.ap[64 * j:64 * j + 64, :], AT[:, 2 * (q // 2) + c, 64 * (q % 2):64 * (q % 2) + 64],
                                       w.ap[:, k, :], k == 0, k == 7, [w.tok, b.free, a], sig=k == 7)
                    for w in ws:
                        w.done(tp)
                    hold["y"] = tp
                    ty = AC.act(Y[:, 0:512], b.ap, ACT.Copy, after=[tp, hold["sc"]])
                    b.done(ty)
                    for t in range(2):
                        for hf in range(2):
                            hs = slice(64 * hf, 64 * hf + 64)
                            b = B.take()
                            tp = PE.mm(b.ap, PGT[hs, i, t * 128:t * 128 + 128], Y[hs, 0:512], True, True,
                                       [ty, tpg, b.free], sig=True)
                            hold["acc"] = VE.tt(ACCM[:, t, hf * 512:hf * 512 + 512], ACCM[:, t, hf * 512:hf * 512 + 512],
                                                b.ap, ADD, tp)
                            b.done(hold["acc"])
                    hold["sc"] = tp
                    hold["pgt"][i] = tp

                def scatter(x, ty):
                    i, tpg = x[1], x[3]
                    for t in range(2):
                        for hf in range(2):
                            b = B.take()
                            tp = PE.mm(b.ap, PGT[:, i, t * 128:t * 128 + 128], Y[:, hf * 512:hf * 512 + 512], True, True,
                                       [ty, tpg, b.free], sig=True)
                            hold["acc"] = VE.tt(ACCM[:, t, hf * 512:hf * 512 + 512], ACCM[:, t, hf * 512:hf * 512 + 512],
                                                b.ap, ADD, tp)
                            b.done(hold["acc"])
                    hold["sc"] = tp
                    hold["pgt"][i] = tp

                x, bt, prev = gather((0, 1), 0, None), bias((0, 1)), None
                for pr in range(E_N // 2):
                    es2 = (2 * pr + 2, 2 * pr + 3)
                    got = {}

                    def then(q, a):
                        if q == 0 and prev is not None:
                            scatter(*prev)
                        if q == 1:
                            got["first"] = a
                            if pr < E_N // 2 - 1:
                                got["x"] = gather(es2, (pr + 1) % 2, None)
                        if q == 2:
                            got["at"] = turn(0, got["first"])
                    a = gate_up(x, bt, then)
                    if pr < E_N // 2 - 1:
                        bt = bias(es2)
                    prev = x, down(x, got["at"], a)
                    x = got.get("x")
                    if pr < 7:
                        background(1)
                scatter(*prev)
                queues = (PE, AC, VE, PO, SP)

                def branch(bit, body):
                    ends = [q.last for q in queues[:4]]
                    start = [q.n for q in queues]
                    uses = list(ring.uses)
                    nbr = lbr.n
                    for q in queues:
                        def enter(e, seen, outer, q=q):
                            for s_, v_ in [tflag]:
                                if seen.get(s_.name, 0) < v_:
                                    e.wait_ge(s_, v_)
                                    seen[s_.name] = v_
                            kept = dict(seen)
                            reg = e.value_load(flag[0:1, bit:bit + 1], min_val=0, max_val=1)
                            g = e.If(reg == 1)
                            g.__enter__()
                            if q is not SP:
                                for s_, v_ in ends:
                                    e.wait_ge(s_, v_)
                                    seen[s_.name] = max(v_, seen.get(s_.name, 0))
                            return (g, kept)
                        q.raw(enter)
                    B.free = [None] * 8
                    body()
                    toks = [q.last for q in queues[:4]]
                    more = {q.sem.name: [(q.sem, q.n - s_)] for q, s_ in zip(queues, start)}
                    more[SP.sem.name] = [(s_, 16 * (u1 - u0)) for s_, u1, u0 in zip(ring.sems, ring.uses, uses)]
                    more[AC.sem.name] += [(lbr.sem, lbr.n - nbr)]
                    before = {q.sem.name: [t_] for q, t_ in zip(queues, ends)}
                    before[SP.sem.name] = [(s_, 16 * u) for s_, u in zip(ring.sems, uses)]
                    before[AC.sem.name] = [ends[1], (lbr.sem, nbr)]
                    for q in queues:
                        def leave(e, seen, outer, q=q):
                            if q is not SP:
                                for s_, v_ in toks:
                                    if seen.get(s_.name, 0) < v_:
                                        e.wait_ge(s_, v_)
                            g, kept = outer
                            g.__exit__(None, None, None)
                            with e.Else():
                                for s_, v_ in before[q.sem.name]:
                                    if v_:
                                        e.wait_ge(s_, v_)
                                for s_, n_ in more[q.sem.name]:
                                    if n_:
                                        e.sem_inc(s_, n_)
                            seen.clear()
                            seen.update(kept)
                            return None
                        q.raw(leave)
                    for q in queues[:4]:
                        q.pend = q.pend + toks
                    B.free = [None] * 8

                def alone(e, base):
                    x = gather((e,), 0, base)
                    a = gate_up(x, bias((e,)), lambda q, a: None)
                    scatter(x, down(x, turn(0, a), a))

                barrier()
                for e in range(E_N):
                    branch(e, lambda: halves(e, 64))

                def rest():
                    for e in range(E_N):
                        alone(e, 128)
                branch(E_N, rest)
                toks = [VE.last]
                post_norm(ACCM, 1, toks, XN[:, 0, :], need(rows[1]))
            barrier()

        def bc(ap, n):
            return ap.unsqueeze(1).broadcast_to([128, n, ap.shape[1]])

        def ex(ap, n):
            return ap.unsqueeze(2).broadcast_to([128, ap.shape[1], n])

        def heads(ap, n):
            return ap.rearrange("p (h d) -> p h d", h=n)

        def second():
            wi = T["w_in_2"][0]
            with ExitStack() as ph:
                XN = sb("XN3", [128, 2, D], c=ph)
                HT = sb("HT3", [128, 8, 256], c=ph)
                O = sb("O3", [128, 2, D], c=ph)
                bgon[0] = True
                h = norm_mod(XN, HT, 2, need(mods[2]), None)
                zd = sb("zd", [128, 2, 512], c=ph)
                CO = sb("CO", [128, 12, 256], c=ph)
                BG = sb("BG", [128, 2, 8], c=ph)
                AD = sb("AD", [128, 8], c=ph)
                zm = sb("zm", [128, 2, 512], c=ph)
                GC = sb("GC", [128, 2, 4, 4], c=ph)
                SG = [GR[:, g:g + 2, :].rearrange("p b (j t) -> p b j t", j=4) for g in (0, 3)]
                ld = loads("decay")
                ld.go(PO, AD[:, 0:4], T["a_log_2"].broadcast_to([128, 4]))
                ld.go(PO, AD[:, 4:8], T["dt_bias_2"].broadcast_to([128, 4]))
                pm = ExitStack()
                qm = sb("qm", [128, 4, 256], c=pm)
                km = sb("km", [128, 4, 256], c=pm)
                vm = sb("vm", [128, 2, 512], c=pm)
                cb = ExitStack()
                CI = [sb("CI", [128, 4, 260], c=cb)[:, :, :] for _ in range(2)]
                ct = [None, None]
                VE.mset(CI[0][:, :, 0:3], 0.0)
                z = VE.mset(CI[1][:, :, 0:3], 0.0)
                for g in range(3):
                    i = g % 2
                    cw = []

                    def put(j, p, tp, i=i):
                        return AC.act(CI[i][:, j, 3:259], p, ACT.Copy, after=[tp, ct[i], z])
                    feats(wtile(wi, 512 * g, 512), 4, HT, h, put)
                    a = AC.last
                    for j in range(4):
                        f = 4 * g + j
                        VE.ts(CO[:, f, :], CI[i][:, j, 0:256], V("conv_w_2", f), MUL, after=a)
                        for k in range(1, 4):
                            ct[i] = VE.stt(CO[:, f, :], CI[i][:, j, k:k + 256], V("conv_w_2", 12 * k + f),
                                           CO[:, f, :], MUL, ADD)
                    cof = CO[:, 4 * g:4 * g + 4, :].rearrange("p j t -> p (j t)")
                    tco = AC.act(cof, cof, ACT.Silu, after=ct[i])
                w = wtile(wi, 1536, 520)
                bytoks(w, 0, 512, HT, h, lambda t, p, tp: AC.act(zd[:, t, :], p, ACT.Silu, after=tp), done=False)
                b = B.take()
                for t in range(2):
                    tp = toks_(w, 512, 8, HT, t, b, 8 * t, h)
                w.done(tp)
                bg = BG[:, :, :]
                a = VE.cp(bg, b.ap[:, 0:16].rearrange("p (t c) -> p t c", t=2), tp)
                b.done(a)
                sp = st[:, 0:8].rearrange("p (t c) -> p t c", t=2)
                a1 = AC.act(BG[:, :, 0:4], BG[:, :, 0:4], ACT.Sigmoid, after=a)
                a2 = VE.tt(BG[:, :, 4:8], BG[:, :, 4:8], AD[:, 4:8].unsqueeze(1).broadcast_to([128, 2, 4]), ADD, ld.tok)
                a2 = AC.act(sp, BG[:, :, 4:8], ACT.Abs, after=a2)
                a2 = AC.act(sp, sp, ACT.Exp, scale=-1.0)
                a2 = AC.act(sp, sp, ACT.Ln, bias=1.0)
                a3 = AC.act(AD[:, 0:4], AD[:, 0:4], ACT.Exp, after=ld.tok)
                a2 = VE.stt(BG[:, :, 4:8], BG[:, :, 4:8], 0.0, sp, MAX, ADD, [a2, a3])
                a2 = VE.stt(BG[:, :, 4:8], BG[:, :, 4:8], -1.0, AD[:, 0:4].unsqueeze(1).broadcast_to([128, 2, 4]), MUL, MUL)
                tbg = [a1, a2]
                SQ = XN[:, 1, :]

                def unit(g, a):
                    cof = CO[:, 4 * g:4 * g + 4, :].rearrange("p j t -> p (j t)")
                    bs = [B.take(), B.take()]
                    for i in range(2):
                        tp = PE.mm(bs[i].ap, ones, SQ[:, 512 * i:512 * i + 512], True, True, [a, bs[i].free], sig=True)
                    for i in range(2):
                        a = AC.act(SQ[:, 512 * i:512 * i + 512], bs[i].ap, ACT.Ln, bias=EPSC[:, :], after=tp)
                        bs[i].done(a)
                    a = AC.act(SQ[:, :], SQ[:, :], ACT.Exp, scale=-0.5)
                    return VE.stt(cof, cof, float(128 ** -0.5) if g == 0 else 1.0, SQ[:, :], MUL, MUL, a)

                def square(g, after):
                    return AC.act(SQ[:, :], CO[:, 4 * g:4 * g + 4, :].rearrange("p j t -> p (j t)"), ACT.Square, after=after)
                a = square(0, h)
                feats(wtile(wi, 2056, 512), 4, HT, h, lambda j, p, tp: AC.act(qm[:, j, :], p, ACT.Copy, scale=0.125, after=tp))
                a = square(1, unit(0, a))
                feats(wtile(wi, 2568, 512), 4, HT, h, lambda j, p, tp: AC.act(km[:, j, :], p, ACT.Copy, after=tp))
                tn = unit(1, a)
                b = B.take()
                for t in range(2):
                    PE.mm(b.ap[:, 8 * t:8 * t + 4], C("U64"), BG[:, t, 4:8], True, True, [tbg, b.free])
                    tp = PE.mm(b.ap[:, 8 * t + 4:8 * t + 8], C("B64"), BG[:, t, 4:8], True, True, sig=True)
                for t in range(2):
                    a = VE.cp(GC[:, t, 0, :], b.ap[:, 8 * t:8 * t + 4], tp)
                    a2 = VE.tt(GC[:, t, 2, :], b.ap[:, 8 * t + 4:8 * t + 8], GC[:, t, 0, :], SUB, a)
                    a = AC.act(GC[:, t, 1, :], GC[:, t, 0, :], ACT.Exp, after=a2)
                    a = AC.act(GC[:, t, 2, :], GC[:, t, 2, :], ACT.Exp)
                    a = VE.stt(GC[:, t, 1, :], GC[:, t, 1, :], -1.0, BG[:, t, 0:4], MUL, MUL, a)
                b.done(a)
                bytoks(wtile(wi, 3080, 512), 0, 512, HT, h, lambda t, p, tp: AC.act(vm[:, t, :], p, ACT.Copy, after=tp))
                bytoks(wtile(wi, 3592, 512), 0, 512, HT, h, lambda t, p, tp: AC.act(zm[:, t, :], p, ACT.Silu, after=tp))
                cb.close()
                barrier()
                for half in range(2):
                    for br in range(2):
                        later_feats(wi, 4104 + 1024 * br + 512 * half, HT, h,
                                    lambda j, p, tp, o=SG[half][:, br, :, :]:
                                    AC.act(o[:, j, :], p, ACT.Copy, after=tp))
                with ExitStack() as pa:
                    to = softmax_attn(pa, qm, km, vm, lambda t: C(f"CB{t}"), lambda t: O[:, t, 512:1024], [AC.last],
                                      XN[:, 1, :].rearrange("p (h n) -> p h n", h=4))
                for t in range(2):
                    VE.tt(O[:, t, 512:1024], O[:, t, 512:1024], zm[:, t, :], MUL)
                pm.close()
                barrier()
                pd = ExitStack()
                qT, kT, vT = CO[:, 0:4, :], CO[:, 4:8, :], CO[:, 8:12, :]
                per = {}
                HC = [slice(hd * 128, hd * 128 + 128) for hd in range(4)]
                for t in range(2):
                    p = per[t] = {n: sb(f"d{n}{t}", [128, 512], c=pd)
                                  for n in ("eR", "aT", "qk", "U", "T", "Y", "kg", "vb")}
                    p["vn"], p["wT"], p["qg"], p["kb"] = p["Y"], p["T"], p["aT"], O[:, t, 0:512]

                def by_heads(b, lhs, rhs, after):
                    for hd in range(4):
                        tp = PE.mm(b.ap[:, HC[hd]], lhs(hd), rhs(hd), True, True, [after, b.free], sig=hd == 3)
                    return tp

                def inverse(t):
                    p = per[t]
                    tok = slice(t * 128, t * 128 + 128)
                    W5, W6 = XN[:, t, 0:512], XN[:, t, 512:1024]
                    a5 = VE.tt(heads(W5, 4), bc(C("U64"), 4), ex(BG[:, t, 4:8], 128), MUL)
                    a6 = VE.tt(heads(W6, 4), bc(ident, 4), ex(BG[:, t, 0:4], 128), MUL)
                    b, b2 = B.take(), B.take()
                    PE.mm(b.ap, ones, W5, True, True, [a5, b.free])
                    tp = PE.mm(b2.ap, ones, W6, True, True, [a6, b2.free], sig=True)
                    yield
                    a = AC.act(p["eR"][:, :], b.ap, ACT.Exp, after=tp)
                    a = VE.tt(heads(W5, 4), heads(b.ap, 4), ex(GC[:, t, 0, :], 128), SUB, [a, tp])
                    b.done(a)
                    a = VE.ts(W5, W5, 0.0, MIN)
                    a = AC.act(W5, W5, ACT.Exp, after=a)
                    bk, bq = B.take(), B.take()
                    by_heads(bk, lambda hd: kT[:, hd, tok], lambda hd: kT[:, hd, tok], tn)
                    tkq = by_heads(bq, lambda hd: kT[:, hd, tok], lambda hd: qT[:, hd, tok], tn)
                    yield
                    a = VE.tt(heads(W6, 4), heads(W5, 4), bc(C("SU64"), 4), MUL, [a, tp])
                    a = VE.tt(W6, W6, b2.ap, MUL)
                    b2.done(a)
                    a = VE.tt(p["aT"][:, :], bk.ap, W6, MUL, tkq)
                    bk.done(a)
                    VE.tt(heads(W6, 4), heads(p["aT"][:, :], 4), bc(C("H1"), 4), MUL)
                    a = VE.tt(heads(p["U"][:, :], 4), bc(ident, 4), heads(W6, 4), SUB)
                    b = B.take()
                    for hd in range(4):
                        tp = PE.tr(b.ap[:, HC[hd]], p["U"][:, HC[hd]], ident, [a, b.free], sig=hd == 3)
                    p["tU"] = p["tT"] = AC.act(p["T"][:, :], b.ap, ACT.Copy, after=tp)
                    b.done(p["tT"])
                    b, b2 = B.take(), B.take()
                    for hd in range(4):
                        PE.tr(b.ap[:, HC[hd]], kT[:, hd, tok], ident, [tn, b.free])
                    for hd in range(4):
                        tp = PE.tr(b2.ap[:, HC[hd]], vT[:, hd, tok], ident, [tco, b2.free], sig=hd == 3)
                    yield
                    VE.tt(heads(W5, 4), heads(W5, 4), bc(C("U64"), 4), MUL)
                    a = VE.tt(p["qk"][:, :], bq.ap, W5, MUL)
                    bq.done(a)
                    VE.tt(heads(p["kb"], 4), heads(b.ap, 4), ex(GC[:, t, 1, :], 128), MUL, tp)
                    a = VE.tt(heads(p["kg"][:, :], 4), heads(b.ap, 4), ex(GC[:, t, 2, :], 128), MUL)
                    b.done(a)
                    a = VE.tt(heads(p["vb"][:, :], 4), heads(b2.ap, 4), ex(BG[:, t, 0:4], 128), MUL)
                    b2.done(a)
                    p["tk"] = a
                    W, rd = (W5, W6), [None, None]

                    def left(i):
                        return VE.tt(heads(W[i % 2], 4), heads(p["aT"][:, :], 4), bc(C(f"H{2 << i}"), 4), MUL, rd[i % 2])
                    tw = left(0)
                    for i in range(5):
                        b = B.take()
                        tp = rd[i % 2] = by_heads(b, lambda hd: W[i % 2][:, HC[hd]], lambda hd: p["T"][:, HC[hd]], [tw, p["tT"]])
                        ty = AC.act(p["Y"][:, :], b.ap, ACT.Copy, after=tp)
                        b.done(ty)
                        if i < 4:
                            tw = left(i + 1)
                        yield
                        if i < 4:
                            b2 = B.take()
                            tp2 = by_heads(b2, lambda hd: p["U"][:, HC[hd]], lambda hd: p["Y"][:, HC[hd]], [ty, p["tU"]])
                        b = B.take()
                        tp = by_heads(b, lambda hd: p["Y"][:, HC[hd]], lambda hd: p["U"][:, HC[hd]], [ty, p["tU"]])
                        if i < 4:
                            p["tT"] = VE.tt(p["T"][:, :], p["T"][:, :], b2.ap, SUB, tp2)
                            b2.done(p["tT"])
                        p["tU"] = VE.tt(p["U"][:, :], p["U"][:, :], b.ap, SUB, tp)
                        b.done(p["tU"])
                        yield
                    b = B.take()
                    tp = by_heads(b, lambda hd: p["kb"][:, HC[hd]], lambda hd: p["U"][:, HC[hd]], [p["tU"], p["tk"]])
                    a = AC.act(p["wT"][:, :], b.ap, ACT.Copy, after=tp)
                    b.done(a)
                    p["tw"] = [a, VE.tt(heads(p["qg"][:, :], 4), qT[:, :, tok], heads(p["eR"][:, :], 4), MUL)]
                steps = [inverse(0), inverse(1)]
                while steps:
                    for g in list(steps):
                        if next(g, steps) is steps:
                            steps.remove(g)
                    fill()
                S = zm[:, 0, :]
                ts_ = VE.mset(S, 0.0)
                for n in range(4):
                    t, c0 = n // 2, 64 * (n % 2)
                    p = per[t]
                    rw = slice(c0, c0 + 64)
                    b = B.take()
                    for hd in range(4):
                        hc = slice(hd * 128, hd * 128 + 128)
                        cc = slice(hd * 128 + c0, hd * 128 + c0 + 64)
                        PE.mm(b.ap[rw, hc], p["U"][:, cc], p["vb"][:, hc], True, False, [p["tw"], ts_, b.free])
                        tp = PE.mm(b.ap[rw, hc], p["wT"][:, cc], S[:, hc], False, True, sig=hd == 3)
                    tv = AC.act(p["vn"][rw, :], b.ap[rw, :], ACT.Copy, after=tp)
                    b.done(tv)
                    if n % 2 == 0:
                        bo = B.take()
                    for hd in range(4):
                        hc = slice(hd * 128, hd * 128 + 128)
                        cc = slice(hd * 128 + c0, hd * 128 + c0 + 64)
                        PE.mm(bo.ap[rw, hc], p["qg"][:, cc], S[:, hc], True, False, [bo.free, ts_, tv])
                        tp = PE.mm(bo.ap[rw, hc], p["qk"][rw, cc], p["vn"][rw, hc], False, True, sig=hd == 3)
                    if n < 3:
                        b = B.take()
                        for hd in range(4):
                            hc = slice(hd * 128, hd * 128 + 128)
                            tp = PE.mm(b.ap[:, hc], p["kg"][rw, hc], p["vn"][rw, hc], True, True, b.free, sig=hd == 3)
                        for hd in range(4):
                            hc = slice(hd * 128, hd * 128 + 128)
                            ts_ = VE.stt(S[:, hc], S[:, hc], p["eR"][:, hd * 128 + c0 + 63:hd * 128 + c0 + 64],
                                         b.ap[:, hc], MUL, ADD, tp)
                        b.done(ts_)
                    if n % 2 == 1:
                        tg = head_norm(bo, tp, zd[:, t, :], O[:, t, 0:512], 4, SQ[:, 0:512], 44 + 4 * t)
                pd.close()
                barrier()
                OT = sb("OT3", [128, 8, 256], c=ph)
                tf = to_features(lambda t, k: O[:, t, k * 128:(k + 1) * 128], OT,
                                 lambda k: V("dn_norm_g_2") if k < 4 else None, lambda k: None, [tg, to])
                fill_rest()
                MX = sb("MX", [128, 8, 256], c=ph)
                for half in range(2):
                    sg = SG[half]
                    for br in range(2):
                        tsg = AC.act(sg[:, br, :, :], sg[:, br, :, :], ACT.Sigmoid)

                    def put0(j, p, tp):
                        return VE.tt(MX[:, 4 * half + j, :], p, sg[:, 0, j, :], MUL, [tp, tsg])

                    def put1(j, p, tp):
                        return VE.tt(sg[:, 1, j, :], p, sg[:, 1, j, :], MUL, [tp, tsg])
                    feats(wtile(T["w_proj_dn_2"][0], 512 * half, 512, 0, 512), 4, OT[:, 0:4, :], tf, put0)
                    feats(wtile(T["w_proj_mb_2"][0], 512 * half, 512, 0, 512), 4, OT[:, 4:8, :], tf, put1)
                    tm = VE.tt(MX[:, 4 * half:4 * half + 4, :], MX[:, 4 * half:4 * half + 4, :], sg[:, 1, :, :], ADD)
                Y = XN
                out_proj([(T["w_out_2"][0], 0, 8)], MX, tm,
                         lambda t, half, p, tp: AC.act(Y[:, t, half * 512:half * 512 + 512], p, ACT.Copy, after=tp))
                post_norm(Y, 2, AC.last, O[:, 0, :], need(rows[2]))
            barrier()

        def add_gated(slot, tmp, tok):
            tok = tok()

            def put(t, half, p, tp):
                hs = slice(half * 512, half * 512 + 512)
                a = VE.tt(tmp[:, t, hs], p, GR[:, slot, hs], MUL, [tp, tok])
                VE.tt(X[:, t, hs], X[:, t, hs], tmp[:, t, hs], ADD, a)
                return a
            return put

        def ffn(layer, slot, grslot, modtok, growtok):
            w_in, w_out = T["ffn_w_in_3"][layer], T["ffn_w_out_3"][layer]
            with ExitStack() as ph:
                XN = sb(f"XF{layer}", [128, 2, D], c=ph)
                HT = sb(f"HF{layer}", [128, 8, 256], c=ph)
                A = sb(f"AF{layer}", [128, FT, 256], c=ph)
                CI = sb(f"CF{layer}", [128, 2, 4, 258], c=ph)
                z = VE.mset(CI[:, :, :, 0:2], 0.0)
                h = norm_mod(XN, HT, slot, modtok, None)
                hold = [None, None]
                for g in range(6):
                    n = 4 if g < 5 else 2
                    i = g % 2

                    def put(j, p, tp, i=i):
                        return AC.act(CI[:, i, j, 2:258], p, ACT.Copy, after=[tp, hold[i], z])
                    feats(wtile(w_in, 512 * g, 128 * n), n, HT, h, put)
                    a = AC.last
                    for j in range(n):
                        f = 4 * g + j
                        cw = 66 * layer + f
                        VE.ts(A[:, f, :], CI[:, i, j, 0:256], V("ffn_conv_w_3", cw), MUL,
                              V("ffn_conv_b_3", 22 * layer + f), ADD, a)
                        VE.stt(A[:, f, :], CI[:, i, j, 1:257], V("ffn_conv_w_3", cw + 22), A[:, f, :], MUL, ADD)
                        hold[i] = VE.stt(A[:, f, :], CI[:, i, j, 2:258], V("ffn_conv_w_3", cw + 44), A[:, f, :], MUL, ADD)
                    af = A[:, 4 * g:4 * g + n, :].rearrange("p j t -> p (j t)")
                    AC.act(af, af, ACT.Gelu_apprx_tanh, after=hold[i])
                ta = AC.last
                for g in range(6):
                    n = 4 if g < 5 else 2

                    def put(j, p, tp, g=g):
                        return VE.tt(A[:, 4 * g + j, :], A[:, 4 * g + j, :], p, MUL, [tp, ta])
                    feats(wtile(w_in, FFN + 512 * g, 128 * n), n, HT, h, put)
                out_proj([(w_out, 0, 8), (w_out, 1024, 8), (w_out, 2048, 6)], A, VE.last, add_gated(grslot, XN, growtok))
            barrier()

        def even(modtok, growtok):
            wi = T["even_w_in_3"][0]
            with ExitStack() as ph:
                XN = sb("XE3", [128, 2, D], c=ph)
                HT = sb("HE3", [128, 8, 256], c=ph)
                h = norm_mod(XN, HT, 3, modtok, None)
                names = ("qa", "ka", "lf", "bcu", "qb", "kb")
                qa, ka, lf, bcu, qb, kb = (sb("e" + n, [128, 4, 256], c=ph) for n in names)
                ia, ga, vb = (sb("e" + n, [128, 2, 512], c=ph) for n in ("ia", "ga", "vb"))
                fl = lambda x: x[:, :, :].rearrange("p j t -> p (j t)")
                feats(wtile(wi, 0, 512), 4, HT, h, lambda j, p, tp: AC.act(qa[:, j, :], p, ACT.Copy, after=tp))
                feats(wtile(wi, 512, 512), 4, HT, h, lambda j, p, tp: AC.act(lf[:, j, :], p, ACT.Copy, after=tp))
                bytoks(wtile(wi, 1024, 512), 0, 512, HT, h, lambda t, p, tp: AC.act(ia[:, t, :], p, ACT.Copy, after=tp))
                bytoks(wtile(wi, 1536, 512), 0, 512, HT, h, lambda t, p, tp: AC.act(ga[:, t, :], p, ACT.Silu, after=tp))
                later_feats(wi, 2048, HT, h,
                            lambda j, p, tp: AC.act(qb[:, j, :], p, ACT.Copy, scale=float(128 ** -0.5), after=tp))
                later_feats(wi, 2560, HT, h, lambda j, p, tp: AC.act(kb[:, j, :], p, ACT.Copy, after=tp))
                later_toks(wi, 3072, HT, h, lambda t, p, tp: AC.act(vb[:, t, :], p, ACT.Copy, after=tp))
                AC.act(fl(ka), fl(lf), ACT.Sigmoid, scale=-1.0)
                fill()
                AC.act(fl(bcu), fl(lf), ACT.Abs)
                AC.act(fl(bcu), fl(bcu), ACT.Exp, scale=-1.0)
                a = AC.act(fl(bcu), fl(bcu), ACT.Ln, bias=1.0)
                VE.stt(fl(lf), fl(lf), 0.0, fl(bcu), MIN, SUB, a)
                for j in range(4):
                    tb = VE.scan(bcu[:, j, :], C("R128"), lf[:, j, :], 0.0, MUL, ADD)
                Et, QL, KL = lf, XN[:, 0, :], XN[:, 1, :]
                SC = sb("SC", [128, 2, 512], c=ph)
                z = VE.mset(SC[:, :, :], 0.0)
                free, tka, et = None, AC.last, None
                for L in (0, 1, 2, 4, 8, 16, 32, 64):
                    if L:
                        v = fl(bcu).rearrange("p (n l) -> p n l", l=2 * L)
                        ev = fl(Et).rearrange("p (n l) -> p n l", l=2 * L)
                        n = 1024 // (2 * L)
                        bm = v[:, :, L - 1:L].broadcast_to([128, n, L])
                        VE.tt(ev[:, :, 0:L], bm, v[:, :, 0:L], SUB, [et, PO.last if PO.n else None])
                        a = VE.tt(ev[:, :, L:2 * L], v[:, :, L:2 * L], bm, SUB)
                        a = et = AC.act(fl(Et), fl(Et), ACT.Exp, after=a)
                        t1 = VE.tt(QL, fl(qa), fl(Et), MUL, [a, free])
                        t2 = [PO.tt(heads(KL, 4)[:, :, c0:c0 + 128], ka[:, :, c0:c0 + 128], Et[:, :, c0:c0 + 128], MUL,
                                    [a, free]) for c0 in (0, 128)]
                        ql, kl, m = heads(QL, 4), heads(KL, 4), C(f"H{L}")
                    else:
                        t1, t2 = tka, [tka, tka]
                        ql, kl, m = qa[:, :, :], ka[:, :, :], ident
                    for t in range(2):
                        b = B.take()
                        tok = slice(t * 128, t * 128 + 128)
                        for hd in range(4):
                            tp = PE.mm(b.ap[:, hd * 128:hd * 128 + 128], kl[:, hd, tok], ql[:, hd, tok], True, True,
                                       [t1, t2[t], b.free], sig=hd == 3)
                        a = VE.cpred(heads(SC[:, t, :], 4), bc(m.bitcast(U32), 4), heads(b.ap, 4), tp)
                        b.done(a)
                        free = tp
                    fill(2)
                tsc = a
                fill_rest()
                tqk = AC.last
                K1, Q1, KT, S0 = (sb("e" + n, [128, 512], c=ph) for n in ("K1", "Q1", "KT", "S0"))
                a = VE.tt(heads(K1[:, :], 4), bcu[:, :, 127:128].broadcast_to([128, 4, 128]), bcu[:, :, 0:128], SUB)
                AC.act(K1[:, :], K1[:, :], ACT.Exp, after=a)
                a = AC.act(heads(Q1[:, :], 4), bcu[:, :, 128:256], ACT.Exp)
                VE.tt(heads(K1[:, :], 4), heads(K1[:, :], 4), ka[:, :, 0:128], MUL, a)
                a = VE.tt(heads(Q1[:, :], 4), heads(Q1[:, :], 4), qa[:, :, 128:256], MUL)
                ZS = sb("ZS", [128, 4, 384], c=ph)
                LK = XN[:, :, :].rearrange("p a d -> p (a d)")[:, 0:1536].rearrange("p (h t) -> p h t", h=4)
                for hd in range(4):
                    b = B.take()
                    PE.mm(b.ap[:, 0:256], kb[:, hd, 0:128], qb[:, hd, :], True, True, [tqk, b.free])
                    tp = PE.mm(b.ap[:, 256:384], kb[:, hd, 128:256], qb[:, hd, 128:256], True, True, sig=True)
                    az = AC.act(ZS[:, hd, :], b.ap[:, 0:384], ACT.Copy, after=tp)
                    b.done(az)
                b = B.take()
                for hd in range(4):
                    hc = slice(hd * 128, hd * 128 + 128)
                    tp = PE.tr(b.ap[:, hc], K1[:, hc], ident, [a, b.free], sig=hd == 3)
                a = AC.act(KT[:, :], b.ap, ACT.Copy, after=tp)
                b.done(a)
                b = B.take()
                for hd in range(4):
                    hc = slice(hd * 128, hd * 128 + 128)
                    tp = PE.mm(b.ap[:, hc], KT[:, hc], ia[:, 0, hc], True, True, [a, b.free], sig=hd == 3)
                ts0 = AC.act(S0[:, :], b.ap, ACT.Copy, after=tp)
                b.done(ts0)
                AC.act(fl(LK), fl(ZS), ACT.Abs, after=free)
                AC.act(fl(LK), fl(LK), ACT.Exp, scale=-1.0)
                tln = AC.act(fl(LK), fl(LK), ACT.Ln, bias=1.0)
                a = VE.stt(fl(LK), fl(ZS), 0.0, fl(LK), MAX, ADD, tln)
                a = VE.ts(fl(LK), fl(LK), -1.0, MUL)
                for c0 in (0, 256):
                    tl = VE.tt(LK[:, :, c0:c0 + 128], LK[:, :, c0:c0 + 128], bc(C("SU"), 4), MUL)
                O = sb("OE", [128, 2, 512], c=ph)
                for t in range(2):
                    b = B.take()
                    for hd in range(4):
                        hc = slice(hd * 128, hd * 128 + 128)
                        tp = PE.mm(b.ap[:, hc], SC[:, t, hc], ia[:, t, hc], True, t == 0, [tsc, ts0, b.free], sig=True)
                        if t == 1:
                            tp = PE.mm(b.ap[:, hc], Q1[:, hc], S0[:, hc], False, True, sig=True)
                    tg = head_norm(b, tp, ga[:, t, :], O[:, t, :], 4, XN[:, 1, 512:1024], 44 + 4 * t)
                for hd in range(4):
                    b = B.take()
                    PE.mm(b.ap[:, 0:256], C("LF"), LK[:, hd, 0:256], True, False, [tl, b.free])
                    PE.mm(b.ap[:, 128:256], ones, LK[:, hd, 256:384], False, True)
                    tp = PE.mm(b.ap[:, 256:384], C("LF"), LK[:, hd, 256:384], True, True, sig=True)
                    a = VE.tt(ZS[:, hd, :], ZS[:, hd, :], b.ap[:, 0:384], ADD, tp)
                    b.done(a)
                for c0 in (0, 256):
                    a = VE.tt(ZS[:, :, c0:c0 + 128], ZS[:, :, c0:c0 + 128], bc(C("NM"), 4), ADD)
                tz = AC.act(fl(ZS), fl(ZS), ACT.Exp, after=a)
                OT = HT
                for hd in range(4):
                    hc = slice(hd * 128, hd * 128 + 128)
                    b = B.take()
                    PE.mm(b.ap[:, 0:256], vb[:, 0, hc], ZS[:, hd, 0:256], True, False, [tz, b.free])
                    tp = PE.mm(b.ap[:, 128:256], vb[:, 1, hc], ZS[:, hd, 256:384], False, True, sig=True)
                    to = AC.act(OT[:, 4 + hd, :], b.ap[:, 0:256], ACT.Copy, after=tp)
                    b.done(to)
                tf = to_features(lambda t, k: O[:, t, k * 128:(k + 1) * 128], OT,
                                 lambda k: V("hgrn_norm_g_3", k), lambda k: None, tg, 4)
                out_proj([(T["even_w_out_3"][0], 0, 8)], OT, [tf, to], add_gated(3, XN, growtok))
            barrier()

        def odd(modtok, growtok):
            wi = T["odd_w_in_3"][0]
            with ExitStack() as ph:
                XN = sb("XO3", [128, 2, D], c=ph)
                HT = sb("HO3", [128, 8, 256], c=ph)
                h = norm_mod(XN, HT, 5, modtok, None)
                CO = sb("COo", [128, 8, 256], c=ph)
                CI = sb("CIo", [128, 4, 260], c=ph)
                VX = sb("VX", [128, 2, 8, 129], c=ph)
                OG = sb("OG", [128, 2, D], c=ph)
                E8 = sb("E8", [8, 6, 256], c=ph)
                GBI = sb("GBI", [8, 2], c=ph)
                CCM = sb("CCM", [128, 2, 16], c=ph)
                lg = loads("gateb")
                gsrc = T["odd_gate_b_3"].rearrange("a (g p) -> (a g) p", p=8)
                for g in range(2):
                    lg.go(PO, GBI[:, g:g + 1], gsrc[g, :].rearrange("(p o) -> p o", o=1))
                z = VE.mset(CI[:, :, 0:3], 0.0)
                z = VE.mset(VX[:, :, :, 128:129], 1.0)
                z = VE.mset(E8[:, 5, :], 1.0)
                w = wtile(wi, 3072, 16)
                b = B.take()
                for g in range(2):
                    tp = PE.mms(b.ap[0:8, 256 * g:256 * g + 256],
                                [(w.ap[:, k, 8 * g:8 * g + 8], HT[:, k, :]) for k in range(8)], [w.tok, b.free, h])
                w.done(tp)
                ig, lf, bs_, cm, nm, one = (E8[:, i, :] for i in range(6))
                VE.ts(ig, b.ap[0:8, 0:256], GBI[:, 0:1], ADD, after=[tp, lg.tok])
                a = VE.ts(lf, b.ap[0:8, 256:512], GBI[:, 1:2], ADD)
                b.done(a)
                a = AC.act(bs_, lf, ACT.Abs, after=a)
                a = AC.act(bs_, bs_, ACT.Exp, scale=-1.0)
                a = AC.act(bs_, bs_, ACT.Ln, bias=1.0)
                VE.stt(lf, lf, 0.0, bs_, MIN, SUB, a)
                VE.scan(bs_, one, lf, 0.0, MUL, ADD)
                VE.tt(ig, ig, bs_, SUB)
                VE.scan(cm, one, ig, 0.0, MUL, MAX)
                a = VE.stt(nm, bs_, -1.0, cm, MUL, SUB)
                b = B.take()
                for t in range(2):
                    tk = slice(t * 128, t * 128 + 128)
                    PE.tr(b.ap[:, 16 * t:16 * t + 8], ig[:, tk], ident[0:8, 0:8], [a, b.free])
                    tp = PE.tr(b.ap[:, 16 * t + 8:16 * t + 16], nm[:, tk], ident[0:8, 0:8], sig=True)
                a = VE.cp(CCM[:, :, :], b.ap[:, 0:32].rearrange("p (t c) -> p t c", t=2), tp)
                b.done(a)
                tcm = AC.act(CCM[:, :, 8:16], CCM[:, :, 8:16], ACT.Exp, after=a)
                ct = None
                for g in range(2):
                    feats(wtile(wi, 512 * g, 512), 4, HT, h,
                          lambda j, p, tp: AC.act(CI[:, j, 3:259], p, ACT.Copy, after=[tp, ct, z]))
                    a = AC.last
                    for j in range(4):
                        f = 4 * g + j
                        VE.ts(CO[:, f, :], CI[:, j, 0:256], V("odd_conv_w_3", f), MUL, V("odd_conv_b_3", f), ADD, a)
                        for k in range(1, 4):
                            ct = VE.stt(CO[:, f, :], CI[:, j, k:k + 256], V("odd_conv_w_3", 8 * k + f), CO[:, f, :], MUL, ADD)
                    cof = CO[:, 4 * g:4 * g + 4, :].rearrange("p j t -> p (j t)")
                    tco = AC.act(cof, cof, ACT.Silu, after=ct)
                for hf in range(2):
                    bytoks(wtile(wi, 1024 + 512 * hf, 512), 0, 512, HT, h,
                           lambda t, p, tp: AC.act(VX[:, t, 4 * hf:4 * hf + 4, 0:128], heads(p, 4), ACT.Copy, after=[tp, z]))
                tv = AC.last
                for hf in range(2):
                    later_toks(wi, 2048 + 512 * hf, HT, h,
                               lambda t, p, tp, hf=hf: AC.act(OG[:, t, 512 * hf:512 * hf + 512], p, ACT.Sigmoid, after=tp))
                O = sb("OO", [128, 2, D], c=ph)
                W = sb("WO", [128, 4, 384], c=ph)
                dn = sb("dn", [128, 8], c=ph)
                fw = None
                for g in range(2):
                    for i in range(4):
                        hd = 4 * g + i
                        b = B.take()
                        tp = PE.mm(b.ap[:, 0:256], SEL[0:8, hd * 128:hd * 128 + 128], cm, True, True, [tcm, b.free], sig=True)
                        VE.ts(W[:, i, 0:256], b.ap[:, 0:256], CCM[:, 0, hd:hd + 1], SUB, 0.0, MAX, [tp, fw])
                        a = VE.ts(W[:, i, 256:384], b.ap[:, 128:256], CCM[:, 1, hd:hd + 1], SUB, 0.0, MAX)
                        b.done(a)
                    fill()
                    wf = W[:, :, :].rearrange("p i t -> p (i t)")
                    a = AC.act(wf, wf, ACT.Exp, scale=-1.0, after=a)
                    for c0 in (0, 256):
                        te = VE.tt(W[:, :, c0:c0 + 128], W[:, :, c0:c0 + 128], bc(C("UF"), 4), MUL, a)
                    for i in (0, 2, 1, 3):
                        hd = 4 * g + i
                        hp = slice(64 * (hd % 2), 64 * (hd % 2) + 64)
                        b = B.take()
                        PE.mm(b.ap[:, 0:256], CO[hp, 4 + hd // 2, 0:128], CO[hp, hd // 2, :], True, True, [tco, b.free])
                        tp = PE.mm(b.ap[:, 256:384], CO[hp, 4 + hd // 2, 128:256], CO[hp, hd // 2, 128:256], True, True, sig=True)
                        tw = VE.stt(W[:, i, :], b.ap[:, 0:384], 0.125, W[:, i, :], MUL, MUL, [tp, te])
                        b.done(tw)
                    fill()
                    for t in range(2):
                        for i in range(0, 4, 2):
                            b = B.take()
                            for j in range(2):
                                hd = 4 * g + i + j
                                o = b.ap[:, 129 * j:129 * j + 129]
                                prs = [(W[:, i + j, t * 128:t * 128 + 128], VX[:, 0, hd, :])]
                                if t:
                                    prs.append((W[:, i + j, 256:384], VX[:, 1, hd, :]))
                                tp = PE.mms(o, prs, [tw, tv, b.free])
                            h0 = 4 * g + i
                            bv = b.ap[:, 0:258].rearrange("p (j c) -> p j c", j=2)
                            a = AC.act(dn[:, 0:2], bv[:, :, 128], ACT.Abs, after=[tp, VE.last])
                            VE.tt(dn[:, 0:2], dn[:, 0:2], CCM[:, t, 8 + h0:8 + h0 + 2], MAX, a)
                            VE.rec(dn[:, 0:2], dn[:, 0:2])
                            a = VE.tt(heads(O[:, t, h0 * 128:h0 * 128 + 256], 2), bv[:, :, 0:128], ex(dn[:, 0:2], 128), MUL)
                            b.done(a)
                    fw = tp
                fill_rest()
                tog = AC.last
                for t in range(2):
                    v = Bank(B, 0, O[:, t, :], None)
                    v.done = lambda *x: None
                    tg = head_norm(v, [VE.last, tog], OG[:, t, :], O[:, t, :], 8, XN[:, 0, :], 44 + 8 * t)
                OT = HT
                tf = to_features(lambda t, k: O[:, t, k * 128:(k + 1) * 128], OT,
                                 lambda k: V("odd_norm_g_3", k), lambda k: None, [tg, PE.last])
                out_proj([(T["odd_w_out_3"][0], 0, 8)], OT, tf, add_gated(0, XN, growtok))
            barrier()

        def third():
            bgon[0] = True
            even(need(mods[3]), lambda: need(rows[3]))
            ffn(0, 4, 4, need(mods[4]), lambda: need(rows[4]))
            odd(need(mods[5]), lambda: need(rows[5]))
            ffn(1, 6, 1, need(mods[6]), lambda: need(rows[6]))
            lf = loads("final")
            lf.go(PO, GB[:, :], T["final_g_3"].rearrange("(a d) -> a d", a=1).broadcast_to([128, D]))
            with ExitStack() as ph:
                SQ = sb("SQF", [128, D], c=ph)
                t = rstd(lambda i: X[:, i, :], 2, D, SQ[:, :], st[:, 0:2], None)
                for i in range(2):
                    VE.stt(X[:, i, :], X[:, i, :], st[:, i:i + 1], GB[:, :], MUL, MUL, [t, lf.tok])
            barrier()

        a2, b2_, a3, b3 = T["w_ada_2"][0], T["b_ada_2"], T["ada_w_3"], T["ada_b_3"]
        v2, v3 = vat["b_ada_2"], vat["ada_b_3"]
        wm = T["w_mod"][0]
        mods = {0: AdaCols(wm, 0, 0, vat["b_mod"], vat["g_pre_mix"], 0),
                1: AdaCols(wm, 3072, 0, vat["b_mod"] + 24, vat["g_pre_ffn"], 1),
                2: AdaCols(a2, 0, 8, v2, vat["g_pre_2"], 2)}
        rows = {0: AdaRow(wm, 2048, 0, T["b_mod"][:, 2048:3072], T["g_post_mix"], 0),
                1: AdaRow(T["w_mod"][0], 5120, 0, T["b_mod"][:, 5120:6144], T["g_post_ffn"], 1),
                2: AdaRow(a2, 2048, 8, b2_[:, 2048:3072], T["g_post_2"], 2)}
        for l in range(2):
            nm, nf = vat["norm_mix_g_3"] + 8 * l, vat["norm_ffn_g_3"] + 8 * l
            mods[3 + 2 * l] = AdaCols(a3[l], 0, 16, v3 + 48 * l, nm, 3 + 2 * l)
            mods[4 + 2 * l] = AdaCols(a3[l], 3072, 16, v3 + 48 * l + 24, nf, 4 + 2 * l)
            rows[3 + 2 * l] = AdaRow(a3[l], 2048, 16, b3[l:l + 1, 2048:3072], None, 3 if l == 0 else 0)
            rows[4 + 2 * l] = AdaRow(a3[l], 5120, 16, b3[l:l + 1, 5120:6144], None, 4 if l == 0 else 1)
        order = {"1": [mods[0], rows[0], mods[1], rows[1]], "2": [mods[2], rows[2]],
                 "3": [mods[3], mods[4], mods[5], rows[3], rows[4], rows[5], mods[6], rows[6]]}
        for p in parts:
            pending += [(o, j) for o in order[p] for j in range(o.n)]
        background(1)
        vectors()
        SP.pend = [lv[0].tok, lv[1].tok]
        need(mods[{"1": 0, "2": 2, "3": 3}[parts[0]]])
        for q in (PE, AC, VE, PO):
            q.pend = q.pend + ready + [l1.tok, l2.tok, lx.tok]
        for p in parts:
            if p == "1":
                first()
            if p == "2":
                second()
            if p == "3":
                third()

        lo = loads("out")
        lo.go(AC, out.rearrange("a (t p) d -> p (a t) d", p=128), X[:, :, :], [VE.last])
        AC.raw(lambda e, seen, outer: e.wait_ge(lo.sem, lo.n))

        with nc.Block() as block:
            @block.tensor
            def _(eng):
                PE.emit(eng)

            @block.scalar
            def _(eng):
                AC.emit(eng)

            @block.vector
            def _(eng):
                VE.emit(eng)

            @block.gpsimd
            def _(eng):
                PO.emit(eng)

            @block.sync
            def _(eng):
                SP.emit(eng)


def make(nc, shapes, parts="123", flip=False):
    T = {}
    for name, shape in shapes.items():
        T[name] = nc.dram_tensor(f"in_{name}", shape, F32, kind="ExternalInput").ap()
    out = nc.dram_tensor("out_0", (1, 256, 1024), F32, kind="ExternalOutput").ap()
    build(nc, T, out, parts, flip)


def kernel(**inputs):
    import concourse.bacc as bacc
    from concourse.bass_utils import run_bass_kernel_spmd as run
    arrays = {}
    for name, a in inputs.items():
        arrays[name] = np.ascontiguousarray(a)
    arrays["consts"] = const_table()[1]
    arrays["sel"] = sel_table()
    nc = bacc.Bacc("TRN2", target_bir_lowering=False, num_devices=1)
    make(nc, {n: a.shape for n, a in arrays.items()})
    r = run(nc, [{f"in_{n}": a for n, a in arrays.items()}], core_ids=[0])
    return r.results[0]["out_0"]
```
